# Optimizing a Trainium2 kernel written in Bass

```python
import math, functools
import jax, jax.numpy as jnp
from jax import lax
import numpy as np

D_MODEL = 1024
BATCH = 1
SEQ = 512
DEPTH = 2
DEC_BATCH = 8
DEC_SEQ = 4
PAST_LEN = 512
PAGE_SIZE = 128

F32 = jnp.float32
D_SSM = D_MODEL // 2
D_ATTN = D_MODEL - D_SSM
SSM_GROUP = 16
N_SSM_GROUPS = D_SSM // SSM_GROUP
SSM_STATE = 64
HEAD_DIM = 64
N_HEADS = D_ATTN // HEAD_DIM
N_KV_HEADS = 2
N_REP = N_HEADS // N_KV_HEADS
N_IDX_HEADS = 8
IDX_DIM = 64
IDX_SCALE = (IDX_DIM ** -0.5) * (N_IDX_HEADS ** -0.5)
TOPK_MAX = 256
Q_BLOCK = 128
N_BUCKETS = 32
MAX_DISTANCE = 128
D_FF = 2816
N_EXPERTS = 8
TOP_K_EXPERTS = 2
D_FF_EXPERT = 1408
N_DENSE = (DEPTH + 1) // 2
N_MOE = DEPTH // 2
D_PLE = 256
LN_EPS = 1e-5
ALPHA = (2 * DEPTH) ** 0.25
BETA = (8 * DEPTH) ** -0.25
IN_SPLITS = (D_SSM, N_HEADS * HEAD_DIM, N_KV_HEADS * HEAD_DIM, N_KV_HEADS * HEAD_DIM,
             N_IDX_HEADS * IDX_DIM, IDX_DIM, N_IDX_HEADS)
D_IN = sum(IN_SPLITS)

kernel_name = 's5_dsa_hymba_deepnorm_step'

def layer_norm(x, g, b):
    xf = x.astype(F32)
    mu = jnp.mean(xf, axis=-1, keepdims=True)
    var = jnp.mean(jnp.square(xf - mu), axis=-1, keepdims=True)
    return ((xf - mu) * lax.rsqrt(var + LN_EPS) * g.astype(F32) + b.astype(F32)).astype(x.dtype)

def split_columns(z):
    outs = []
    start = 0
    for width in IN_SPLITS:
        outs.append(z[..., start:start + width])
        start += width
    return outs

def t5_bucket(dist):
    max_exact = N_BUCKETS // 2
    n = jnp.maximum(dist, 0)
    nf = jnp.maximum(n, 1).astype(F32)
    large = max_exact + (jnp.log(nf / max_exact) / math.log(MAX_DISTANCE / max_exact)
                         * (N_BUCKETS - max_exact)).astype(jnp.int32)
    large = jnp.minimum(large, N_BUCKETS - 1)
    return jnp.where(n < max_exact, n, large)

def s5_mixer(u, h0_re, h0_im, a_re, a_im, log_dt, b_re, b_im, c_re, c_im, d_skip, w_glu):
    bsz, length, _ = u.shape
    uf = u.astype(F32).reshape(bsz, length, N_SSM_GROUPS, SSM_GROUP)
    lam = lax.complex(a_re.astype(F32), a_im.astype(F32))
    dt = jnp.exp(log_dt.astype(F32))[:, None]
    a_bar = jnp.exp(lam * dt)
    b_bar = ((a_bar - 1.0) / lam)[:, :, None] * lax.complex(b_re.astype(F32), b_im.astype(F32))
    bu = jnp.einsum('blgc,gnc->blgn', uf.astype(jnp.complex64), b_bar)
    h0 = lax.complex(h0_re.astype(F32), h0_im.astype(F32))
    bu = bu.at[:, 0].add(a_bar * h0)
    a_seq = jnp.broadcast_to(a_bar, bu.shape)

    def combine(left, right):
        a_l, b_l = left
        a_r, b_r = right
        return a_r * a_l, a_r * b_l + b_r

    _, h = lax.associative_scan(combine, (a_seq, bu), axis=1)
    c = lax.complex(c_re.astype(F32), c_im.astype(F32))
    y = jnp.einsum('blgn,gcn->blgc', h, c).real + d_skip.astype(F32).reshape(N_SSM_GROUPS, SSM_GROUP) * uf
    y = jax.nn.gelu(y.reshape(bsz, length, D_SSM))
    z = y @ w_glu.astype(F32)
    out = z[..., :D_SSM] * jax.nn.sigmoid(z[..., D_SSM:])
    h_last = h[:, -1]
    return out.astype(u.dtype), h_last.real, h_last.imag

def indexer_scores(q_idx, w_idx, k_idx):
    s = jnp.einsum('bthd,bsd->bths', q_idx.astype(F32), k_idx.astype(F32))
    return jnp.einsum('bths,bth->bts', jax.nn.relu(s), w_idx.astype(F32)) * IDX_SCALE

def select_keys(scores, q_pos, topk):
    k_pos = jnp.arange(scores.shape[-1])
    causal = k_pos[None, None, :] <= q_pos[None, :, None]
    _, idx = lax.top_k(jnp.where(causal, scores, -jnp.inf), topk)
    valid = idx <= q_pos[None, :, None]
    return idx, valid

def sparse_attend(q, k_sel, v_sel, q_pos, idx, valid, rel_bias):
    bsz, t = q.shape[:2]
    qg = q.reshape(bsz, t, N_KV_HEADS, N_REP, HEAD_DIM)
    logits = jnp.einsum('btgrd,btkgd->btgrk', qg, k_sel).astype(F32) * (HEAD_DIM ** -0.5)
    bias = rel_bias[t5_bucket(q_pos[None, :, None] - idx)].astype(F32)
    bias = bias.reshape(bsz, t, -1, N_KV_HEADS, N_REP).transpose(0, 1, 3, 4, 2)
    logits = jnp.where(valid[:, :, None, None, :], logits + bias, -jnp.inf)
    probs = jax.nn.softmax(logits, axis=-1).astype(v_sel.dtype)
    out = jnp.einsum('btgrk,btkgd->btgrd', probs, v_sel)
    return out.reshape(bsz, t, N_HEADS * HEAD_DIM)

def gather_rows(rows, ids):
    return jax.vmap(lambda r, i: r[i])(rows, ids)

def prompt_attention(q, k, v, q_idx, w_idx, k_idx, rel_bias):
    bsz, seq = q.shape[:2]
    topk = min(TOPK_MAX, seq // 4)
    n_blocks = seq // Q_BLOCK

    def blockify(a):
        return jnp.moveaxis(a.reshape((bsz, n_blocks, Q_BLOCK) + a.shape[2:]), 1, 0)

    def one_block(args):
        qb, qib, wb, t0 = args
        q_pos = t0 + jnp.arange(Q_BLOCK)
        idx, valid = select_keys(indexer_scores(qib, wb, k_idx), q_pos, topk)
        return sparse_attend(qb, gather_rows(k, idx), gather_rows(v, idx), q_pos, idx, valid, rel_bias)

    out = lax.map(one_block, (blockify(q), blockify(q_idx), blockify(w_idx),
                              jnp.arange(n_blocks, dtype=jnp.int32) * Q_BLOCK))
    return jnp.moveaxis(out, 0, 1).reshape(bsz, seq, N_HEADS * HEAD_DIM)

def sample_attention(q, k_new, v_new, q_idx, w_idx, kidx_new, cache_k, cache_v, cache_kidx, page_table, rel_bias):
    bsz, t = q.shape[:2]
    n_pages = page_table.shape[1]
    past = n_pages * PAGE_SIZE
    topk = min(TOPK_MAX, (past + t) // 4)
    kidx_past = cache_kidx[page_table].reshape(bsz, past, IDX_DIM)
    kidx_all = jnp.concatenate([kidx_past, kidx_new.astype(kidx_past.dtype)], axis=1)
    q_pos = past + jnp.arange(t)
    idx, valid = select_keys(indexer_scores(q_idx, w_idx, kidx_all), q_pos, topk)
    pi = jnp.minimum(idx, past - 1)
    phys = page_table[jnp.arange(bsz)[:, None, None], pi // PAGE_SIZE]
    off = pi % PAGE_SIZE
    ni = jnp.clip(idx - past, 0, t - 1)
    is_new = (idx >= past)[..., None, None]
    k_sel = jnp.where(is_new, gather_rows(k_new, ni).astype(cache_k.dtype), cache_k[phys, off])
    v_sel = jnp.where(is_new, gather_rows(v_new, ni).astype(cache_v.dtype), cache_v[phys, off])
    return sparse_attend(q, k_sel.astype(q.dtype), v_sel.astype(q.dtype), q_pos, idx, valid, rel_bias)

def swiglu(x, w_gate, w_up, w_down):
    return (jax.nn.silu(x @ w_gate) * (x @ w_up)) @ w_down

def moe_swiglu(x, w_router, b_router, w_gate, w_up, w_down):
    logits = (x @ w_router).astype(F32) + b_router.astype(F32)
    top_vals, top_idx = lax.top_k(logits, TOP_K_EXPERTS)
    probs = jax.nn.softmax(top_vals, axis=-1)
    gates = jnp.sum(jax.nn.one_hot(top_idx, N_EXPERTS, dtype=F32) * probs[..., None], axis=-2)
    y = jnp.zeros_like(x)
    for e in range(N_EXPERTS):
        y = y + gates[..., e:e + 1].astype(x.dtype) * swiglu(x, w_gate[e], w_up[e], w_down[e])
    return y

def trunk_layer(x, p, attend, h0_re, h0_im, w_in, ssm_params, w_out, ln1_g, ln1_b,
                channel_mixer, ple_w_gate, ple_w_proj, ln2_g, ln2_b):
    bsz, t, _ = x.shape
    u, q, k, v, q_idx, k_idx, w_idx = split_columns(x @ w_in)
    q = q.reshape(bsz, t, N_HEADS, HEAD_DIM)
    k = k.reshape(bsz, t, N_KV_HEADS, HEAD_DIM)
    v = v.reshape(bsz, t, N_KV_HEADS, HEAD_DIM)
    q_idx = q_idx.reshape(bsz, t, N_IDX_HEADS, IDX_DIM)
    ssm_out, h_re, h_im = s5_mixer(u, h0_re, h0_im, *ssm_params)
    attn_out = attend(q, k, v, q_idx, w_idx, k_idx)
    mixed = jnp.concatenate([ssm_out, attn_out.astype(ssm_out.dtype)], axis=-1) @ w_out
    x = layer_norm(ALPHA * x + mixed, ln1_g, ln1_b)
    ple = jax.nn.sigmoid(x @ ple_w_gate) * (p @ ple_w_proj)
    x = layer_norm(ALPHA * x + channel_mixer(x) + ple, ln2_g, ln2_b)
    return x, k, v, k_idx, h_re, h_im

def setup_inputs(seed: int = 0) -> dict:
    key = jax.random.key(seed)
    keys = iter(jax.random.split(key, 64))

    def normal(shape, scale):
        return scale * jax.random.normal(next(keys), shape, F32)

    n_pages = PAST_LEN // PAGE_SIZE
    n_used = DEC_BATCH * n_pages
    n_pool = n_used + (n_used + 3) // 4
    perm = jax.random.permutation(next(keys), n_pool).astype(jnp.int32)
    page_table = perm[:n_used].reshape(DEC_BATCH, n_pages)

    a_im_base = jnp.pi * jnp.arange(SSM_STATE, dtype=F32)
    return {
        'x_prompt': normal((BATCH, SEQ, D_MODEL), 1.0),
        'x_sample': normal((DEC_BATCH, DEC_SEQ, D_MODEL), 1.0),
        'p_prompt': normal((DEPTH, BATCH, SEQ, D_PLE), 1.0),
        'p_sample': normal((DEPTH, DEC_BATCH, DEC_SEQ, D_PLE), 1.0),
        'cache_k': normal((DEPTH, n_pool, PAGE_SIZE, N_KV_HEADS, HEAD_DIM), 1.0),
        'cache_v': normal((DEPTH, n_pool, PAGE_SIZE, N_KV_HEADS, HEAD_DIM), 1.0),
        'cache_kidx': normal((DEPTH, n_pool, PAGE_SIZE, IDX_DIM), 1.0),
        'state_ssm_re': normal((DEPTH, DEC_BATCH, N_SSM_GROUPS, SSM_STATE), 0.1),
        'state_ssm_im': normal((DEPTH, DEC_BATCH, N_SSM_GROUPS, SSM_STATE), 0.1),
        'page_table': page_table,
        'ln_emb_g': 1.0 + normal((D_MODEL,), 0.01),
        'ln_emb_b': normal((D_MODEL,), 0.01),
        'w_in': normal((DEPTH, D_MODEL, D_IN), D_MODEL ** -0.5),
        'ssm_a_re': -0.5 + normal((DEPTH, N_SSM_GROUPS, SSM_STATE), 0.01),
        'ssm_a_im': a_im_base + normal((DEPTH, N_SSM_GROUPS, SSM_STATE), 0.01),
        'ssm_log_dt': jax.random.uniform(next(keys), (DEPTH, N_SSM_GROUPS), F32, math.log(1e-3), math.log(1e-1)),
        'ssm_b_re': normal((DEPTH, N_SSM_GROUPS, SSM_STATE, SSM_GROUP), (2 * SSM_GROUP) ** -0.5),
        'ssm_b_im': normal((DEPTH, N_SSM_GROUPS, SSM_STATE, SSM_GROUP), (2 * SSM_GROUP) ** -0.5),
        'ssm_c_re': normal((DEPTH, N_SSM_GROUPS, SSM_GROUP, SSM_STATE), SSM_STATE ** -0.5),
        'ssm_c_im': normal((DEPTH, N_SSM_GROUPS, SSM_GROUP, SSM_STATE), SSM_STATE ** -0.5),
        'ssm_d': normal((DEPTH, D_SSM), 1.0),
        'ssm_w_glu': normal((DEPTH, D_SSM, 2 * D_SSM), D_SSM ** -0.5),
        'rel_bias': normal((N_BUCKETS, N_HEADS), 0.3),
        'w_out': normal((DEPTH, D_MODEL, D_MODEL), BETA * D_MODEL ** -0.5),
        'ln1_g': 1.0 + normal((DEPTH, D_MODEL), 0.01),
        'ln1_b': normal((DEPTH, D_MODEL), 0.01),
        'ffn_w_gate': normal((N_DENSE, D_MODEL, D_FF), D_MODEL ** -0.5),
        'ffn_w_up': normal((N_DENSE, D_MODEL, D_FF), D_MODEL ** -0.5),
        'ffn_w_down': normal((N_DENSE, D_FF, D_MODEL), BETA * D_FF ** -0.5),
        'moe_w_router': normal((N_MOE, D_MODEL, N_EXPERTS), D_MODEL ** -0.5),
        'moe_b_router': normal((N_MOE, N_EXPERTS), 0.01),
        'moe_w_gate': normal((N_MOE, N_EXPERTS, D_MODEL, D_FF_EXPERT), D_MODEL ** -0.5),
        'moe_w_up': normal((N_MOE, N_EXPERTS, D_MODEL, D_FF_EXPERT), D_MODEL ** -0.5),
        'moe_w_down': normal((N_MOE, N_EXPERTS, D_FF_EXPERT, D_MODEL), BETA * D_FF_EXPERT ** -0.5),
        'ple_w_gate': normal((DEPTH, D_MODEL, D_MODEL), D_MODEL ** -0.5),
        'ple_w_proj': normal((DEPTH, D_PLE, D_MODEL), BETA * D_PLE ** -0.5),
        'ln2_g': 1.0 + normal((DEPTH, D_MODEL), 0.01),
        'ln2_b': normal((DEPTH, D_MODEL), 0.01),
    }

def reference(x_prompt, x_sample, p_prompt, p_sample, cache_k, cache_v, cache_kidx, state_ssm_re, state_ssm_im,
              page_table, ln_emb_g, ln_emb_b, w_in, ssm_a_re, ssm_a_im, ssm_log_dt, ssm_b_re, ssm_b_im,
              ssm_c_re, ssm_c_im, ssm_d, ssm_w_glu, rel_bias, w_out, ln1_g, ln1_b, ffn_w_gate, ffn_w_up,
              ffn_w_down, moe_w_router, moe_b_router, moe_w_gate, moe_w_up, moe_w_down, ple_w_gate,
              ple_w_proj, ln2_g, ln2_b):
    xp = layer_norm(x_prompt, ln_emb_g, ln_emb_b)
    xs = layer_norm(x_sample, ln_emb_g, ln_emb_b)
    h0_prompt = jnp.zeros((x_prompt.shape[0], N_SSM_GROUPS, SSM_STATE), F32)
    kp_l, vp_l, kip_l, hrp_l, hip_l = [], [], [], [], []
    ks_l, vs_l, kis_l, hrs_l, his_l = [], [], [], [], []
    prompt_attend = functools.partial(prompt_attention, rel_bias=rel_bias)
    for i in range(DEPTH):
        ssm_params = (ssm_a_re[i], ssm_a_im[i], ssm_log_dt[i], ssm_b_re[i], ssm_b_im[i],
                      ssm_c_re[i], ssm_c_im[i], ssm_d[i], ssm_w_glu[i])
        j = i // 2
        if i % 2 == 0:
            cm = functools.partial(swiglu, w_gate=ffn_w_gate[j], w_up=ffn_w_up[j], w_down=ffn_w_down[j])
        else:
            cm = functools.partial(moe_swiglu, w_router=moe_w_router[j], b_router=moe_b_router[j],
                                   w_gate=moe_w_gate[j], w_up=moe_w_up[j], w_down=moe_w_down[j])
        sample_attend = functools.partial(sample_attention, cache_k=cache_k[i], cache_v=cache_v[i],
                                          cache_kidx=cache_kidx[i], page_table=page_table, rel_bias=rel_bias)
        xp, kp, vp, kip, hrp, hip = trunk_layer(xp, p_prompt[i], prompt_attend, h0_prompt, h0_prompt, w_in[i],
                                                ssm_params, w_out[i], ln1_g[i], ln1_b[i], cm,
                                                ple_w_gate[i], ple_w_proj[i], ln2_g[i], ln2_b[i])
        xs, ks, vs, kis, hrs, his = trunk_layer(xs, p_sample[i], sample_attend, state_ssm_re[i], state_ssm_im[i],
                                                w_in[i], ssm_params, w_out[i], ln1_g[i], ln1_b[i], cm,
                                                ple_w_gate[i], ple_w_proj[i], ln2_g[i], ln2_b[i])
        kp_l.append(kp); vp_l.append(vp); kip_l.append(kip); hrp_l.append(hrp); hip_l.append(hip)
        ks_l.append(ks); vs_l.append(vs); kis_l.append(kis); hrs_l.append(hrs); his_l.append(his)
    return (xp, xs,
            jnp.stack(kp_l), jnp.stack(vp_l), jnp.stack(kip_l), jnp.stack(hrp_l), jnp.stack(hip_l),
            jnp.stack(ks_l), jnp.stack(vs_l), jnp.stack(kis_l), jnp.stack(hrs_l), jnp.stack(his_l))


_drawn_inputs = setup_inputs


def setup_inputs(seed=0):
    import zlib

    import numpy as np

    out = dict(_drawn_inputs(seed))
    spreads = {}
    factors = {'ln_emb_g': 3.416,
     'ssm_a_re': 4.239,
     'ssm_c_im': 4.334,
     'ln1_g': 2.931,
     'ln1_b': 3.254,
     'moe_b_router': 6.518,
     'ln2_g': 2.939}
    for name, (base, spread) in spreads.items():
        noise = np.random.default_rng([zlib.crc32(name.encode()), seed]).standard_normal(out[name].shape)
        drawn = base * np.exp(spread * noise) if base else spread * noise
        out[name] = __import__('jax').numpy.asarray(drawn.astype(out[name].dtype))
    for name, factor in factors.items():
        out[name] = (out[name] * factor).astype(out[name].dtype)
    return out
```

```python
import math

import concourse.bass as bass
from concourse import mybir
from contextlib import ExitStack

DM, SEQ, L, NB, DT, PAST, PAGE = 1024, 512, 2, 8, 4, 512, 128
NS = NB * DT
T = SEQ + NS
KC = DM // 128
CH = 8
NC = SEQ // CH
G, GC, SN = 32, 16, 64
HG = G // 2
HP = HG // 2
CW = NB + NC
NH, HD = 8, 64
NQT = SEQ // 128
TOPK_P = min(256, SEQ // 4)
TOPK_S = min(256, (PAST + DT) // 4)
NPG = PAST // PAGE
NPOOL = NB * NPG + (NB * NPG + 3) // 4
FE, NE = 1408, 8
FT = FE // 128
ALPHA = (2 * L) ** 0.25
LN_EPS = 1e-5
IDX_SCALE = (64 ** -0.5) * (8 ** -0.5)
NEG = -1e30
GONE = -3.0e38
RING = 6
SLOT = FT * 128
BLOCK_JOBS = 2 * FT + KC
WIN_T = 15
PAR_F = 3 + 4 * GC + 2 * NB
BW = SEQ + 128

C_ID, C_CM, C_MC, C_EX, C_MW, C_OH, C_MS, C_TK, C_MT, C_OF = 0, 128, 256, 384, 640, 704, 832, 864, 1408, 1536
C_END = C_OF + BW


def build(nc, io):
    fp32, i32 = mybir.dt.float32, mybir.dt.int32
    ALU, ACT, AX = mybir.AluOpType, mybir.ActivationFunctionType, mybir.AxisListType
    ctx = ExitStack()
    with ctx:
        def sb(name, shape, dt=fp32):
            return ctx.enter_context(nc.sbuf_tensor(name, shape, dt))

        def sem(name):
            return ctx.enter_context(nc.semaphore(name))

        x = sb("x_res", [128, KC, T])
        acc = sb("acc", [128, KC, T])
        cat = sb("cat", [128, KC, T])
        ring = sb("ring", [128, RING, SLOT])
        rbias = sb("rbias", [128, NH, SEQ])
        cst = sb("cst", [128, C_END])
        bs = sb("bs", [128, PAST + NS])
        lnp = sb("lnp", [128, 2 + 4 * L, KC])
        dsk = sb("dsk", [128, L, 4])
        wrt = sb("wrt", [128, KC, NE])
        brt = sb("brt", [128, NE])
        ones = sb("ones", [128, 128])
        ptab = sb("ptab", [1, NB * NPG], i32)
        q = sb("q", [128, 4, T])
        kn = sb("kn", [128, T])
        kin = sb("kin", [128, T])
        vn = sb("vn", [128, T])
        wn = sb("wn", [NH, T])
        vtok = sb("vtok", [128, NQT + 1, 128])
        wtok = sb("wtok", [128, NQT, NH])
        sg = sb("sg", [128, 2, T])
        m8x = sb("mark", [128, 1])
        ph = sb("phase", [128, 18400])
        u = acc[:, 0:4, :]
        qi = acc[:, 4:8, :]
        ident = cst[:, C_ID:C_ID + 128]

        class Cut:
            def __init__(self, t, at=0):
                self.t, self.at = t, at

            def __call__(self, n, rows=128, lo=0):
                self.at += n
                return self.t[lo:lo + rows, self.at - n:self.at]

        cut = Cut(ph)
        U = cut(G * CW).rearrange("p (g c) -> p g c", g=G)
        U2 = cut(G * NB).rearrange("p (g b) -> p g b", g=G)
        par_at = cut.at
        par = cut(HP * PAR_F).rearrange("p (f e) -> p f e", e=HP)
        pB = par[:, 3:3 + 4 * GC, :].rearrange("p (k c) e -> p k e c", k=4)
        pH = par[:, 3 + 4 * GC:, :].rearrange("p (k b) e -> p k e b", k=2)
        toep = cut(HG * 128).rearrange("p (g n) -> p g n", g=HG)
        BT = cut(2 * HP * 128).rearrange("p (k e n) -> p k e n", k=2, e=HP)
        CP = [cut(HP * (CH + 1) * GC).rearrange("p (e m c) -> p e m c", e=HP, c=GC) for _ in range(2)]
        BP = [cut(HP * CH * GC).rearrange("p (e m c) -> p e m c", e=HP, c=GC) for _ in range(2)]
        Bb = [cut(HP * GC).rearrange("p (e c) -> p e c", e=HP) for _ in range(2)]
        E = [cut(HP * NC).rearrange("p (e c) -> p e c", e=HP) for _ in range(2)]
        GM = [cut(HP * NC).rearrange("p (e c) -> p e c", e=HP) for _ in range(2)]
        GS = [cut(HP * NC).rearrange("p (e c) -> p e c", e=HP) for _ in range(2)]
        HW_ = NB + NC + 1
        H = [cut(HP * HW_).rearrange("p (e c) -> p e c", e=HP) for _ in range(2)]
        R8 = cut(HP * NC).rearrange("p (e c) -> p e c", e=HP)
        Y = cut(HG * CW).rearrange("p (g c) -> p g c", g=HG)
        hout = cut(2 * HP * (NB + 1)).rearrange("p (k e b) -> p k e b", k=2, e=HP)
        P = [cut((CH + 1) * HP).rearrange("p (m e) -> p m e", e=HP) for _ in range(2)]
        sm = cut(24 * HP).rearrange("p (n e) -> p n e", e=HP)
        cf = cat[:, :, :].rearrange("p k t -> p (k t)")
        Kd = cf[0:GC, 0:HG * 128].rearrange("p (g n) -> p g n", g=HG)
        T1 = cf[:, 2048:2048 + 1152]
        T2 = cf[:, 3200:3200 + 1152]
        cut = Cut(ph)
        pgK = cut(16 * PAGE).rearrange("p (n c) -> p n c", n=16)
        pgV = cut(16 * PAGE).rearrange("p (n c) -> p n c", n=16)
        pgI = cut(16 * PAGE).rearrange("p (n c) -> p n c", n=16)
        shared = cut.at
        rl = cut(4 * SEQ).rearrange("p (n c) -> p n c", n=4)
        sc = cut(SEQ)
        wk = cut(SEQ)
        nosel = cut(SEQ)
        Lg = cut(NH * SEQ).rearrange("p (h c) -> p h c", h=NH)
        PT = cut(2 * NQT * 512).rearrange("p (g k c) -> p g k c", g=2, k=NQT)
        m8 = cut(8)
        nmx = cut(NH)
        sums = cut(NH)
        rs = cut(NH)
        cut = Cut(ph, shared)
        Qzi = cut(256).rearrange("p (b a i t) -> p b a i t", b=NB, a=2, i=4)
        Qz = cut(256).rearrange("p (b a i t) -> p b a i t", b=NB, a=2, i=4)
        SK = PAST + NS
        rls = cut(SK)
        wr = cut(2 * NS).rearrange("p (r y) -> p r y", r=2)
        scs = cut(SK)
        wks = cut(SK + 7)
        nss = cut(SK)
        Ls = cut(SK)
        PTs = cut(5 * 128).rearrange("p (k c) -> p k c", k=5)
        m8s = cut(8)
        nms = cut(4)
        cut = Cut(ph)
        hid = cut(FT * T).rearrange("p (f t) -> p f t", f=FT)
        gb = cut(NE * T).rearrange("p (e t) -> p e t", e=NE)
        pt = cut(2 * T).rearrange("p (k t) -> p k t", k=2)
        rlog = cut(5 * NE).rearrange("p (n e) -> p n e", n=5)
        rtop = cut(5 * NE).rearrange("p (n e) -> p n e", n=5)
        rtwo = cut(5 * NE).rearrange("p (n e) -> p n e", n=5)
        rwk = cut(5 * 14).rearrange("p (n e) -> p n e", n=5)
        gts = cut(5 * NE).rearrange("p (n e) -> p n e", n=5)
        rsm = cut(5 * 4).rearrange("p (n e) -> p n e", n=5)
        rst = cut(T)
        cut = Cut(ph)
        relb = cut(NH * 128).rearrange("p (h n) -> p h n", h=NH)
        reltk = cut(128)
        frow = cut(NH * BW).rearrange("p (h n) -> p h n", h=NH)

        pair = [ctx.enter_context(nc.psum_tensor(f"pair{i}", [128, 1024], fp32)) for i in range(4)]

        def bank(i):
            return pair[i // 2][:, 512 * (i % 2):512 * (i % 2) + 512]

        def even(i):
            return pair[i][:, :].rearrange("p (h c) -> p h c", h=2)[:, :, 0:T // 2]

        udram = nc.dram_tensor("u_scratch", (4 * 128, T), fp32, kind="Internal")
        ydram = nc.dram_tensor("y_scratch", (4 * 128, T), fp32, kind="Internal")
        fdram = nc.dram_tensor("f_scratch", (NH, 128, BW), fp32, kind="Internal")

        w_loaded = [sem(f"w_loaded{i}") for i in range(RING)]
        jobs_begun = sem("jobs_begun")
        filled = [sem(f"filled{i}") for i in range(4)]
        emptied = [sem(f"emptied{i}") for i in range(4)]
        dve_step, act_step, pool_step = sem("dve_step"), sem("act_step"), sem("pool_step")
        consts_in, rel_in, x_in = sem("consts_in"), sem("rel_in"), sem("x_in")
        ones_set = sem("ones_set")
        f_mm, f_ready, f_out, rbias_in = sem("f_mm"), sem("f_ready"), sem("f_out"), sem("rbias_in")
        tk_ready, bs_mm, bs_ready = sem("tk_ready"), sem("bs_mm"), sem("bs_ready")
        acc_ready, squares, rstd, x_ready = sem("acc_ready"), sem("squares"), sem("var_inv"), sem("x_ready")
        rst_ready = sem("rstd_ready")
        u_out, u_zero, u_in = sem("u_out"), sem("u_zero"), sem("u_in")
        par_in, ldt, expd, theta, sincos = sem("par_in"), sem("dt_exp"), sem("radii"), sem("theta"), sem("sincos")
        bp_ready, cp_ready, bt_mm, bt_ready = sem("bp_ready"), sem("cp_ready"), sem("bt_mm"), sem("bt_ready")
        toep_zero, kd_mm, kd_ready, toep_in = sem("toep_zero"), sem("kd_mm"), sem("kd_ready"), sem("toep_in")
        g_mm, h_ready, y_mm, y_ready = sem("g_mm"), sem("h_ready"), sem("y_mm"), sem("y_ready")
        y_out, y_in, yd_ready, gelu_ready = sem("y_out"), sem("y_in"), sem("yd_ready"), sem("gelu_ready")
        tok_mm, tok_ready = sem("tok_mm"), sem("tok_ready")
        idx_mm, relu_ready, relu_used = sem("idx_mm"), sem("relu_ready"), sem("relu_used")
        lg_mm, lg_used, nmx_ready, exp_ready = sem("lg_mm"), sem("lg_used"), sem("nmx_ready"), sem("exp_ready")
        rs_ready, prob_ready = sem("rs_ready"), sem("prob_ready")
        pt_mm, pt_ready, pv_mm, pv_ready = sem("pt_mm"), sem("pt_ready"), sem("pv_mm"), sem("pv_ready")
        pages_kv = sem("pages_kv")
        pages_in, qz_ready, wr_mm, wr_ready = sem("pages_in"), sem("qz_ready"), sem("wr_mm"), sem("wr_ready")
        si_mm, srelu, sc_mm, nosel_ready = sem("si_mm"), sem("srelu"), sem("sc_mm"), sem("nosel_ready")
        sl_mm, snmx, sexp, sprob = sem("sl_mm"), sem("snmx"), sem("sexp"), sem("sprob")
        spt_mm, spt_ready, spv_mm, spv_ready = sem("spt_mm"), sem("spt_ready"), sem("spv_mm"), sem("spv_ready")
        pt_in, r_mm, gts_ready, gb_mm, gb_ready = sem("p_in"), sem("r_mm"), sem("gts_ready"), sem("gb_mm"), sem("gb_ready")
        ple_used = sem("ple_used")
        gdiff, gexp = sem("gate_diff"), sem("gate_exp")
        hid_ready = sem("hid_ready")
        stored = sem("stored")

        class Count:
            def __init__(self):
                self.n = [0] * 4

            def take(self, s):
                self.n[s] += 1
                return self.n[s]

        def experts(l):
            return 2 if l == 0 else NE

        def first_block(l):
            return 0 if l == 0 else 2

        LAYER_JOBS = WIN_T + 8 + 8 + 8
        JOBS = [0, LAYER_JOBS + BLOCK_JOBS * experts(0)]
        FFN_USES = [8, 8, 7, 7]

        def ffn_plan():
            seen = [0] * 4
            steps = [("up", f, (0, 1) if f % 2 == 0 else (2, 3)) for f in range(FT)]
            steps += [("down", m, ((2 + m) % 4,)) for m in range(KC)]
            for kind, i, ps in steps:
                yield kind, i, [(s, seen[s]) for s in ps]
                for s in ps:
                    seen[s] += 1

        def uses_before(l, s):
            n = int(s < 2)
            for k in range(l):
                n += 12 + 2 * int(s < 2) + FFN_USES[s] * experts(k)
            return n

        def halves(t):
            return t.rearrange("p (h c) -> p h c", h=2)

        def bc(t, axis, n):
            t = t.unsqueeze(axis)
            shape = list(t.shape)
            shape[axis] = n
            return t.to_broadcast(shape)

        block = ctx.enter_context(nc.Block())

        @block.sync
        def _(sp):
            sp.dma_start(x[:, :, :], io["x_t"]).then_inc(x_in, 16)
            sp.dma_start(lnp[:, :, :], io["ln_p"]).then_inc(x_in, 16)

            def load(n, cols, src):
                if n >= RING:
                    sp.wait_ge(jobs_begun, n - RING + 2)
                sp.dma_start(ring[:, n % RING, 0:cols], src).then_inc(w_loaded[n % RING], 16)

            for l in range(L):
                n = JOBS[l]
                for m in range(WIN_T - 1):
                    load(n + m, 1024, io["w_in_t"][l, m])
                load(n + WIN_T - 1, KC * 136, io["w_v_t"][l])
                n += WIN_T
                for m in range(8):
                    load(n + m, 512, io["w_glu_t"][l, m])
                for m in range(8):
                    load(n + 8 + m, 1024, io["w_out_t"][l, m])
                for m in range(8):
                    load(n + 16 + m, 1280, io["w_ple_t"][l, m])
                n += 24
                with sp.Fori(0, experts(l)) as e:
                    blk = e + first_block(l)
                    for k in range(BLOCK_JOBS):
                        sp.wait_ge(jobs_begun, e * BLOCK_JOBS + (n + k - RING + 2))
                        if k < 2 * FT:
                            src = io["w_gu_t"][bass.ds(blk, 1), k, :, :]
                            cols = 1024
                        else:
                            src = io["w_dn_t"][bass.ds(blk, 1), k - 2 * FT, :, :]
                            cols = SLOT
                        sp.dma_start(ring[:, (n + k) % RING, 0:cols],
                                     src.rearrange("o p c -> p (o c)")).then_inc(w_loaded[(n + k) % RING], 16)

        @block.gpsimd
        def _(pool):
            pool.dma_start(cst[:, :], io["consts"]).then_inc(consts_in, 16)
            pool.dma_start(dsk[:, :, :], io["d_t"]).then_inc(consts_in, 16)
            pool.dma_start(wrt[:, :, :], io["w_router_t"]).then_inc(consts_in, 16)
            pool.dma_start(brt[:, :], io["b_router_t"]).then_inc(consts_in, 16)
            pool.dma_start(ptab[:, :], io["pages"]).then_inc(consts_in, 16)
            pool.dma_start(relb[0:32, :, :], io["rel_rows"]).then_inc(rel_in, 16)
            pool.dma_start(reltk, io["rel_tk"]).then_inc(rel_in, 16)
            nc.gpsimd.memset(ones[:, :], 1.0 / DM).then_inc(ones_set, 1)
            pool.wait_ge(f_ready, NH)
            pool.dma_start(fdram.ap().rearrange("h p n -> p h n"), frow[:, :, :]).then_inc(f_out, 16)
            pool.wait_ge(f_out, 16)
            pool.dma_start(rbias[:, :, :], bass.AP(fdram, 127, [[BW - 1, 128], [128 * BW, NH], [1, SEQ]])).then_inc(rbias_in, 16)
            pool.wait_ge(consts_in, 16 * 5)
            for l in range(L):
                for s in range(4):
                    pool.wait_ge(emptied[s], uses_before(l, s) + 1)
                if l:
                    pool.wait_ge(x_ready, 1 + 2 * l)
                pool.dma_start(udram.ap().rearrange("(k p) c -> p k c", p=128), u).then_inc(u_out, 16)
                nc.gpsimd.memset(U[0:64, :, 0:NB], 0.0).then_inc(u_zero, 1)
                pool.wait_ge(u_out, 16 * (l + 1))
                uv = udram.ap().rearrange("(g h) c -> h g c", h=GC)
                for r in range(CH):
                    j = CH - 1 - r
                    rows = slice(GC * r, GC * r + GC)
                    pool.dma_start(U[rows, :, NB:CW], uv[:, :, NC * j:NC * j + NC]).then_inc(u_in, 16)
                    if j < DT:
                        pool.dma_start(U[rows, :, 0:NB], uv[:, :, SEQ + NB * j:SEQ + NB * j + NB]).then_inc(u_in, 16)
                    else:
                        jj = j - DT
                        pool.dma_start(U2[rows, :, :], uv[:, :, SEQ + NB * jj:SEQ + NB * jj + NB]).then_inc(u_in, 16)
                for hf in range(2):
                    v = 2 * l + hf
                    if hf:
                        pool.wait_ge(y_ready, v)
                    pool.dma_start(ph[:, par_at:par_at + HP * PAR_F], io["ssm_t"][l, hf]).then_inc(par_in, 16)
                    nc.gpsimd.memset(toep[:, :, :], 0.0).then_inc(toep_zero, 1)
                    pool.wait_ge(kd_ready, v + 1)
                    pool.wait_ge(toep_zero, v + 1)
                    for s in range(CH):
                        r = CH - 1 - s
                        pool.dma_start(toep[GC * r:GC * r + GC, :, GC * s:128],
                                       Kd[:, :, 0:128 - GC * s]).then_inc(toep_in, 16)
                    pool.wait_ge(h_ready, v + 1)
                    pool.dma_start(io["o_h"][l, hf], hout[:, :, :, :].rearrange("p k e b -> p (k e b)")).then_inc(stored, 16)
                    pool.wait_ge(y_ready, v + 1)
                    yv = ydram.ap().rearrange("(g h) c -> h g c", h=GC)[:, HG * hf:HG * hf + HG, :]
                    for t in range(CH):
                        rows = slice(GC * t, GC * t + GC)
                        pool.dma_start(yv[:, :, NC * t:NC * t + NC], Y[rows, :, NB:CW]).then_inc(y_out, 16)
                        if t < DT:
                            pool.dma_start(yv[:, :, SEQ + NB * t:SEQ + NB * t + NB], Y[rows, :, 0:NB]).then_inc(y_out, 16)
                    pool.wait_ge(y_out, 16 * 12 * (v + 1))
                pool.wait_ge(stored, 16 * (2 * (l + 1) + 4 * l))
                pool.dma_start(cat[:, 0:4, :], ydram.ap().rearrange("(k p) c -> p k c", p=128)).then_inc(y_in, 16)
                def load_pages(r, kinds, done):
                    with pool.Fori(0, 16) as i:
                        pg = pool.value_load(ptab[0:1, bass.ds(i + 16 * r, 1)], min_val=0, max_val=NPOOL - 1)
                        for dst, src in kinds:
                            pool.dma_start(dst[:, bass.ds(i, 1), :],
                                           src[l, bass.ds(pg, 1), :, :].rearrange("o p c -> p o c")).then_inc(done, 16)

                index_pages = ((pgI[0:64], io["c_i"]), (pgI[64:128], io["c_i"]))
                kv_pages = ((pgK, io["c_k"]), (pgV, io["c_v"]))
                load_pages(0, index_pages, pages_in)
                load_pages(0, kv_pages, pages_kv)
                pool.wait_ge(tok_ready, 2 * l + 2)
                pool.dma_start(io["o_k"][l], kn[:, :]).then_inc(stored, 16)
                pool.dma_start(io["o_v"][l, :, 0:NQT, :], vtok[:, 0:NQT, :]).then_inc(stored, 16)
                pool.dma_start(io["o_v"][l, 0:NS, NQT, :], vtok[0:NS, NQT, :]).then_inc(stored, 16)
                pool.dma_start(io["o_ki"][l], kin[0:64, :]).then_inc(stored, 16)
                pool.wait_ge(si_mm, 2 * l + 1)
                load_pages(1, index_pages, pages_in)
                pool.wait_ge(spv_ready, 2 * l + 1)
                load_pages(1, kv_pages, pages_kv)
                pool.wait_ge(spv_ready, 2 * l + 2)
                pool.dma_start(pt[:, :, :], io["p_t"][l]).then_inc(pt_in, 16)
            pool.wait_ge(x_ready, 1 + 2 * L)
            pool.dma_start(io["o_y"], x[:, :, :]).then_inc(stored, 16)
            pool.wait_ge(stored, 16 * (6 * L + 1))

        @block.tensor
        def _(pe):
            mm = nc.tensor.matmul
            c = Count()

            def begin(s):
                n = c.take(s)
                if n > 1:
                    pe.wait_ge(emptied[s], n - 1)
                return n

            def all_empty():
                for s in range(4):
                    if c.n[s]:
                        pe.wait_ge(emptied[s], c.n[s])

            def product(s, w, kcs, rhs, split, rows=128, note=None):
                for half, (a, b) in enumerate(((0, split), (split, T))):
                    for i, kc in enumerate(kcs):
                        last = mm(pair[s][0:rows, 512 * half:512 * half + b - a], w(kc), rhs(kc)[:, a:b],
                                  start=(i == 0), stop=(i == len(kcs) - 1))
                        if note is not None and half == 0 and i == 0:
                            last.then_inc(note, 1)
                last.then_inc(filled[s], 1)

            def job(n, s, cols, kcs, rhs, split=T // 2):
                begin(s)
                pe.wait_ge(w_loaded[n % RING], 16 * (n // RING + 1))
                product(s, lambda kc: ring[:, n % RING, cols * kc:cols * kc + 128], kcs, rhs, split, note=jobs_begun)

            def layer_norm(k):
                if k == 0:
                    pe.wait_ge(x_in, 32)
                    pe.wait_ge(ones_set, 1)
                src = x if k == 0 else acc
                begin(0)
                if k:
                    pe.wait_ge(acc_ready, k)
                product(0, lambda kc: ones[:, :], range(KC), lambda kc: src[:, kc, :], T // 2)
                begin(1)
                pe.wait_ge(squares, k + 1)
                product(1, lambda kc: ones[:, :], range(KC), lambda kc: cat[:, kc, :], T // 2)

            pe.wait_ge(rel_in, 32)
            pe.wait_ge(consts_in, 80)
            for h in range(NH):
                p = pair[h % 2]
                if h >= 2:
                    pe.wait_ge(f_ready, h - 1)
                mm(p[:, 0:512], relb[0:32, h, :], cst[0:32, C_OF:C_OF + 512], start=True, stop=True)
                mm(p[:, 512:512 + 128], relb[0:32, h, :], cst[0:32, C_OF + 512:C_OF + BW], start=True, stop=True).then_inc(f_mm, 1)
            pe.wait_ge(tk_ready, 1)
            mm(pair[2][:, 0:512], reltk, cst[:, C_TK:C_TK + 512], start=True, stop=True)
            mm(pair[2][:, 512:512 + NS], reltk, cst[:, C_TK + 512:C_TK + SK], start=True, stop=True).then_inc(bs_mm, 1)
            pe.wait_ge(f_ready, NH)
            pe.wait_ge(bs_ready, 1)
            layer_norm(0)

            for l in range(L):
                n = JOBS[l]
                xr = lambda kc: x[:, kc, :]
                pe.wait_ge(x_ready, 1 + 2 * l)
                for m in range(WIN_T - 1):
                    job(n + m, m % 4, 128, range(KC), xr, split=256)
                nv = n + WIN_T - 1
                job(nv, 2, 136, range(KC), xr, split=256)
                begin(3)
                product(3, lambda kc: ring[:, nv % RING, 136 * kc + 128:136 * kc + 136], range(KC), xr, 256, rows=NH)
                n += WIN_T
                all_empty()
                if l == 0:
                    pe.wait_ge(consts_in, 80)
                for b in range(NQT):
                    nc.tensor.transpose(bank(0)[:, 128 * b:128 * b + 128], vn[:, 128 * b:128 * b + 128], ident)
                    nc.tensor.transpose(bank(2)[:, NH * b:NH * b + NH], wn[:, 128 * b:128 * b + 128], cst[0:NH, C_ID:C_ID + NH])
                nc.tensor.transpose(bank(1)[0:NS, 0:128], vn[:, SEQ:T], ident).then_inc(tok_mm, 1)

                for hf in range(2):
                    v = 2 * l + hf + 1
                    if hf == 0:
                        pe.wait_ge(tok_ready, 2 * l + 2)
                    pe.wait_ge(bp_ready, v)
                    if hf:
                        pe.wait_ge(h_ready, v - 1)
                    for k in range(2):
                        for e in range(HP):
                            last = nc.tensor.transpose(pair[k][:, 128 * e:128 * e + 128],
                                                       BP[k][:, e].rearrange("p m c -> p (m c)"), ident)
                    last.then_inc(bt_mm, 1)
                    pe.wait_ge(cp_ready, v)
                    if hf:
                        pe.wait_ge(y_ready, v - 1)
                    for g in range(HG):
                        e, lo = g // 2, 64 * (g % 2)
                        o = pair[2 + g % 2][0:GC, 128 * e:128 * e + 128]
                        for k in range(2):
                            last = mm(o, Bb[k][lo:lo + 64, e], CP[k][lo:lo + 64, e, 0:CH].rearrange("p m c -> p (m c)"),
                                      start=(k == 0), stop=(k == 1))
                    last.then_inc(kd_mm, 1)
                    pe.wait_ge(bt_ready, v)
                    pe.wait_ge(u_in, 256 * (l + 1))
                    pe.wait_ge(u_zero, l + 1)
                    for k in range(2):
                        for gl in range(HG):
                            e, lo, g = gl // 2, 64 * (gl % 2), HG * hf + gl
                            mm(bank(k)[lo:lo + 64, NC * e:NC * e + NC], BT[:, k, e, lo:lo + 64], U[:, g, NB:CW],
                               start=True, stop=True)
                            last = mm(bank(2)[lo:lo + 64, 64 * k + NB * e:64 * k + NB * e + NB], BT[0:64, k, e, lo:lo + 64],
                                      U2[0:64, g, :], start=True, stop=True)
                    last.then_inc(g_mm, 1)
                    pe.wait_ge(h_ready, v)
                    pe.wait_ge(toep_in, 128 * v)
                    for gl in range(HG):
                        e, lo, g = gl // 2, 64 * (gl % 2), HG * hf + gl
                        o = bank(4 + 2 * (gl % 2) + e // 6)[:, CW * (e % 6):CW * (e % 6) + CW]
                        mm(o, toep[:, HP * (gl % 2) + e, :], U[:, g, :], start=True, stop=False)
                        for k in range(2):
                            last = mm(o, CP[k][lo:lo + 64, e, 1:CH + 1].rearrange("p m c -> p (m c)"),
                                      H[k][lo:lo + 64, e, 0:CW], start=False, stop=(k == 1))
                    last.then_inc(y_mm, 1)

                pe.wait_ge(y_ready, 2 * l + 2)
                ni, nl, npt = 8 * 3 * l, 8 * NQT * l, 20 * l
                for b in range(NQT):
                    w = 128 * (b + 1)
                    qs = slice(128 * b, 128 * b + 128)
                    if b:
                        for h in range(NH):
                            lo = 64 * (h % 2)
                            if ni >= 2:
                                pe.wait_ge(relu_ready, ni - 1)
                            mm(bank(ni % 2)[:, 0:w], qi[lo:lo + 64, h // 2, qs], kin[lo:lo + 64, 0:w],
                               start=True, stop=True).then_inc(idx_mm, 1)
                            ni += 1
                    for h in range(NH):
                        lo = 64 * (h // 4)
                        if nl >= 3:
                            pe.wait_ge(lg_used, nl - 2)
                        mm(bank(2 + nl % 3)[:, 0:w], q[lo:lo + 64, h % 4, qs], kn[lo:lo + 64, 0:w],
                           start=True, stop=True).then_inc(lg_mm, 1)
                        nl += 1
                    pe.wait_ge(prob_ready, NQT * l + b + 1)
                    for g in range(2):
                        for kt in range(b + 1):
                            if npt >= 2:
                                pe.wait_ge(pt_ready, npt - 1)
                            for i in range(4):
                                last = nc.tensor.transpose(bank(5 + npt % 2)[:, 128 * i:128 * i + 128],
                                                           Lg[:, 4 * g + i, 128 * kt:128 * kt + 128], ident)
                            last.then_inc(pt_mm, 1)
                            npt += 1
                    pe.wait_ge(pt_ready, npt)
                    nb = NQT * l + b
                    if nb:
                        pe.wait_ge(pv_ready, nb)
                    for g in range(2):
                        for kt in range(b + 1):
                            last = mm(bank(7)[64 * g:64 * g + 64, :], vtok[:, kt, 64 * g:64 * g + 64], PT[:, g, kt, :],
                                      start=(kt == 0), stop=(kt == b))
                    last.then_inc(pv_mm, 1)

                pe.wait_ge(pv_ready, NQT * (l + 1))
                mm(bank(4)[:, 0:NS], cst[0:NH, C_OH:C_OH + 128], wn[0:NH, SEQ:T], start=True, stop=True).then_inc(wr_mm, 1)
                pe.wait_ge(wr_ready, l + 1)
                pe.wait_ge(qz_ready, l + 1)
                for r in range(2):
                    v = 2 * l + r + 1
                    pe.wait_ge(pages_in, 512 * v)
                    if r:
                        pe.wait_ge(srelu, v - 1)
                    lz = Qzi[:, 4 * r:4 * r + 4].rearrange("p b a i t -> p (b a i t)")
                    for bi in range(4):
                        mm(bank(0)[32 * bi:32 * bi + 32, :], lz[:, 32 * bi:32 * bi + 32],
                           pgI[:, 4 * bi:4 * bi + 4, :], start=True, stop=True)
                    mm(bank(1)[:, 0:NS], lz, kin[:, SEQ:T], start=True, stop=True).then_inc(si_mm, 1)
                    pe.wait_ge(srelu, v)
                    mm(bank(2)[0:NS, :], wr[:, r, :], rls[:, 0:PAST], start=(r == 0), stop=(r == 1))
                    mm(bank(3)[0:NS, 0:NS], wr[:, r, :], rls[:, PAST:SK], start=(r == 0), stop=(r == 1)).then_inc(sc_mm, 1)
                pe.wait_ge(nosel_ready, l + 1)
                for r in range(2):
                    v = 2 * l + r + 1
                    lz = Qz[:, 4 * r:4 * r + 4].rearrange("p b a i t -> p (b a i t)")
                    ex = cst[0:NS, C_EX + 128 * r:C_EX + 128 * r + 128]
                    pe.wait_ge(pages_kv, 512 * v)
                    if r:
                        pe.wait_ge(spv_ready, v - 1)
                    mm(bank(0), ex, nss[0:NS, 0:PAST], start=True, stop=False)
                    for bi in range(4):
                        mm(bank(0)[32 * bi:32 * bi + 32, :], lz[:, 32 * bi:32 * bi + 32],
                           pgK[:, 4 * bi:4 * bi + 4, :], start=False, stop=True)
                    mm(bank(1)[:, 0:NS], ex, nss[0:NS, PAST:SK], start=True, stop=False)
                    mm(bank(1)[:, 0:NS], lz, kn[:, SEQ:T], start=False, stop=True).then_inc(sl_mm, 1)
                    pe.wait_ge(sprob, v)
                    for k in range(NPG):
                        nc.tensor.transpose(bank(4)[:, 128 * k:128 * k + 128], Ls[:, 128 * k:128 * k + 128], ident)
                    nc.tensor.transpose(bank(5)[0:NS, 0:128], Ls[:, PAST:SK], ident).then_inc(spt_mm, 1)
                    pe.wait_ge(spt_ready, v)
                    for bi in range(4):
                        o = bank(6)[:, 32 * bi:32 * bi + 32]
                        for k in range(NPG):
                            mm(o, pgV[:, NPG * bi + k, :], PTs[:, k, 32 * bi:32 * bi + 32], start=(k == 0), stop=False)
                        last = mm(o, vtok[0:NS, NQT, :], PTs[0:NS, NPG, 32 * bi:32 * bi + 32], start=False, stop=True)
                    last.then_inc(spv_mm, 1)

                pe.wait_ge(spv_ready, 2 * l + 2)
                pe.wait_ge(gelu_ready, l + 1)
                for m in range(8):
                    job(n + m, m % 4, 128, range(4), lambda kc: u[:, kc, :])
                n += 8
                for m in range(8):
                    if m == 0:
                        pe.wait_ge(emptied[2], c.n[2])
                        pe.wait_ge(emptied[0], c.n[0])
                    job(n + m, m % 4, 128, range(KC), lambda kc: cat[:, kc, :])
                n += 8
                layer_norm(1 + 2 * l)
                pe.wait_ge(x_ready, 2 + 2 * l)
                pe.wait_ge(pt_in, 16 * (l + 1))
                for m in range(8):
                    job(n + m, (2 * m) % 4, 128, range(KC), xr)
                    s = (2 * m + 1) % 4
                    begin(s)
                    product(s, lambda kc: ring[:, (n + m) % RING, 1024 + 128 * kc:1152 + 128 * kc], range(2),
                            lambda kc: pt[:, kc, :], T // 2)
                n += 8
                if l == 1:
                    all_empty()
                    for tt in range(5):
                        rows = 128 if tt < 4 else NS
                        for kc in range(KC):
                            last = mm(bank(0)[0:rows, NE * tt:NE * tt + NE], x[:, kc, 128 * tt:128 * tt + rows], wrt[:, kc, :],
                                      start=(kc == 0), stop=(kc == KC - 1))
                    last.then_inc(r_mm, 1)
                    pe.wait_ge(gts_ready, 1)
                    for e in range(NE):
                        if e >= 2:
                            pe.wait_ge(gb_ready, e - 1)
                        p = pair[2 + e % 2]
                        for tt in range(5):
                            rows = 128 if tt < 4 else NS
                            last = mm(p[:, 128 * tt:128 * tt + rows], gts[0:rows, tt, e:e + 1].to_broadcast([rows, 128]),
                                      cst[0:rows, C_ID:C_ID + rows], start=True, stop=True)
                        last.then_inc(gb_mm, 1)
                    pe.wait_ge(gb_ready, NE)
                all_empty()
                c0 = list(c.n)
                with pe.Fori(0, experts(l)) as e:
                    k = 0
                    for kind, i, ps in ffn_plan():
                        if kind == "down" and i == 0:
                            pe.wait_ge(hid_ready, e * FT + (FT * (0 if l == 0 else 2) + FT))
                        for s, seen in ps:
                            nn = n + k
                            pe.wait_ge(emptied[s], e * FFN_USES[s] + (c0[s] + seen))
                            pe.wait_ge(w_loaded[nn % RING], e * (16 * BLOCK_JOBS // RING) + 16 * (nn // RING + 1))
                            tile = lambda kc: ring[:, nn % RING, 128 * kc:128 * kc + 128]
                            if kind == "up":
                                product(s, tile, range(KC), xr, T // 2, note=jobs_begun)
                            else:
                                product(s, tile, range(FT), lambda kc: hid[:, kc, :], T // 2, note=jobs_begun)
                            k += 1
                for s in range(4):
                    c.n[s] += FFN_USES[s] * experts(l)
                layer_norm(2 + 2 * l)

        @block.scalar
        def _(act):
            A = nc.scalar.activation
            steps = [0]
            c = Count()

            def link(ins):
                steps[0] += 1
                ins.then_inc(act_step, 1)
                act.wait_ge(act_step, steps[0])

            def got(s):
                act.wait_ge(filled[s], c.take(s))

            def layer_norm(k):
                act.wait_ge(emptied[0], c.take(0))
                src = x if k == 0 else acc
                A(cat[:, :, :], src[:, :, :], ACT.Square).then_inc(squares, 1)
                c.take(1)
                act.wait_ge(rstd, k + 1)
                A(rst, rst, ACT.Sqrt).then_inc(rst_ready, 1)

            for h in range(NH):
                act.wait_ge(f_mm, h + 1)
                A(frow[:, h, 0:512], pair[h % 2][:, 0:512], ACT.Copy)
                A(frow[:, h, 512:BW], pair[h % 2][:, 512:BW], ACT.Copy).then_inc(f_ready, 1)
            layer_norm(0)

            for l in range(L):
                dst = [u[:, k, :] for k in range(4)] + [q[:, k, :] for k in range(4)] + [qi[:, k, :] for k in range(4)]
                dst += [kn[:, :], kin[:, :], vn[:, :], wn[:, :]]
                for m in range(16):
                    s = m % 4
                    got(s)
                    d = dst[m]
                    if m < 4:
                        A(d[:, 0:256], pair[s][:, 0:256], ACT.Copy)
                        A(d[:, 256:T], pair[s][:, 512:512 + T - 256], ACT.Copy).then_inc(emptied[s], 1)
                        continue
                    rows = NH if m == 15 else 128
                    dn = d[:, 0:SEQ].rearrange("p (c j) -> p j c", j=CH)
                    A(dn[:, 0:4, :], pair[s][0:rows, 0:256].rearrange("p (j c) -> p j c", j=4), ACT.Copy)
                    A(dn[:, 4:8, :], pair[s][0:rows, 512:768].rearrange("p (j c) -> p j c", j=4), ACT.Copy)
                    A(d[:, SEQ:T], pair[s][0:rows, 768:768 + NS], ACT.Copy).then_inc(emptied[s], 1)
                act.wait_ge(tok_mm, l + 1)
                A(vtok[:, 0:NQT, :], bank(0).rearrange("p (b c) -> p b c", b=NQT), ACT.Copy)
                A(vtok[0:NS, NQT, :], bank(1)[0:NS, 0:128], ACT.Copy).then_inc(tok_ready, 1)
                A(wtok[:, :, :], bank(2)[:, 0:NQT * NH].rearrange("p (b c) -> p b c", b=NQT), ACT.Copy).then_inc(tok_ready, 1)

                for hf in range(2):
                    v = 2 * l + hf + 1
                    act.wait_ge(par_in, 16 * v)
                    A(sm[:, 0, :], par[:, 2, :], ACT.Exp).then_inc(ldt, 1)
                    act.wait_ge(theta, 2 * v - 1)
                    A(sm[:, 3, :], sm[:, 1, :], ACT.Exp)
                    A(sm[:, 4, :], sm[:, 1, :], ACT.Exp, scale=float(CH)).then_inc(expd, 1)
                    act.wait_ge(theta, 2 * v)
                    A(sm[:, 5:7, :], sm[:, 7:9, :], ACT.Sin).then_inc(sincos, 1)
                    act.wait_ge(bt_mm, v)
                    for k in range(2):
                        ins = A(BT[:, k].rearrange("p e n -> p (e n)"), pair[k][:, :], ACT.Copy)
                    ins.then_inc(bt_ready, 1)
                    act.wait_ge(kd_mm, v)
                    for k in range(2):
                        ins = A(cf[0:GC, 1024 * k:1024 * k + 1024], pair[2 + k][0:GC, :], ACT.Copy)
                    ins.then_inc(kd_ready, 1)
                    act.wait_ge(y_mm, v)
                    for a in range(2):
                        ya = Y.rearrange("p (e a) c -> p a e c", a=2)[:, a]
                        for k, n in enumerate((6, HP - 6)):
                            ins = A(ya[:, 6 * k:6 * k + n, :], bank(4 + 2 * a + k)[:, 0:CW * n].rearrange("p (g c) -> p g c", g=n), ACT.Copy)
                    ins.then_inc(y_ready, 1)
                act.wait_ge(yd_ready, l + 1)
                A(u, u, ACT.Gelu_apprx_tanh).then_inc(gelu_ready, 1)

                ni, npt = 24 * l, 20 * l
                for b in range(NQT):
                    w = 128 * (b + 1)
                    if b:
                        for h in range(NH):
                            act.wait_ge(idx_mm, ni + 1)
                            if ni >= 4:
                                act.wait_ge(relu_used, ni - 3)
                            A(rl[:, ni % 4, 0:w], bank(ni % 2)[:, 0:w], ACT.Relu).then_inc(relu_ready, 1)
                            ni += 1
                    for h in range(NH):
                        act.wait_ge(nmx_ready, NH * (NQT * l + b) + h + 1)
                        A(Lg[:, h, 0:w], Lg[:, h, 0:w], ACT.Exp, bias=nmx[:, h:h + 1],
                          accum_out=sums[:, h:h + 1]).then_inc(exp_ready, 1)
                    act.wait_ge(rs_ready, NQT * l + b + 1)
                    for h in range(NH):
                        ins = A(Lg[:, h, 0:w], Lg[:, h, 0:w], ACT.Copy, scale=rs[:, h:h + 1])
                    ins.then_inc(prob_ready, 1)
                    for g in range(2):
                        for kt in range(b + 1):
                            act.wait_ge(pt_mm, npt + 1)
                            A(PT[:, g, kt, :], bank(5 + npt % 2), ACT.Copy).then_inc(pt_ready, 1)
                            npt += 1
                    act.wait_ge(pv_mm, NQT * l + b + 1)
                    for i in range(4):
                        o = cat[:, 4 + i, 0:SEQ].rearrange("p (j c) -> p c j", j=CH)[:, 16 * b:16 * b + 16, :]
                        ins = A(o, bank(7)[:, 128 * i:128 * i + 128].rearrange("p (c j) -> p c j", j=CH), ACT.Copy)
                    ins.then_inc(pv_ready, 1)

                for r in range(2):
                    v = 2 * l + r + 1
                    act.wait_ge(si_mm, v)
                    if r:
                        act.wait_ge(sc_mm, v - 1)
                    A(rls[:, 0:PAST], bank(0), ACT.Relu)
                    A(rls[:, PAST:SK], bank(1)[:, 0:NS], ACT.Relu).then_inc(srelu, 1)
                for r in range(2):
                    v = 2 * l + r + 1
                    act.wait_ge(snmx, v)
                    A(Ls, Ls, ACT.Exp, bias=nms[:, 0:1], accum_out=nms[:, 1:2]).then_inc(sexp, 1)
                    act.wait_ge(spt_mm, v)
                    A(PTs[:, 0:NPG, :], bank(4).rearrange("p (k c) -> p k c", k=NPG), ACT.Copy)
                    A(PTs[0:NS, NPG, :], bank(5)[0:NS, 0:128], ACT.Copy).then_inc(spt_ready, 1)
                    act.wait_ge(spv_mm, v)
                    pv = bank(6)[:, 0:128].rearrange("p (b g i t) -> p g b i t", b=4, g=2, i=4)
                    for g in range(2):
                        for i in range(4):
                            o = cat[64 * g:64 * g + 64, 4 + i, SEQ:T].rearrange("p (t b) -> p b t", b=NB)[:, 4 * r:4 * r + 4, :]
                            ins = A(o, pv[64 * g:64 * g + 64, g, :, i, :], ACT.Copy)
                    ins.then_inc(spv_ready, 1)

                for m in range(8):
                    s = m % 4
                    if m % 2 == 0:
                        a_use = c.take(s)
                        continue
                    got(s)
                    act.wait_ge(emptied[s - 1], a_use - 1)
                    A(halves(sg[:, m // 2 % 2, :]), even(s), ACT.Sigmoid).then_inc(emptied[s], 1)
                for m in range(8):
                    c.take(m % 4)
                layer_norm(1 + 2 * l)
                for m in range(8):
                    s = (2 * m) % 4
                    got(s)
                    c.take(s + 1)
                    if m >= 2:
                        act.wait_ge(ple_used, 8 * l + m - 1)
                    A(halves(sg[:, m % 2, :]), even(s), ACT.Sigmoid).then_inc(emptied[s], 1)
                if l == 1:
                    act.wait_ge(gdiff, 1)
                    A(rlog, rlog, ACT.Exp).then_inc(gexp, 1)
                    A(rsm[:, :, 1:2], rsm[:, :, 0:1], ACT.Exp).then_inc(gexp, 1)
                    for e in range(NE):
                        act.wait_ge(gb_mm, e + 1)
                        A(gb[:, e, :], pair[2 + e % 2][:, 0:T], ACT.Copy).then_inc(gb_ready, 1)
                act.wait_ge(ple_used, 8 * (l + 1))
                c0 = list(c.n)
                with act.Fori(0, experts(l)) as e:
                    for kind, f, ps in ffn_plan():
                        if kind == "up":
                            (s, seen), (s2, seen2) = ps
                            act.wait_ge(filled[s], e * FFN_USES[s] + (c0[s] + seen + 1))
                            if f >= 2:
                                act.wait_ge(emptied[s2], e * FFN_USES[s2] + (c0[s2] + seen2))
                            A(halves(sg[:, f % 2, :]), even(s), ACT.Silu).then_inc(emptied[s], 1)
                for s in range(4):
                    c.n[s] += FFN_USES[s] * experts(l)
                layer_norm(2 + 2 * l)

        @block.vector
        def _(dve):
            V = nc.vector
            MAGIC = 1.5 * 2.0 ** 23
            TWO_PI = (6.28125, 1.93500518798828125e-3, 2 * math.pi - 6.28125 - 1.93500518798828125e-3)
            steps = [0]
            c = Count()

            def link(ins):
                steps[0] += 1
                ins.then_inc(dve_step, 1)
                dve.wait_ge(dve_step, steps[0])

            def got(s):
                dve.wait_ge(filled[s], c.take(s))

            def layer_norm(k):
                src = x if k == 0 else acc
                got(0)
                for h in range(2):
                    cols = slice(T // 2 * h, T // 2 * h + T // 2)
                    ins = V.tensor_tensor(src[:, :, cols], src[:, :, cols],
                                          bc(pair[0][:, 512 * h:512 * h + T // 2], 1, KC), ALU.subtract)
                ins.then_inc(emptied[0], 1)
                got(1)
                ins = V.tensor_scalar(halves(rst), even(1), LN_EPS, None, ALU.add)
                ins.then_inc(emptied[1], 1)
                dve.wait_ge(emptied[1], c.n[1])
                V.reciprocal(rst, rst).then_inc(rstd, 1)
                dve.wait_ge(rst_ready, k + 1)
                link(V.tensor_tensor(src[:, :, :], src[:, :, :], bc(rst, 1, KC), ALU.mult))
                for kc in range(KC):
                    ins = V.tensor_scalar(x[:, kc, :], src[:, kc, :], lnp[:, 2 * k, kc:kc + 1], lnp[:, 2 * k + 1, kc:kc + 1],
                                          ALU.mult, ALU.add)
                ins.then_inc(x_ready, 1)

            def cmul(o, a, b, t1, t2, negate_im=False):
                V.tensor_tensor(t1, a[0], b[0], ALU.mult)
                link(V.tensor_tensor(t2, a[1], b[1], ALU.mult))
                link(V.tensor_tensor(o[0], t1, t2, ALU.subtract))
                V.tensor_tensor(t1, a[0], b[1], ALU.mult)
                link(V.tensor_tensor(t2, a[1], b[0], ALU.mult))
                if negate_im:
                    link(V.scalar_tensor_tensor(o[1], t1, -1.0, t2, ALU.mult, ALU.subtract))
                else:
                    link(V.tensor_tensor(o[1], t1, t2, ALU.add))

            def top(vals, work, eight, k, pad=None):
                src, n = vals, vals.shape[1]
                for i in range(k // 8):
                    link(V.max(eight, src))
                    link(V.match_replace(work[:, 0:n], eight, src, GONE))
                    src = work[:, 0:n]
                if k % 8:
                    link(V.max(eight, src))
                    link(V.memset(eight[:, k % 8:8], pad))
                    link(V.match_replace(work, eight, work, GONE))

            dve.wait_ge(consts_in, 80)
            dve.wait_ge(rel_in, 32)
            V.tensor_tensor(reltk, reltk, cst[:, C_MT:C_MT + 128], ALU.mult).then_inc(tk_ready, 1)
            dve.wait_ge(bs_mm, 1)
            V.tensor_copy(bs[:, 0:512], pair[2][:, 0:512])
            V.tensor_copy(bs[:, 512:SK], pair[2][:, 512:SK]).then_inc(bs_ready, 1)
            dve.wait_ge(x_in, 32)
            layer_norm(0)

            for l in range(L):
                for s in range(4):
                    for _ in range(4):
                        c.take(s)
                for hf in range(2):
                    v = 2 * l + hf + 1
                    dve.wait_ge(par_in, 16 * v)
                    dve.wait_ge(ldt, v)
                    if hf == 0:
                        for s in range(4):
                            dve.wait_ge(emptied[s], c.n[s])
                        dve.wait_ge(u_out, 16 * (l + 1))
                    r_ = lambda i: sm[:, i, :]
                    are, aim = par[:, 0, :], par[:, 1, :]
                    V.tensor_tensor(r_(2), aim, r_(0), ALU.mult)
                    V.tensor_tensor(r_(1), are, r_(0), ALU.mult).then_inc(theta, 1)
                    dve.wait_ge(theta, 2 * v - 1)
                    link(V.tensor_scalar(r_(9), r_(2), 1 / (2 * math.pi), MAGIC, ALU.mult, ALU.add))
                    link(V.tensor_scalar(r_(9), r_(9), MAGIC, None, ALU.subtract))
                    for i, part in enumerate(TWO_PI):
                        link(V.scalar_tensor_tensor(r_(7) if i == 2 else r_(2), r_(9), -part, r_(2), ALU.mult, ALU.add))
                    link(V.tensor_scalar(r_(10), r_(7), math.pi / 2, None, ALU.add))
                    link(V.tensor_scalar(r_(11), r_(10), math.pi, 2 * math.pi, ALU.is_gt, ALU.mult))
                    link(V.tensor_tensor(r_(8), r_(10), r_(11), ALU.subtract))
                    V.tensor_scalar(sm[:, 7:9, :], sm[:, 7:9, :], 3.1415925, -3.1415925, ALU.min, ALU.max).then_inc(theta, 1)
                    V.memset(P[0][:, 0, :], 1.0)
                    V.memset(P[1][:, 0, :], 0.0)
                    dve.wait_ge(sincos, v)
                    dve.wait_ge(expd, v)
                    V.tensor_tensor(P[0][:, 1, :], r_(6), r_(3), ALU.mult)
                    link(V.tensor_tensor(P[1][:, 1, :], r_(5), r_(3), ALU.mult))
                    for w in (1, 2, 4):
                        t1 = T1[:, 0:w * HP].rearrange("p (m e) -> p m e", e=HP)
                        t2 = T2[:, 0:w * HP].rearrange("p (m e) -> p m e", e=HP)
                        cmul([P[k][:, w + 1:2 * w + 1, :] for k in range(2)], [P[k][:, 1:w + 1, :] for k in range(2)],
                             [P[k][:, w:w + 1, :].to_broadcast([128, w, HP]) for k in range(2)], t1, t2)
                    V.tensor_scalar(r_(12), P[0][:, 1, :], -1.0, None, ALU.add)
                    V.tensor_tensor(r_(14), are, are, ALU.mult)
                    link(V.tensor_tensor(r_(15), aim, aim, ALU.mult))
                    link(V.tensor_tensor(r_(13), r_(14), r_(15), ALU.add))
                    link(V.reciprocal(r_(16), r_(13)))
                    V.tensor_tensor(r_(14), r_(12), are, ALU.mult)
                    link(V.tensor_tensor(r_(15), P[1][:, 1, :], aim, ALU.mult))
                    link(V.tensor_tensor(r_(17), r_(14), r_(15), ALU.add))
                    V.tensor_tensor(r_(14), P[1][:, 1, :], are, ALU.mult)
                    link(V.tensor_tensor(r_(15), r_(12), aim, ALU.mult))
                    link(V.tensor_tensor(r_(18), r_(14), r_(15), ALU.subtract))
                    V.tensor_tensor(r_(17), r_(17), r_(16), ALU.mult)
                    link(V.tensor_tensor(r_(18), r_(18), r_(16), ALU.mult))
                    t1 = T1[:, 0:HP * GC].rearrange("p (e c) -> p e c", e=HP)
                    t2 = T2[:, 0:HP * GC].rearrange("p (e c) -> p e c", e=HP)
                    cmul(Bb, [bc(r_(17 + k), 2, GC) for k in range(2)], [pB[:, k] for k in range(2)], t1, t2)

                    def powers(o, base, n, **kw):
                        t1 = T1[:, 0:HP * n * GC].rearrange("p (e m c) -> p e m c", e=HP, m=n)
                        t2 = T2[:, 0:HP * n * GC].rearrange("p (e m c) -> p e m c", e=HP, m=n)
                        cmul(o, [bc(P[k][:, 0:n, :].rearrange("p m e -> p e m"), 3, GC) for k in range(2)],
                             [bc(t, 2, n) for t in base], t1, t2, **kw)

                    powers(BP, Bb, CH)
                    V.memset(m8x[:, 0:1], 0.0).then_inc(bp_ready, 1)
                    powers(CP, [pB[:, 2], pB[:, 3]], CH + 1, negate_im=True)
                    V.memset(m8x[:, 0:1], 0.0).then_inc(cp_ready, 1)
                    a, b_ = [r_(6), r_(5)], [r_(19), r_(20)]
                    for o in ([r_(19), r_(20)], [r_(21), r_(22)], [E[k][:, :, 0] for k in range(2)]):
                        cmul(o, a, a, T1[:, 0:HP], T2[:, 0:HP])
                        a = o
                    w = 1
                    while w < NC:
                        t1 = T1[:, 0:HP * w].rearrange("p (e c) -> p e c", e=HP)
                        t2 = T2[:, 0:HP * w].rearrange("p (e c) -> p e c", e=HP)
                        cmul([E[k][:, :, w:2 * w] for k in range(2)], [E[k][:, :, 0:w] for k in range(2)],
                             [E[k][:, :, w - 1:w].to_broadcast([128, HP, w]) for k in range(2)], t1, t2)
                        w *= 2
                    link(V.tensor_copy(R8, bc(r_(4), 2, NC)))
                    link(V.memset(R8[:, :, 0:1], 0.0))
                    dve.wait_ge(g_mm, v)
                    g_in = [bank(k).rearrange("p (e c) -> p e c", e=HP) for k in range(2)]
                    t1 = T1[:, 0:HP * NC].rearrange("p (e c) -> p e c", e=HP)
                    t2 = T2[:, 0:HP * NC].rearrange("p (e c) -> p e c", e=HP)
                    V.tensor_tensor(t1, E[0], g_in[0], ALU.mult)
                    link(V.tensor_tensor(t2, E[1], g_in[1], ALU.mult))
                    link(V.tensor_tensor(GM[0], t1, t2, ALU.add))
                    V.tensor_tensor(t1, E[0], g_in[1], ALU.mult)
                    link(V.tensor_tensor(t2, E[1], g_in[0], ALU.mult))
                    link(V.tensor_tensor(GM[1], t1, t2, ALU.subtract))
                    flat = lambda t: t.rearrange("p e c -> p (e c)")
                    for k in range(2):
                        ins = V.tensor_tensor_scan(flat(GS[k]), flat(R8), flat(GM[k]), 0.0, ALU.mult, ALU.add)
                    link(ins)
                    cmul([H[k][:, :, NB + 1:] for k in range(2)], E, GS, t1, t2)
                    for k in range(2):
                        V.memset(H[k][:, :, NB:NB + 1], 0.0)
                        V.tensor_copy(H[k][:, :, 0:NB], pH[:, k])
                    t1 = T1[:, 0:HP * NB].rearrange("p (e c) -> p e c", e=HP)
                    t2 = T2[:, 0:HP * NB].rearrange("p (e c) -> p e c", e=HP)
                    if hf or l:
                        dve.wait_ge(stored, 16 * (2 * l + hf + 4 * l))
                    so = [hout[:, k, :, 1:NB + 1] for k in range(2)]
                    cmul(so, [bc(P[k][:, DT, :], 2, NB) for k in range(2)], [pH[:, k] for k in range(2)], t1, t2)
                    for k in range(2):
                        V.tensor_tensor(so[k], so[k], bank(2)[:, 64 * k:64 * k + 64].rearrange("p (e b) -> p e b", e=HP), ALU.add)
                        ins = V.tensor_copy(hout[:, k, :, 0:1], H[k][:, :, NB + NC:NB + NC + 1])
                    ins.then_inc(h_ready, 1)

                dve.wait_ge(y_in, 16 * (l + 1))
                for k in range(4):
                    ins = V.scalar_tensor_tensor(u[:, k, :], u[:, k, :], dsk[:, l, k:k + 1], cat[:, k, :], ALU.mult, ALU.add)
                ins.then_inc(yd_ready, 1)

                dve.wait_ge(tok_ready, 2 * l + 2)
                dve.wait_ge(rbias_in, 16)
                ni, nl = 24 * l, NH * NQT * l
                for b in range(NQT):
                    w = 128 * (b + 1)
                    lo = w - 128
                    if b:
                        for h in range(NH):
                            dve.wait_ge(relu_ready, ni + 1)
                            if h == 0:
                                V.tensor_scalar(sc[:, 0:w], rl[:, ni % 4, 0:w], wtok[:, b, h:h + 1], None, ALU.mult).then_inc(relu_used, 1)
                            else:
                                V.scalar_tensor_tensor(sc[:, 0:w], rl[:, ni % 4, 0:w], wtok[:, b, h:h + 1], sc[:, 0:w],
                                                       ALU.mult, ALU.add).then_inc(relu_used, 1)
                            ni += 1
                            dve.wait_ge(relu_used, ni)
                        V.tensor_scalar(sc[:, 0:lo], sc[:, 0:lo], IDX_SCALE, None, ALU.mult)
                        link(V.scalar_tensor_tensor(sc[:, lo:w], sc[:, lo:w], IDX_SCALE, cst[:, C_MC:C_MC + 128], ALU.mult, ALU.add))
                        top(sc[:, 0:w], wk, m8, TOPK_P)
                        link(V.tensor_tensor(nosel[:, 0:w], wk[:, 0:w], sc[:, 0:w], ALU.is_equal))
                        hide = nosel
                    else:
                        hide = cst[:, C_CM:C_CM + 128]
                    if l or b:
                        dve.wait_ge(pt_ready, 20 * l + b * (b + 1))
                    for h in range(NH):
                        dve.wait_ge(lg_mm, nl + 1)
                        V.scalar_tensor_tensor(Lg[:, h, 0:w], bank(2 + nl % 3)[:, 0:w], HD ** -0.5,
                                               rbias[:, h, SEQ - w:SEQ], ALU.mult, ALU.add).then_inc(lg_used, 1)
                        nl += 1
                        dve.wait_ge(lg_used, nl)
                        link(V.scalar_tensor_tensor(Lg[:, h, 0:w], hide[:, 0:w], NEG, Lg[:, h, 0:w], ALU.mult, ALU.add))
                        link(V.tensor_reduce(nmx[:, h:h + 1], Lg[:, h, 0:w], AX.X, ALU.max))
                        V.tensor_scalar(nmx[:, h:h + 1], nmx[:, h:h + 1], -1.0, None, ALU.mult).then_inc(nmx_ready, 1)
                    dve.wait_ge(exp_ready, nl)
                    V.reciprocal(rs, sums).then_inc(rs_ready, 1)

                dve.wait_ge(pv_ready, NQT * (l + 1))
                V.memset(Qzi, 0.0)
                link(V.memset(Qz, 0.0))
                for a in range(2):
                    for dst, src in ((Qzi, qi), (Qz, q)):
                        for i in range(4):
                            ins = V.tensor_copy(dst[64 * a:64 * a + 64, :, a, i, :],
                                                src[64 * a:64 * a + 64, i, SEQ:T].rearrange("p (t b) -> p b t", b=NB))
                ins.then_inc(qz_ready, 1)
                dve.wait_ge(wr_mm, l + 1)
                for r in range(2):
                    ins = V.tensor_tensor(wr[:, r, :], bank(4)[:, 0:NS], cst[:, C_MW + NS * r:C_MW + NS * r + NS], ALU.mult)
                ins.then_inc(wr_ready, 1)
                dve.wait_ge(sc_mm, 2 * l + 2)
                V.tensor_scalar(scs[0:NS, 0:PAST], bank(2)[0:NS, :], IDX_SCALE, None, ALU.mult)
                V.memset(wks[0:NS, SK:SK + 7], 3.0e38)
                link(V.scalar_tensor_tensor(scs[0:NS, PAST:SK], bank(3)[0:NS, 0:NS], IDX_SCALE, cst[0:NS, C_MS:C_MS + NS],
                                            ALU.mult, ALU.add))
                top(scs[0:NS, :], wks[0:NS, :], m8s[0:NS, :], TOPK_S, 3.0e38)
                link(V.tensor_tensor(nss[0:NS, :], wks[0:NS, 0:SK], scs[0:NS, :], ALU.is_equal))
                V.tensor_scalar(nss[0:NS, :], nss[0:NS, :], NEG, None, ALU.mult).then_inc(nosel_ready, 1)
                for r in range(2):
                    v = 2 * l + r + 1
                    dve.wait_ge(sl_mm, v)
                    if r:
                        dve.wait_ge(spt_ready, v - 1)
                    V.scalar_tensor_tensor(Ls[:, 0:PAST], bank(0), HD ** -0.5, bs[:, 0:PAST], ALU.mult, ALU.add)
                    link(V.scalar_tensor_tensor(Ls[:, PAST:SK], bank(1)[:, 0:NS], HD ** -0.5, bs[:, PAST:SK], ALU.mult, ALU.add))
                    link(V.tensor_reduce(nms[:, 0:1], Ls, AX.X, ALU.max))
                    V.tensor_scalar(nms[:, 0:1], nms[:, 0:1], -1.0, None, ALU.mult).then_inc(snmx, 1)
                    dve.wait_ge(sexp, v)
                    link(V.reciprocal(nms[:, 2:3], nms[:, 1:2]))
                    V.tensor_scalar(Ls, Ls, nms[:, 2:3], None, ALU.mult).then_inc(sprob, 1)

                for m in range(0, 8, 2):
                    s = m % 4
                    got(s)
                    dve.wait_ge(emptied[s + 1], c.take(s + 1))
                    V.tensor_tensor(halves(cat[:, m // 2, :]), halves(sg[:, m // 2 % 2, :]), even(s), ALU.mult).then_inc(emptied[s], 1)
                for m in range(8):
                    s = m % 4
                    got(s)
                    V.scalar_tensor_tensor(halves(acc[:, m, :]), halves(x[:, m, :]), ALPHA, even(s), ALU.mult, ALU.add).then_inc(emptied[s], 1)
                for s in range(4):
                    dve.wait_ge(emptied[s], c.n[s])
                V.memset(m8x[:, 0:1], 0.0).then_inc(acc_ready, 1)
                layer_norm(1 + 2 * l)
                for m in range(8):
                    s = (2 * m) % 4
                    dve.wait_ge(emptied[s], c.take(s))
                    got(s + 1)
                    sv = halves(sg[:, m % 2, :])
                    V.tensor_tensor(sv, sv, even(s + 1), ALU.mult).then_inc(emptied[s + 1], 1)
                    dve.wait_ge(emptied[s + 1], c.n[s + 1])
                    V.scalar_tensor_tensor(acc[:, m, :], x[:, m, :], ALPHA, sg[:, m % 2, :], ALU.mult, ALU.add).then_inc(ple_used, 1)
                if l == 1:
                    link(V.memset(rlog, 0.0))
                    dve.wait_ge(r_mm, 1)
                    V.tensor_tensor(rlog[:, 0:4, :], bank(0)[:, 0:4 * NE].rearrange("p (n e) -> p n e", n=4), bc(brt[:, :], 1, 4), ALU.add)
                    V.memset(rwk, 3.0e38)
                    link(V.tensor_tensor(rlog[0:NS, 4, :], bank(0)[0:NS, 4 * NE:5 * NE], brt[0:NS, :], ALU.add))
                    V.tensor_copy(rwk[:, :, 0:NE], rlog)
                    for tt in range(5):
                        ins = V.max(rtop[:, tt, :], rlog[:, tt, :])
                    link(ins)
                    V.tensor_copy(rtwo[:, :, 0:2], rtop[:, :, 0:2])
                    link(V.memset(rtwo[:, :, 2:8], 3.0e38))
                    for tt in range(5):
                        ins = V.match_replace(rwk[:, tt, :], rtwo[:, tt, :], rwk[:, tt, :], GONE)
                    link(ins)
                    link(V.tensor_tensor(gts, rwk[:, :, 0:NE], rlog, ALU.not_equal))
                    V.tensor_tensor(rlog, rlog, rtop[:, :, 0:1].to_broadcast([128, 5, NE]), ALU.subtract)
                    V.tensor_tensor(rsm[:, :, 0:1], rtop[:, :, 1:2], rtop[:, :, 0:1], ALU.subtract).then_inc(gdiff, 1)
                    dve.wait_ge(gexp, 2)
                    link(V.tensor_scalar(rsm[:, :, 2:3], rsm[:, :, 1:2], 1.0, None, ALU.add))
                    link(V.reciprocal(rsm[:, :, 3:4], rsm[:, :, 2:3]))
                    link(V.tensor_tensor(gts, gts, rlog, ALU.mult))
                    V.tensor_tensor(gts, gts, rsm[:, :, 3:4].to_broadcast([128, 5, NE]), ALU.mult).then_inc(gts_ready, 1)
                    dve.wait_ge(gb_ready, NE)
                c0 = list(c.n)
                with dve.Fori(0, experts(l)) as e:
                    for kind, i, ps in ffn_plan():
                        def count(s, seen):
                            return e * FFN_USES[s] + (c0[s] + seen + 1)
                        if kind == "up":
                            (s, seen), (s2, seen2) = ps
                            dve.wait_ge(emptied[s], count(s, seen))
                            dve.wait_ge(filled[s2], count(s2, seen2))
                            V.tensor_tensor(halves(hid[:, i, :]), halves(sg[:, i % 2, :]), even(s2), ALU.mult).then_inc(emptied[s2], 1)
                            dve.wait_ge(emptied[s2], count(s2, seen2))
                            if l == 0:
                                V.memset(m8x[:, 0:1], 0.0).then_inc(hid_ready, 1)
                            else:
                                V.tensor_tensor(hid[:, i, :], hid[:, i, :], gb[:, bass.ds(e, 1), :].rearrange("p o t -> p (o t)"),
                                                ALU.mult).then_inc(hid_ready, 1)
                        else:
                            (s, seen), = ps
                            dve.wait_ge(filled[s], count(s, seen))
                            V.tensor_tensor(halves(acc[:, i, :]), halves(acc[:, i, :]), even(s), ALU.add).then_inc(emptied[s], 1)
                for s in range(4):
                    c.n[s] += FFN_USES[s] * experts(l)
                    dve.wait_ge(emptied[s], c.n[s])
                V.memset(m8x[:, 0:1], 0.0).then_inc(acc_ready, 1)
                layer_norm(2 + 2 * l)


def _bucket(dist):
    import numpy as np
    n = np.maximum(dist, 0)
    big = 16 + (np.log(np.maximum(n, 1).astype(np.float32) / np.float32(16)) / np.float32(math.log(8.0)) * np.float32(16)).astype(np.int32)
    return np.where(n < 16, n, np.minimum(big, 31))


def _consts():
    import numpy as np
    c = np.zeros((128, C_END), np.float32)
    c[:, C_ID:C_ID + 128] = np.eye(128)
    p, f = np.arange(128)[:, None], np.arange(128)[None, :]
    c[:, C_CM:C_CM + 128] = f > p
    c[:, C_MC:C_MC + 128] = np.where(f > p, NEG, 0.0)
    row = np.arange(128)
    bi, a, i, t = row // 32, row // 16 % 2, row // 4 % 4, row % 4
    ys = np.arange(NS)
    yt, yb = ys // NB, ys % NB
    for r in range(2):
        same = (yt[:, None] == t[None]) & (yb[:, None] == 4 * r + bi[None])
        c[0:NS, C_EX + 128 * r:C_EX + 128 * r + 128] = same
        c[:, C_MW + NS * r:C_MW + NS * r + NS] = same.T
    c[0:NH, C_OH:C_OH + 128] = np.arange(NH)[:, None] == (2 * i + a)[None]
    c[0:NS, C_MS:C_MS + NS] = np.where((yb[None] == yb[:, None]) & (yt[None] <= yt[:, None]), 0.0, NEG)
    tk = np.arange(128)
    kt, kb = tk // 32, tk % 32
    past = PAST + kt[:, None] - np.arange(PAST)[None]
    new = kt[:, None] - yt[None]
    c[:, C_TK:C_TK + PAST + NS] = _bucket(np.concatenate([past, new], 1)) == kb[:, None]
    c[:, C_MT:C_MT + 128] = kt[:, None] == t[None]
    c[0:32, C_OF:C_OF + BW] = np.arange(32)[:, None] == _bucket(SEQ - 1 - np.arange(BW))[None]
    return c


def _tokens(prompt, sample):
    import numpy as np
    f = prompt.shape[-1]
    a = np.concatenate([prompt.reshape(NC, CH, f).transpose(1, 0, 2).reshape(SEQ, f),
                        sample.transpose(1, 0, 2).reshape(NS, f)], 0)
    return np.ascontiguousarray(a.T.reshape(f // 128, 128, T).transpose(1, 0, 2))


def _tiles(w):
    k, m = w.shape
    return w.reshape(k // 128, 128, m // 128, 128).transpose(2, 1, 0, 3).reshape(m // 128, 128, k)


def _vec(v):
    return v.reshape(-1, 128).T


_OUTS = {"o_y": (128, KC, T), "o_k": (L, 128, T), "o_v": (L, 128, NQT + 1, 128), "o_ki": (L, 64, T),
         "o_h": (L, 2, 128, 2 * HP * (NB + 1))}


def _layout(a):
    import numpy as np
    o = {}
    o["x_t"] = _tokens(a["x_prompt"][0], a["x_sample"])
    o["p_t"] = np.stack([_tokens(a["p_prompt"][l, 0], a["p_sample"][l]) for l in range(L)])
    ln = [a["ln_emb_g"], a["ln_emb_b"]]
    for l in range(L):
        ln += [a["ln1_g"][l], a["ln1_b"][l], a["ln2_g"][l], a["ln2_b"][l]]
    o["ln_p"] = np.stack([_vec(v) for v in ln], 1)
    o["d_t"] = np.stack([_vec(a["ssm_d"][l]) for l in range(L)], 1)
    o["w_router_t"] = a["moe_w_router"][0].reshape(KC, 128, NE).transpose(1, 0, 2)
    o["b_router_t"] = np.broadcast_to(a["moe_b_router"][0][None], (128, NE))
    o["pages"] = a["page_table"].reshape(1, -1)
    o["rel_rows"] = np.broadcast_to(a["rel_bias"][:, :, None], (32, NH, 128))
    row = np.arange(128)
    o["rel_tk"] = np.tile(a["rel_bias"][:, 4 * (row // 16 % 2) + row // 4 % 4], (4, 1))
    win, wv, glu, wo, ple, ssm = [], [], [], [], [], []
    qcols = np.concatenate([np.arange(64) + 64 * h for i in range(4) for h in (i, i + 4)])
    rows = np.concatenate([np.arange(512), 512 + qcols])
    for l in range(L):
        w = a["w_in"][l]
        cols = np.concatenate([np.arange(512), 512 + qcols, 1280 + np.arange(512), 1024 + np.arange(128),
                               1792 + np.arange(64), 1792 + np.arange(64)])
        win.append(_tiles(w[:, cols]))
        vc = np.concatenate([1152 + np.arange(128), 1856 + np.arange(8)])
        wv.append(w[:, vc].reshape(KC, 128, 136).transpose(1, 0, 2).reshape(128, KC * 136))
        gt = _tiles(a["ssm_w_glu"][l])
        glu.append(gt[[0, 4, 1, 5, 2, 6, 3, 7]])
        wo.append(_tiles(a["w_out"][l][rows]))
        ple.append(np.concatenate([_tiles(a["ple_w_gate"][l]), _tiles(a["ple_w_proj"][l])], 2))
        halves_ = []
        for hf in range(2):
            g = slice(HG * hf, HG * hf + HG)
            st = lambda v: v.reshape(HP, 2 * SN, -1).transpose(1, 2, 0)
            parts = [st(a["ssm_a_re"][l, g]), st(a["ssm_a_im"][l, g]),
                     st(np.broadcast_to(a["ssm_log_dt"][l, g][:, None], (HG, SN))),
                     st(a["ssm_b_re"][l, g]), st(a["ssm_b_im"][l, g]),
                     st(a["ssm_c_re"][l, g].transpose(0, 2, 1)), st(a["ssm_c_im"][l, g].transpose(0, 2, 1)),
                     st(a["state_ssm_re"][l][:, g].transpose(1, 2, 0)), st(a["state_ssm_im"][l][:, g].transpose(1, 2, 0))]
            halves_.append(np.concatenate(parts, 1).reshape(128, -1))
        ssm.append(np.stack(halves_))
    o["w_in_t"], o["w_v_t"], o["w_glu_t"], o["w_out_t"], o["w_ple_t"], o["ssm_t"] = map(np.stack, (win, wv, glu, wo, ple, ssm))
    gu, dn = [], []

    def block(g, u_, d):
        gu.append(np.stack([_tiles(g), _tiles(u_)], 1).reshape(2 * FT, 128, DM))
        dn.append(_tiles(d))

    for i in range(2):
        s = slice(FE * i, FE * i + FE)
        block(a["ffn_w_gate"][0][:, s], a["ffn_w_up"][0][:, s], a["ffn_w_down"][0][s])
    for e in range(NE):
        block(a["moe_w_gate"][0, e], a["moe_w_up"][0, e], a["moe_w_down"][0, e])
    o["w_gu_t"], o["w_dn_t"] = np.stack(gu), np.stack(dn)
    o["c_k"] = a["cache_k"].reshape(L, NPOOL, PAGE, 128).transpose(0, 1, 3, 2)
    o["c_v"] = a["cache_v"].reshape(L, NPOOL, PAGE, 128)
    o["c_i"] = a["cache_kidx"].transpose(0, 1, 3, 2)
    o["consts"] = _consts()
    return {k: np.ascontiguousarray(v) for k, v in o.items()}


def _split(t):
    return t[:, :SEQ].T, t[:, SEQ:].T.reshape(DT, NB, -1).transpose(1, 0, 2)


def kernel(**inputs):
    import numpy as np
    import concourse.bacc as bacc
    from concourse.bass_utils import run_bass_kernel_spmd

    arrays = _layout({k: np.asarray(v) for k, v in inputs.items()})
    nc = bacc.Bacc("TRN2", target_bir_lowering=False, num_devices=1)
    io = {k: nc.dram_tensor(k, v.shape, mybir.dt.from_np(v.dtype), kind="ExternalInput").ap() for k, v in arrays.items()}
    io.update({k: nc.dram_tensor(k, s, mybir.dt.float32, kind="ExternalOutput").ap() for k, s in _OUTS.items()})
    build(nc, io)
    res = run_bass_kernel_spmd(nc, [arrays], core_ids=[0]).results[0]
    y = np.asarray(res["o_y"]).transpose(1, 0, 2).reshape(DM, T)
    xp = y[:, :SEQ].reshape(DM, CH, NC).transpose(2, 1, 0).reshape(1, SEQ, DM)
    xs = y[:, SEQ:].T.reshape(DT, NB, DM).transpose(1, 0, 2)
    k = [_split(np.asarray(res["o_k"])[l]) for l in range(L)]
    ki = [_split(np.asarray(res["o_ki"])[l]) for l in range(L)]
    v = np.asarray(res["o_v"])
    vp = v[:, :, :NQT, :].transpose(0, 2, 1, 3).reshape(L, 1, SEQ, 2, HD)
    vs = v[:, :NS, NQT, :].reshape(L, DT, NB, 2, HD).transpose(0, 2, 1, 3, 4)
    h = np.asarray(res["o_h"]).reshape(L, 2, 2, SN, 2, HP, NB + 1)
    h = h.transpose(4, 0, 6, 1, 5, 2, 3).reshape(2, L, NB + 1, G, SN)
    c = np.ascontiguousarray
    return (c(xp), c(xs),
            np.stack([t[0] for t in k]).reshape(L, 1, SEQ, 2, HD), c(vp), np.stack([t[0] for t in ki])[:, None],
            c(h[0][:, :1]), c(h[1][:, :1]),
            np.stack([t[1] for t in k]).reshape(L, NB, DT, 2, HD), c(vs), np.stack([t[1] for t in ki]),
            c(h[0][:, 1:]), c(h[1][:, 1:]))
```

```python
import math

import concourse.bass as bass
from concourse import mybir
from contextlib import ExitStack

DM, SEQ, L, NB, DT, PAST, PAGE = 1024, 512, 2, 8, 4, 512, 128
NS = NB * DT
T = SEQ + NS
KC = DM // 128
CH = 8
NC = SEQ // CH
G, GC, SN = 32, 16, 64
HG = G // 2
HP = HG // 2
CW = NB + NC
NH, HD = 8, 64
NQT = SEQ // 128
TOPK_P = min(256, SEQ // 4)
TOPK_S = min(256, (PAST + DT) // 4)
NPG = PAST // PAGE
NPOOL = NB * NPG + (NB * NPG + 3) // 4
FE, NE = 1408, 8
FT = FE // 128
ALPHA = (2 * L) ** 0.25
LN_EPS = 1e-5
IDX_SCALE = (64 ** -0.5) * (8 ** -0.5)
NEG = -1e30
GONE = -3.0e38
RING = 6
SLOT = FT * 128
BLOCK_JOBS = 2 * FT + KC
WIN_T = 15
PAR_F = 3 + 4 * GC + 2 * NB
BW = SEQ + 128

C_ID, C_CM, C_MC, C_EX, C_MW, C_OH, C_MS, C_TK, C_MT, C_OF = 0, 128, 256, 384, 640, 704, 832, 864, 1408, 1536
C_TI = C_OF + BW
C_E1, C_EC = C_TI + 5, C_TI + 13
C_END = C_TI + 21
CAP = 176
ORD = 1024
TT = 5
XROWS = (NE + 1) * CAP


def build(nc, io):
    fp32, i32 = mybir.dt.float32, mybir.dt.int32
    ALU, ACT, AX = mybir.AluOpType, mybir.ActivationFunctionType, mybir.AxisListType
    ctx = ExitStack()
    with ctx:
        def sb(name, shape, dt=fp32):
            return ctx.enter_context(nc.sbuf_tensor(name, shape, dt))

        def sem(name):
            return ctx.enter_context(nc.semaphore(name))

        x = sb("x_res", [128, KC, T])
        acc = sb("acc", [128, KC, T])
        cat = sb("cat", [128, KC, T])
        ring = sb("ring", [128, RING, SLOT])
        rbias = sb("rbias", [128, NH, SEQ])
        cst = sb("cst", [128, C_END])
        bs = sb("bs", [128, PAST + NS])
        lnp = sb("lnp", [128, 2 + 4 * L, KC])
        dsk = sb("dsk", [128, L, 4])
        wrt = sb("wrt", [128, KC, NE])
        brt = sb("brt", [128, NE])
        ones = sb("ones", [128, 128])
        ptab = sb("ptab", [1, NB * NPG], i32)
        q = sb("q", [128, 4, T])
        kn = sb("kn", [128, T])
        kin = sb("kin", [128, T])
        vn = sb("vn", [128, T])
        wn = sb("wn", [NH, T])
        vtok = sb("vtok", [128, NQT + 1, 128])
        wtok = sb("wtok", [128, NQT, NH])
        sg = sb("sg", [128, 2, T])
        m8x = sb("mark", [128, 1])
        ph = sb("phase", [128, 18340])
        idx = sb("idx", [128, 4 * TT], i32)
        flag = sb("flag", [1, 1], i32)
        u = acc[:, 0:4, :]
        qi = acc[:, 4:8, :]
        ident = cst[:, C_ID:C_ID + 128]

        class Cut:
            def __init__(self, t, at=0):
                self.t, self.at = t, at

            def __call__(self, n, rows=128, lo=0):
                self.at += n
                return self.t[lo:lo + rows, self.at - n:self.at]

        cut = Cut(ph)
        U = cut(G * CW).rearrange("p (g c) -> p g c", g=G)
        U2 = cut(G * NB).rearrange("p (g b) -> p g b", g=G)
        par_at = cut.at
        par = cut(HP * PAR_F).rearrange("p (f e) -> p f e", e=HP)
        pB = par[:, 3:3 + 4 * GC, :].rearrange("p (k c) e -> p k e c", k=4)
        pH = par[:, 3 + 4 * GC:, :].rearrange("p (k b) e -> p k e b", k=2)
        toep = cut(HG * 128).rearrange("p (g n) -> p g n", g=HG)
        BT = cut(2 * HP * 128).rearrange("p (k e n) -> p k e n", k=2, e=HP)
        CP = [cut(HP * (CH + 1) * GC).rearrange("p (e m c) -> p e m c", e=HP, c=GC) for _ in range(2)]
        BP = [cut(HP * CH * GC).rearrange("p (e m c) -> p e m c", e=HP, c=GC) for _ in range(2)]
        Bb = [cut(HP * GC).rearrange("p (e c) -> p e c", e=HP) for _ in range(2)]
        E = [cut(HP * NC).rearrange("p (e c) -> p e c", e=HP) for _ in range(2)]
        GM = [cut(HP * NC).rearrange("p (e c) -> p e c", e=HP) for _ in range(2)]
        GS = [cut(HP * NC).rearrange("p (e c) -> p e c", e=HP) for _ in range(2)]
        HW_ = NB + NC + 1
        H = [cut(HP * HW_).rearrange("p (e c) -> p e c", e=HP) for _ in range(2)]
        R8 = cut(HP * NC).rearrange("p (e c) -> p e c", e=HP)
        Y = cut(HG * CW).rearrange("p (g c) -> p g c", g=HG)
        hout = cut(2 * HP * (NB + 1)).rearrange("p (k e b) -> p k e b", k=2, e=HP)
        P = [cut((CH + 1) * HP).rearrange("p (m e) -> p m e", e=HP) for _ in range(2)]
        sm = cut(24 * HP).rearrange("p (n e) -> p n e", e=HP)
        cf = cat[:, :, :].rearrange("p k t -> p (k t)")
        Kd = cf[0:GC, 0:HG * 128].rearrange("p (g n) -> p g n", g=HG)
        T1 = cf[:, 2048:2048 + 1152]
        T2 = cf[:, 3200:3200 + 1152]
        cut = Cut(ph)
        pgK = cut(16 * PAGE).rearrange("p (n c) -> p n c", n=16)
        pgV = cut(16 * PAGE).rearrange("p (n c) -> p n c", n=16)
        pgI = cut(16 * PAGE).rearrange("p (n c) -> p n c", n=16)
        shared = cut.at
        rl = cut(4 * SEQ).rearrange("p (n c) -> p n c", n=4)
        sc = cut(SEQ)
        wk = cut(SEQ)
        nosel = cut(SEQ)
        Lg = cut(NH * SEQ).rearrange("p (h c) -> p h c", h=NH)
        PT = cut(2 * NQT * 512).rearrange("p (g k c) -> p g k c", g=2, k=NQT)
        m8 = cut(8)
        nmx = cut(NH)
        sums = cut(NH)
        rs = cut(NH)
        negid = cut(128)
        pgs = {0: (pgK, pgV, pgI)}
        two = PT.rearrange("p g k c -> p (g k c)").rearrange("p (z n c) -> p z n c", z=2, n=16)
        pgs[1] = (two[:, 0], two[:, 1], cf[:, 0:16 * PAGE].rearrange("p (n c) -> p n c", n=16))
        cut = Cut(ph, shared)
        Qzi = cut(256).rearrange("p (b a i t) -> p b a i t", b=NB, a=2, i=4)
        Qz = cut(256).rearrange("p (b a i t) -> p b a i t", b=NB, a=2, i=4)
        SK = PAST + NS
        rls = cut(SK)
        wr = cut(2 * NS).rearrange("p (r y) -> p r y", r=2)
        scs = cut(SK)
        wks = cut(SK + 7)
        nss = cut(SK)
        Ls = cut(SK)
        PTs = cut(5 * 128).rearrange("p (k c) -> p k c", k=5)
        m8s = cut(8)
        nms = cut(4)
        cut = Cut(ph)
        hid = cut(FT * T).rearrange("p (f t) -> p f t", f=FT)
        gb = cut(NE * T).rearrange("p (e t) -> p e t", e=NE)
        pt = cut(2 * T).rearrange("p (k t) -> p k t", k=2)
        rlog = cut(5 * NE).rearrange("p (n e) -> p n e", n=5)
        rtop = cut(5 * NE).rearrange("p (n e) -> p n e", n=5)
        rtwo = cut(5 * NE).rearrange("p (n e) -> p n e", n=5)
        rwk = cut(5 * 14).rearrange("p (n e) -> p n e", n=5)
        gts = cut(5 * NE).rearrange("p (n e) -> p n e", n=5)
        rsm = cut(5 * 4).rearrange("p (n e) -> p n e", n=5)
        rst = cut(T)
        ygt = cut(2 * DM).rearrange("p (c d) -> p c d", c=2)
        xgt = cut(2 * DM).rearrange("p (c d) -> p c d", c=2)
        zt = ygt[:, 0, :]
        one = cut(128)
        small = lambda n: cut(TT * n).rearrange("p (t n) -> p t n", t=TT)
        sel, rank, order, tmp8 = small(NE), small(NE), small(NE), small(NE)
        over = small(NE)
        v01, r01, b01, g01, ok01, ix01 = (small(2) for _ in range(6))
        ovs = cut(1)
        cut = Cut(ph)
        xtok = cut(TT * DM).rearrange("p (t d) -> p t d", t=TT)
        gt1_at = cut.at
        xg = cut(KC * CAP).rearrange("p (k c) -> p k c", k=KC)
        hidg = cut(FT * CAP).rearrange("p (f c) -> p f c", f=FT)
        yT = cut(KC * CAP).rearrange("p (k c) -> p k c", k=KC)
        gt = [xtok, ph[:, gt1_at:gt1_at + TT * DM].rearrange("p (t d) -> p t d", t=TT)]
        cut = Cut(ph)
        relb = cut(NH * 128).rearrange("p (h n) -> p h n", h=NH)
        reltk = cut(128)
        frow = cut(NH * BW).rearrange("p (h n) -> p h n", h=NH)
        NXZ = (XROWS + 127) // 128

        pair = [ctx.enter_context(nc.psum_tensor(f"pair{i}", [128, 1024], fp32)) for i in range(4)]

        def bank(i):
            return pair[i // 2][:, 512 * (i % 2):512 * (i % 2) + 512]

        def even(i):
            return pair[i][:, :].rearrange("p (h c) -> p h c", h=2)[:, :, 0:T // 2]

        udram = nc.dram_tensor("u_scratch", (4 * 128, T), fp32, kind="Internal")
        ydram = nc.dram_tensor("y_scratch", (4 * 128, T), fp32, kind="Internal")
        fdram = nc.dram_tensor("f_scratch", (NH, 128, BW), fp32, kind="Internal")

        xs = nc.dram_tensor("gathered_x", (XROWS + 2 * TT * 128, DM), fp32, kind="Internal")
        ys = nc.dram_tensor("gathered_y", (NE * CAP, DM), fp32, kind="Internal")

        w_loaded = [sem(f"w_loaded{i}") for i in range(RING)]
        jobs_begun = sem("jobs_begun")
        filled = [sem(f"filled{i}") for i in range(4)]
        emptied = [sem(f"emptied{i}") for i in range(4)]
        dve_step, act_step, pool_step = sem("dve_step"), sem("act_step"), sem("pool_step")
        consts_in, rel_in, x_in = sem("consts_in"), sem("rel_in"), sem("x_in")
        ones_set = sem("ones_set")
        f_mm, f_ready, f_out, rbias_in = sem("f_mm"), sem("f_ready"), sem("f_out"), sem("rbias_in")
        tk_ready, bs_mm, bs_ready = sem("tk_ready"), sem("bs_mm"), sem("bs_ready")
        acc_ready, squares, rstd, x_ready = sem("acc_ready"), sem("squares"), sem("var_inv"), sem("x_ready")
        rst_ready = sem("rstd_ready")
        u_out, u_zero, u_in = sem("u_out"), sem("u_zero"), sem("u_in")
        par_in, ldt, expd, theta, sincos = sem("par_in"), sem("dt_exp"), sem("radii"), sem("theta"), sem("sincos")
        bp_ready, cp_ready, bt_mm, bt_ready = sem("bp_ready"), sem("cp_ready"), sem("bt_mm"), sem("bt_ready")
        toep_zero, kd_mm, kd_ready, toep_in = sem("toep_zero"), sem("kd_mm"), sem("kd_ready"), sem("toep_in")
        g_mm, h_ready, y_mm, y_ready = sem("g_mm"), sem("h_ready"), sem("y_mm"), sem("y_ready")
        y_out, y_in, yd_ready, gelu_ready = sem("y_out"), sem("y_in"), sem("yd_ready"), sem("gelu_ready")
        tok_mm, tok_ready = sem("tok_mm"), sem("tok_ready")
        idx_mm, relu_ready, relu_used = sem("idx_mm"), sem("relu_ready"), sem("relu_used")
        lg_mm, lg_used, nmx_ready, exp_ready = sem("lg_mm"), sem("lg_used"), sem("nmx_ready"), sem("exp_ready")
        rs_ready, prob_ready = sem("rs_ready"), sem("prob_ready")
        pt_mm, pt_ready, pv_mm, pv_ready = sem("pt_mm"), sem("pt_ready"), sem("pv_mm"), sem("pv_ready")
        pages_kv = [sem("pages_kv0"), sem("pages_kv1")]
        pages_in = [sem("index_pages0"), sem("index_pages1")]
        hide_ready = sem("hide_ready")
        qz_ready, wr_mm, wr_ready = sem("qz_ready"), sem("wr_mm"), sem("wr_ready")
        si_mm, srelu, sc_mm, nosel_ready = sem("si_mm"), sem("srelu"), sem("sc_mm"), sem("nosel_ready")
        sl_mm, snmx, sexp, sprob = sem("sl_mm"), sem("snmx"), sem("sexp"), sem("sprob")
        spt_mm, spt_ready, spv_mm, spv_ready = sem("spt_mm"), sem("spt_ready"), sem("spv_mm"), sem("spv_ready")
        pt_in, r_mm, gts_ready, gb_mm, gb_ready = sem("p_in"), sem("r_mm"), sem("gts_ready"), sem("gb_mm"), sem("gb_ready")
        ple_used = sem("ple_used")
        gdiff, gexp = sem("gate_diff"), sem("gate_exp")
        hid_ready = sem("hid_ready")
        zero_set, xs_zero = sem("zero_set"), sem("xs_zero")
        xt_mm, xt_ready, sel_ready, rank_mm = sem("xt_mm"), sem("xt_ready"), sem("sel_ready"), sem("rank_mm")
        one_set, idx_ready, scattered, ov_ready = sem("one_set"), sem("idx_ready"), sem("scattered"), sem("ov_ready")
        flag_mm, flag_ready = sem("flag_mm"), sem("flag_ready")
        xg_in, silu_ready, y_free, ys_out = sem("xg_in"), sem("silu_ready"), sem("y_free"), sem("ys_out")
        gt_in, comb_ready = sem("gt_in"), sem("comb_ready")
        last_filled = [sem("last_filled0"), sem("last_filled1")]
        last_emptied = [sem("last_emptied0"), sem("last_emptied1")]
        stored = sem("stored")

        class Count:
            def __init__(self):
                self.n = [0] * 4

            def take(self, s):
                self.n[s] += 1
                return self.n[s]

        def experts(l):
            return 2 if l == 0 else NE

        def first_block(l):
            return 0 if l == 0 else 2

        LAYER_JOBS = WIN_T + 8 + 8 + 8
        JOBS = [0, LAYER_JOBS + BLOCK_JOBS * experts(0)]
        FFN_USES = [8, 8, 7, 7]

        def ffn_plan():
            seen = [0] * 4
            steps = [("up", f, (0, 1) if f % 2 == 0 else (2, 3)) for f in range(FT)]
            steps += [("down", m, ((2 + m) % 4,)) for m in range(KC)]
            for kind, i, ps in steps:
                yield kind, i, [(s, seen[s]) for s in ps]
                for s in ps:
                    seen[s] += 1

        def moe_plan():
            seen = [0] * 4
            steps = [("up", f, f % 4) for f in range(FT)] + [("down", i, (3, 0, 1, 2)[i]) for i in range(4)]
            steps += [("xg", 0, 3), ("xg", 1, 0), ("yg", 0, 1), ("yg", 1, 2)]
            for kind, i, s in steps:
                yield kind, i, s, seen[s]
                seen[s] += 1

        MOE_USES = [5, 5, 5, 4]
        C_ROWS = (128, CAP - 128)

        def banks(s, n):
            return pair[s][:, :].rearrange("p (h c) -> p h c", h=2)[:, :, 0:n]

        def uses_before(l, s):
            n = int(s < 2)
            for k in range(l):
                n += 12 + 2 * int(s < 2) + FFN_USES[s] * experts(k)
            return n

        def halves(t):
            return t.rearrange("p (h c) -> p h c", h=2)

        def bc(t, axis, n):
            t = t.unsqueeze(axis)
            shape = list(t.shape)
            shape[axis] = n
            return t.to_broadcast(shape)

        block = ctx.enter_context(nc.Block())

        @block.sync
        def _(sp):
            sp.dma_start(x[:, :, :], io["x_t"]).then_inc(x_in, 16)
            sp.dma_start(lnp[:, :, :], io["ln_p"]).then_inc(x_in, 16)

            def load(n, cols, src):
                if n >= RING:
                    sp.wait_ge(jobs_begun, n - RING + 2)
                sp.dma_start(ring[:, n % RING, 0:cols], src).then_inc(w_loaded[n % RING], 16)

            for l in range(L):
                n = JOBS[l]
                for m in range(WIN_T - 1):
                    load(n + m, 1024, io["w_in_t"][l, m])
                load(n + WIN_T - 1, KC * 136, io["w_v_t"][l])
                n += WIN_T
                for m in range(8):
                    load(n + m, 512, io["w_glu_t"][l, m])
                for m in range(8):
                    load(n + 8 + m, 1024, io["w_out_t"][l, m])
                for m in range(8):
                    load(n + 16 + m, 1280, io["w_ple_t"][l, m])
                n += 24
                def blocks(n, first, count):
                    with sp.Fori(0, count) as e:
                        blk = e + first
                        for k in range(BLOCK_JOBS):
                            sp.wait_ge(jobs_begun, e * BLOCK_JOBS + (n + k - RING + 2))
                            if k < 2 * FT:
                                src, cols = io["w_gu_t"][bass.ds(blk, 1), k, :, :], 1024
                            else:
                                src, cols = io["w_dn_t"][bass.ds(blk, 1), k - 2 * FT, :, :], SLOT
                            sp.dma_start(ring[:, (n + k) % RING, 0:cols],
                                         src.rearrange("o p c -> p (o c)")).then_inc(w_loaded[(n + k) % RING], 16)

                blocks(n, first_block(l), experts(l))
                if l == 1:
                    sp.wait_ge(flag_ready, 1)
                    left = sp.value_load(flag[0:1, 0:1], min_val=0, max_val=2 * T)
                    with sp.If(left > 0):
                        blocks(n + BLOCK_JOBS * NE, first_block(l), NE)

        @block.gpsimd
        def _(pool):
            pool.dma_start(cst[:, :], io["consts"]).then_inc(consts_in, 16)
            pool.dma_start(dsk[:, :, :], io["d_t"]).then_inc(consts_in, 16)
            pool.dma_start(wrt[:, :, :], io["w_router_t"]).then_inc(consts_in, 16)
            pool.dma_start(brt[:, :], io["b_router_t"]).then_inc(consts_in, 16)
            pool.dma_start(ptab[:, :], io["pages"]).then_inc(consts_in, 16)
            pool.dma_start(relb[0:32, :, :], io["rel_rows"]).then_inc(rel_in, 16)
            pool.dma_start(reltk, io["rel_tk"]).then_inc(rel_in, 16)
            nc.gpsimd.memset(ones[:, :], 1.0 / DM).then_inc(ones_set, 1)
            pool.wait_ge(f_ready, NH)
            pool.dma_start(fdram.ap().rearrange("h p n -> p h n"), frow[:, :, :]).then_inc(f_out, 16)
            pool.wait_ge(f_out, 16)
            pool.dma_start(rbias[:, :, :], bass.AP(fdram, 127, [[BW - 1, 128], [128 * BW, NH], [1, SEQ]])).then_inc(rbias_in, 16)
            pool.wait_ge(consts_in, 16 * 5)
            for l in range(L):
                pool.wait_ge(x_ready, 1 + 2 * l)
                if l:
                    pool.wait_ge(xs_zero, 16 * NXZ)
                pool.dma_start(ph[:, par_at:par_at + HP * PAR_F], io["ssm_t"][l, 0]).then_inc(par_in, 16)
                for s in range(4):
                    pool.wait_ge(emptied[s], uses_before(l, s) + 1)
                pool.dma_start(udram.ap().rearrange("(k p) c -> p k c", p=128), u).then_inc(u_out, 16)
                nc.gpsimd.memset(U[0:64, :, 0:NB], 0.0).then_inc(u_zero, 1)
                pool.wait_ge(u_out, 16 * (l + 1))
                uv = udram.ap().rearrange("(g h) c -> h g c", h=GC)
                for r in range(CH):
                    j = CH - 1 - r
                    rows = slice(GC * r, GC * r + GC)
                    pool.dma_start(U[rows, :, NB:CW], uv[:, :, NC * j:NC * j + NC]).then_inc(u_in, 16)
                    if j < DT:
                        pool.dma_start(U[rows, :, 0:NB], uv[:, :, SEQ + NB * j:SEQ + NB * j + NB]).then_inc(u_in, 16)
                    else:
                        jj = j - DT
                        pool.dma_start(U2[rows, :, :], uv[:, :, SEQ + NB * jj:SEQ + NB * jj + NB]).then_inc(u_in, 16)
                nc.gpsimd.memset(toep[:, :, :], 0.0).then_inc(toep_zero, 1)
                for hf in range(2):
                    v = 2 * l + hf
                    pool.wait_ge(kd_ready, v + 1)
                    pool.wait_ge(toep_zero, v + 1)
                    for s in range(CH):
                        r = CH - 1 - s
                        pool.dma_start(toep[GC * r:GC * r + GC, :, GC * s:128],
                                       Kd[:, :, 0:128 - GC * s]).then_inc(toep_in, 16)
                    pool.wait_ge(h_ready, v + 1)
                    if hf == 0:
                        pool.dma_start(ph[:, par_at:par_at + HP * PAR_F], io["ssm_t"][l, 1]).then_inc(par_in, 16)
                    pool.dma_start(io["o_h"][l, hf], hout[:, :, :, :].rearrange("p k e b -> p (k e b)")).then_inc(stored, 16)
                    pool.wait_ge(y_ready, v + 1)
                    if hf == 0:
                        nc.gpsimd.memset(toep[:, :, :], 0.0).then_inc(toep_zero, 1)
                    yv = ydram.ap().rearrange("(g h) c -> h g c", h=GC)[:, HG * hf:HG * hf + HG, :]
                    for t in range(CH):
                        rows = slice(GC * t, GC * t + GC)
                        pool.dma_start(yv[:, :, NC * t:NC * t + NC], Y[rows, :, NB:CW]).then_inc(y_out, 16)
                        if t < DT:
                            pool.dma_start(yv[:, :, SEQ + NB * t:SEQ + NB * t + NB], Y[rows, :, 0:NB]).then_inc(y_out, 16)
                pool.wait_ge(y_out, 16 * 12 * 2 * (l + 1))
                pool.dma_start(cat[:, 0:4, :], ydram.ap().rearrange("(k p) c -> p k c", p=128)).then_inc(y_in, 16)
                def load_pages(r, kinds, done):
                    with pool.Fori(0, 16) as i:
                        pg = pool.value_load(ptab[0:1, bass.ds(i + 16 * r, 1)], min_val=0, max_val=NPOOL - 1)
                        for dst, src in kinds:
                            pool.dma_start(dst[:, bass.ds(i, 1), :],
                                           src[l, bass.ds(pg, 1), :, :].rearrange("o p c -> p o c")).then_inc(done, 16)

                load_pages(0, ((pgs[0][2], io["c_i"]),), pages_in[0])
                load_pages(0, ((pgs[0][0], io["c_k"]), (pgs[0][1], io["c_v"])), pages_kv[0])
                pool.wait_ge(yd_ready, l + 1)
                load_pages(1, ((pgs[1][2], io["c_i"]),), pages_in[1])
                pool.wait_ge(tok_ready, 2 * l + 2)
                pool.dma_start(io["o_k"][l], kn[:, :]).then_inc(stored, 16)
                pool.dma_start(io["o_v"][l, :, 0:NQT, :], vtok[:, 0:NQT, :]).then_inc(stored, 16)
                pool.dma_start(io["o_v"][l, 0:NS, NQT, :], vtok[0:NS, NQT, :]).then_inc(stored, 16)
                pool.dma_start(io["o_ki"][l], kin[0:64, :]).then_inc(stored, 16)
                pool.wait_ge(pv_ready, NQT * (l + 1))
                load_pages(1, ((pgs[1][0], io["c_k"]), (pgs[1][1], io["c_v"])), pages_kv[1])
                pool.wait_ge(spv_ready, 2 * l + 2)
                pool.dma_start(pt[:, :, :], io["p_t"][l]).then_inc(pt_in, 16)
                if l == 0:
                    nc.gpsimd.memset(zt, 0.0).then_inc(zero_set, 1)
                    pool.wait_ge(zero_set, 1)
                    for i in range(NXZ):
                        rows = min(128, XROWS - 128 * i)
                        pool.dma_start(xs.ap()[128 * i:128 * i + rows, :], zt[0:rows, :]).then_inc(xs_zero, 16)
            nc.gpsimd.memset(one[:, :], 1.0).then_inc(one_set, 1)
            pool.wait_ge(xt_ready, TT)
            pool.wait_ge(idx_ready, 1)
            for tt in range(TT):
                rows = 128 if tt < 4 else NS
                for k in range(2):
                    pool.indirect_dma_start(xs.ap(), bass.IndirectOffsetOnAxis(ap=idx[0:rows, 2 * tt + k:2 * tt + k + 1].bitcast(mybir.dt.uint32), axis=0),
                                            xtok[0:rows, tt, :], None).then_inc(scattered, 16)
            pool.wait_ge(scattered, 16 * 2 * TT)

            def load_rows(e):
                src = xs.ap()[0:XROWS, :].rearrange("(e c) d -> e c d", c=CAP)[bass.ds(e, 1), :, :]
                pool.dma_start(xgt[:, 0, :], src[:, 0:128, :].rearrange("o c d -> c (o d)")).then_inc(xg_in, 16)
                pool.dma_start(xgt[0:C_ROWS[1], 1, :], src[:, 128:CAP, :].rearrange("o c d -> c (o d)")).then_inc(xg_in, 16)

            load_rows(0)
            pool.sem_inc(y_free, 1)
            base = [uses_before(1, s) + 12 + int(s < 2) + int(s in (0, 3)) for s in range(4)]
            with pool.Fori(0, NE) as e:
                pool.wait_ge(filled[0], e * MOE_USES[0] + base[0])
                load_rows(e + 1)
                for s in (1, 2):
                    pool.wait_ge(emptied[s], e * MOE_USES[s] + (base[s] + MOE_USES[s]))
                dst = ys.ap().rearrange("(e c) d -> e c d", c=CAP)[bass.ds(e, 1), :, :]
                pool.dma_start(dst[:, 0:128, :].rearrange("o c d -> c (o d)"), ygt[:, 0, :]).then_inc(ys_out, 16)
                pool.dma_start(dst[:, 128:CAP, :].rearrange("o c d -> c (o d)"), ygt[0:C_ROWS[1], 1, :]).then_inc(ys_out, 16)
                pool.wait_ge(ys_out, e * 32 + 32)
                pool.sem_inc(y_free, 1)
            for tt in range(TT):
                rows = 128 if tt < 4 else NS
                for k in range(2):
                    col = 2 * TT + 2 * tt + k
                    pool.indirect_dma_start(gt[k][0:rows, tt, :], None, ys.ap(),
                                            bass.IndirectOffsetOnAxis(ap=idx[0:rows, col:col + 1].bitcast(mybir.dt.uint32), axis=0)).then_inc(gt_in, 16)
            pool.wait_ge(x_ready, 1 + 2 * L)
            pool.dma_start(io["o_y"], x[:, :, :]).then_inc(stored, 16)
            pool.wait_ge(stored, 16 * (6 * L + 1))

        @block.tensor
        def _(pe):
            mm = nc.tensor.matmul
            c = Count()

            def begin(s):
                n = c.take(s)
                if n > 1:
                    pe.wait_ge(emptied[s], n - 1)
                return n

            def all_empty():
                for s in range(4):
                    if c.n[s]:
                        pe.wait_ge(emptied[s], c.n[s])

            def product(s, w, kcs, rhs, split, rows=128, note=None, done=None):
                for half, (a, b) in enumerate(((0, split), (split, T))):
                    for i, kc in enumerate(kcs):
                        last = mm(pair[s][0:rows, 512 * half:512 * half + b - a], w(kc), rhs(kc)[:, a:b],
                                  start=(i == 0), stop=(i == len(kcs) - 1))
                        if note is not None and half == 0 and i == 0:
                            last.then_inc(note, 1)
                last.then_inc(filled[s] if done is None else done, 1)

            def job(n, s, cols, kcs, rhs, split=T // 2):
                begin(s)
                pe.wait_ge(w_loaded[n % RING], 16 * (n // RING + 1))
                product(s, lambda kc: ring[:, n % RING, cols * kc:cols * kc + 128], kcs, rhs, split, note=jobs_begun)

            def layer_norm(k):
                if k == 0:
                    pe.wait_ge(x_in, 32)
                    pe.wait_ge(ones_set, 1)
                src = x if k == 0 else acc
                end = k == 2 * L
                if not end:
                    begin(0)
                if k:
                    pe.wait_ge(acc_ready, k)
                product(0, lambda kc: ones[:, :], range(KC), lambda kc: src[:, kc, :], T // 2, done=last_filled[0] if end else None)
                if not end:
                    begin(1)
                pe.wait_ge(squares, k + 1)
                product(1, lambda kc: ones[:, :], range(KC), lambda kc: cat[:, kc, :], T // 2, done=last_filled[1] if end else None)

            layer_norm(0)
            pe.wait_ge(rel_in, 32)
            pe.wait_ge(consts_in, 80)
            for h in range(NH):
                p = pair[2 + h % 2]
                if h >= 2:
                    pe.wait_ge(f_ready, h - 1)
                mm(p[:, 0:512], relb[0:32, h, :], cst[0:32, C_OF:C_OF + 512], start=True, stop=True)
                mm(p[:, 512:512 + 128], relb[0:32, h, :], cst[0:32, C_OF + 512:C_OF + BW], start=True, stop=True).then_inc(f_mm, 1)
            pe.wait_ge(tk_ready, 1)
            pe.wait_ge(f_ready, NH)
            mm(pair[2][:, 0:512], reltk, cst[:, C_TK:C_TK + 512], start=True, stop=True)
            mm(pair[2][:, 512:512 + NS], reltk, cst[:, C_TK + 512:C_TK + SK], start=True, stop=True).then_inc(bs_mm, 1)

            for l in range(L):
                n = JOBS[l]
                xr = lambda kc: x[:, kc, :]
                pe.wait_ge(x_ready, 1 + 2 * l)
                for m in range(WIN_T - 1):
                    if l == 0 and m == 2:
                        pe.wait_ge(bs_ready, 1)
                    job(n + m, m % 4, 128, range(KC), xr, split=256)
                nv = n + WIN_T - 1
                job(nv, 2, 136, range(KC), xr, split=256)
                begin(3)
                product(3, lambda kc: ring[:, nv % RING, 136 * kc + 128:136 * kc + 136], range(KC), xr, 256, rows=NH)
                n += WIN_T
                all_empty()
                if l == 0:
                    pe.wait_ge(consts_in, 80)
                for b in range(NQT):
                    nc.tensor.transpose(bank(0)[:, 128 * b:128 * b + 128], vn[:, 128 * b:128 * b + 128], ident)
                    nc.tensor.transpose(bank(2)[:, NH * b:NH * b + NH], wn[:, 128 * b:128 * b + 128], cst[0:NH, C_ID:C_ID + NH])
                nc.tensor.transpose(bank(1)[0:NS, 0:128], vn[:, SEQ:T], ident).then_inc(tok_mm, 1)

                for hf in range(2):
                    v = 2 * l + hf + 1
                    if hf == 0:
                        pe.wait_ge(tok_ready, 2 * l + 2)
                    pe.wait_ge(bp_ready, v)
                    if hf:
                        pe.wait_ge(h_ready, v - 1)
                    for k in range(2):
                        for e in range(HP):
                            last = nc.tensor.transpose(pair[k][:, 128 * e:128 * e + 128],
                                                       BP[k][:, e].rearrange("p m c -> p (m c)"), ident)
                    last.then_inc(bt_mm, 1)
                    pe.wait_ge(cp_ready, v)
                    if hf:
                        pe.wait_ge(y_ready, v - 1)
                    for g in range(HG):
                        e, lo = g // 2, 64 * (g % 2)
                        o = pair[2 + g % 2][0:GC, 128 * e:128 * e + 128]
                        for k in range(2):
                            last = mm(o, Bb[k][lo:lo + 64, e], CP[k][lo:lo + 64, e, 0:CH].rearrange("p m c -> p (m c)"),
                                      start=(k == 0), stop=(k == 1))
                    last.then_inc(kd_mm, 1)
                    pe.wait_ge(bt_ready, v)
                    pe.wait_ge(u_in, 256 * (l + 1))
                    pe.wait_ge(u_zero, l + 1)
                    for k in range(2):
                        for gl in range(HG):
                            e, lo, g = gl // 2, 64 * (gl % 2), HG * hf + gl
                            mm(bank(k)[lo:lo + 64, NC * e:NC * e + NC], BT[:, k, e, lo:lo + 64], U[:, g, NB:CW],
                               start=True, stop=True)
                            last = mm(bank(2)[lo:lo + 64, 64 * k + NB * e:64 * k + NB * e + NB], BT[0:64, k, e, lo:lo + 64],
                                      U2[0:64, g, :], start=True, stop=True)
                    last.then_inc(g_mm, 1)
                    pe.wait_ge(h_ready, v)
                    pe.wait_ge(toep_in, 128 * v)
                    for gl in range(HG):
                        e, lo, g = gl // 2, 64 * (gl % 2), HG * hf + gl
                        o = bank(4 + 2 * (gl % 2) + e // 6)[:, CW * (e % 6):CW * (e % 6) + CW]
                        mm(o, toep[:, HP * (gl % 2) + e, :], U[:, g, :], start=True, stop=False)
                        for k in range(2):
                            last = mm(o, CP[k][lo:lo + 64, e, 1:CH + 1].rearrange("p m c -> p (m c)"),
                                      H[k][lo:lo + 64, e, 0:CW], start=False, stop=(k == 1))
                    last.then_inc(y_mm, 1)

                pe.wait_ge(y_ready, 2 * l + 2)
                ni, nl, npt = 8 * 3 * l, 8 * NQT * l, 20 * l
                for b in range(NQT):
                    w = 128 * (b + 1)
                    qs = slice(128 * b, 128 * b + 128)
                    for h in range(NH):
                        lo = 64 * (h // 4)
                        if nl >= 3:
                            pe.wait_ge(lg_used, nl - 2)
                        o = bank(2 + nl % 3)[:, 0:w]
                        mm(o, q[lo:lo + 64, h % 4, qs], kn[lo:lo + 64, 0:w], start=True, stop=False)
                        if h == 0:
                            pe.wait_ge(hide_ready, NQT * l + b + 1)
                        hide = nosel[:, 0:w] if b else cst[:, C_CM:C_CM + 128]
                        mm(o, negid, hide, start=False, stop=True).then_inc(lg_mm, 1)
                        nl += 1
                    if b + 1 < NQT:
                        for h in range(NH):
                            lo = 64 * (h % 2)
                            if ni >= 2:
                                pe.wait_ge(relu_ready, ni - 1)
                            mm(bank(ni % 2)[:, 0:w + 128], qi[lo:lo + 64, h // 2, 128 * b + 128:128 * b + 256], kin[lo:lo + 64, 0:w + 128],
                               start=True, stop=True).then_inc(idx_mm, 1)
                            ni += 1
                    pe.wait_ge(prob_ready, NQT * l + b + 1)
                    for g in range(2):
                        for kt in range(b + 1):
                            if npt >= 2:
                                pe.wait_ge(pt_ready, npt - 1)
                            for i in range(4):
                                last = nc.tensor.transpose(bank(5 + npt % 2)[:, 128 * i:128 * i + 128],
                                                           Lg[:, 4 * g + i, 128 * kt:128 * kt + 128], ident)
                            last.then_inc(pt_mm, 1)
                            npt += 1
                    pe.wait_ge(pt_ready, npt)
                    nb = NQT * l + b
                    if nb:
                        pe.wait_ge(pv_ready, nb)
                    for g in range(2):
                        for kt in range(b + 1):
                            last = mm(bank(7)[64 * g:64 * g + 64, :], vtok[:, kt, 64 * g:64 * g + 64], PT[:, g, kt, :],
                                      start=(kt == 0), stop=(kt == b))
                    last.then_inc(pv_mm, 1)

                pe.wait_ge(pv_ready, NQT * (l + 1))
                mm(bank(4)[:, 0:NS], cst[0:NH, C_OH:C_OH + 128], wn[0:NH, SEQ:T], start=True, stop=True).then_inc(wr_mm, 1)
                pe.wait_ge(wr_ready, l + 1)
                pe.wait_ge(qz_ready, l + 1)
                for r in range(2):
                    v = 2 * l + r + 1
                    pgK, pgV, pgI = pgs[r]
                    pe.wait_ge(pages_in[r], 256 * (l + 1))
                    if r:
                        pe.wait_ge(srelu, v - 1)
                    lz = Qzi[:, 4 * r:4 * r + 4].rearrange("p b a i t -> p (b a i t)")
                    for bi in range(4):
                        mm(bank(0)[32 * bi:32 * bi + 32, :], lz[:, 32 * bi:32 * bi + 32],
                           pgI[:, 4 * bi:4 * bi + 4, :], start=True, stop=True)
                    mm(bank(1)[:, 0:NS], lz, kin[:, SEQ:T], start=True, stop=True).then_inc(si_mm, 1)
                    pe.wait_ge(srelu, v)
                    mm(bank(2)[0:NS, :], wr[:, r, :], rls[:, 0:PAST], start=(r == 0), stop=(r == 1))
                    mm(bank(3)[0:NS, 0:NS], wr[:, r, :], rls[:, PAST:SK], start=(r == 0), stop=(r == 1)).then_inc(sc_mm, 1)
                pe.wait_ge(nosel_ready, l + 1)
                for r in range(2):
                    v = 2 * l + r + 1
                    lz = Qz[:, 4 * r:4 * r + 4].rearrange("p b a i t -> p (b a i t)")
                    ex = cst[0:NS, C_EX + 128 * r:C_EX + 128 * r + 128]
                    pgK, pgV, pgI = pgs[r]
                    pe.wait_ge(pages_kv[r], 512 * (l + 1))
                    if r:
                        pe.wait_ge(spv_ready, v - 1)
                    mm(bank(0), ex, nss[0:NS, 0:PAST], start=True, stop=False)
                    for bi in range(4):
                        mm(bank(0)[32 * bi:32 * bi + 32, :], lz[:, 32 * bi:32 * bi + 32],
                           pgK[:, 4 * bi:4 * bi + 4, :], start=False, stop=True)
                    mm(bank(1)[:, 0:NS], ex, nss[0:NS, PAST:SK], start=True, stop=False)
                    mm(bank(1)[:, 0:NS], lz, kn[:, SEQ:T], start=False, stop=True).then_inc(sl_mm, 1)
                    pe.wait_ge(sprob, v)
                    for k in range(NPG):
                        nc.tensor.transpose(bank(4)[:, 128 * k:128 * k + 128], Ls[:, 128 * k:128 * k + 128], ident)
                    nc.tensor.transpose(bank(5)[0:NS, 0:128], Ls[:, PAST:SK], ident).then_inc(spt_mm, 1)
                    pe.wait_ge(spt_ready, v)
                    for bi in range(4):
                        o = bank(6)[:, 32 * bi:32 * bi + 32]
                        for k in range(NPG):
                            mm(o, pgV[:, NPG * bi + k, :], PTs[:, k, 32 * bi:32 * bi + 32], start=(k == 0), stop=False)
                        last = mm(o, vtok[0:NS, NQT, :], PTs[0:NS, NPG, 32 * bi:32 * bi + 32], start=False, stop=True)
                    last.then_inc(spv_mm, 1)

                pe.wait_ge(spv_ready, 2 * l + 2)
                pe.wait_ge(gelu_ready, l + 1)
                for m in range(8):
                    job(n + m, m % 4, 128, range(4), lambda kc: u[:, kc, :])
                n += 8
                for m in range(8):
                    if m == 0:
                        pe.wait_ge(emptied[2], c.n[2])
                        pe.wait_ge(emptied[0], c.n[0])
                    job(n + m, m % 4, 128, range(KC), lambda kc: cat[:, kc, :])
                n += 8
                layer_norm(1 + 2 * l)
                pe.wait_ge(x_ready, 2 + 2 * l)
                if l == 1:
                    all_empty()
                    for tt in range(TT):
                        rows = 128 if tt < 4 else NS
                        for kc in range(KC):
                            last = mm(bank(0)[0:rows, NE * tt:NE * tt + NE], x[:, kc, 128 * tt:128 * tt + rows], wrt[:, kc, :],
                                      start=(kc == 0), stop=(kc == KC - 1))
                    last.then_inc(r_mm, 1)
                    for tt in range(TT):
                        rows = 128 if tt < 4 else NS
                        if tt >= 3:
                            pe.wait_ge(xt_ready, tt - 2)
                        for kc in range(KC):
                            last = nc.tensor.transpose(pair[1 + tt % 3][0:rows, 128 * kc:128 * kc + 128],
                                                       x[:, kc, 128 * tt:128 * tt + rows], ident)
                        last.then_inc(xt_mm, 1)
                    pe.wait_ge(sel_ready, 1)
                    pe.wait_ge(one_set, 1)
                    for tt in range(TT):
                        rows = 128 if tt < 4 else NS
                        o = bank(0)[0:rows, 64 + NE * tt:64 + NE * tt + NE]
                        for t0 in range(tt):
                            mm(o, one[:, 0:rows], sel[:, t0, :], start=(t0 == 0), stop=False)
                        last = mm(o, cst[0:rows, C_CM:C_CM + rows], sel[0:rows, tt, :], start=(tt == 0), stop=True)
                    last.then_inc(rank_mm, 1)
                    pe.wait_ge(ov_ready, 1)
                    mm(bank(0)[0:1, 0:1], ovs, one[:, 0:1], start=True, stop=True).then_inc(flag_mm, 1)
                    pe.wait_ge(flag_ready, 1)
                    pe.wait_ge(xt_ready, TT)
                pe.wait_ge(pt_in, 16 * (l + 1))
                for m in range(8):
                    job(n + m, (2 * m) % 4, 128, range(KC), xr)
                    s = (2 * m + 1) % 4
                    begin(s)
                    product(s, lambda kc: ring[:, (n + m) % RING, 1024 + 128 * kc:1152 + 128 * kc], range(2),
                            lambda kc: pt[:, kc, :], T // 2)
                n += 8
                def dense_blocks(n, count, blocks_before):
                    c0 = list(c.n)
                    with pe.Fori(0, count) as e:
                        k = 0
                        for kind, i, ps in ffn_plan():
                            if kind == "down" and i == 0:
                                pe.wait_ge(hid_ready, e * FT + (FT * blocks_before + FT))
                            for s, seen in ps:
                                nn = n + k
                                pe.wait_ge(emptied[s], e * FFN_USES[s] + (c0[s] + seen))
                                pe.wait_ge(w_loaded[nn % RING], e * (16 * BLOCK_JOBS // RING) + 16 * (nn // RING + 1))
                                tile = lambda kc: ring[:, nn % RING, 128 * kc:128 * kc + 128]
                                if kind == "up":
                                    product(s, tile, range(KC), xr, T // 2, note=jobs_begun)
                                else:
                                    product(s, tile, range(FT), lambda kc: hid[:, kc, :], T // 2, note=jobs_begun)
                                k += 1
                    for s in range(4):
                        c.n[s] += FFN_USES[s] * count

                all_empty()
                if l == 0:
                    dense_blocks(n, 2, 0)
                else:
                    def rows_in(i):
                        s = (3, 0)[i]
                        for q_ in range(4):
                            kc = 4 * i + q_
                            o = pair[s][:, 512 * (q_ // 2) + CAP * (q_ % 2):][:, 0:CAP]
                            for ct, rows in enumerate(C_ROWS):
                                last = nc.tensor.transpose(o[:, 128 * ct:128 * ct + rows], xgt[0:rows, ct, 128 * kc:128 * kc + 128],
                                                           cst[0:rows, C_ID:C_ID + rows])
                        last.then_inc(filled[s], 1)

                    pe.wait_ge(xg_in, 32)
                    for i, s in enumerate((3, 0)):
                        begin(s)
                        rows_in(i)
                    c0 = list(c.n)
                    with pe.Fori(0, NE) as e:
                        def held(s, seen):
                            pe.wait_ge(emptied[s], e * MOE_USES[s] + (c0[s] + seen))

                        def tile_in(k):
                            nn = n + k
                            pe.wait_ge(w_loaded[nn % RING], e * (16 * BLOCK_JOBS // RING) + 16 * (nn // RING + 1))
                            return ring[:, nn % RING, :]

                        held(3, 0)
                        for kind, i, s, seen in moe_plan():
                            if kind == "down" and i == 0:
                                for s2, n2 in ((0, 3), (1, 3), (2, 3), (3, 2)):
                                    held(s2, n2)
                            if kind == "xg" and i == 0:
                                pe.wait_ge(xg_in, e * 32 + 64)
                            if kind == "yg" and i == 0:
                                for s2, n2 in ((3, 3), (0, 4), (1, 4), (2, 4)):
                                    held(s2, n2)
                            if (kind, i) != ("yg", 1):
                                held(s, seen)
                            if kind == "xg":
                                rows_in(i)
                                continue
                            if kind == "yg":
                                rows = C_ROWS[i]
                                for kc in range(KC):
                                    last = nc.tensor.transpose(pair[s][0:rows, 128 * kc:128 * kc + 128],
                                                               yT[:, kc, 128 * i:128 * i + rows], ident)
                                last.then_inc(filled[s], 1)
                                continue
                            for j in range(2):
                                w = tile_in((2 * i if kind == "up" else 2 * FT + 2 * i) + j)
                                src, kn_ = (xg, KC) if kind == "up" else (hidg, FT)
                                for kc in range(kn_):
                                    last = mm(pair[s][:, 512 * j:512 * j + CAP], w[:, 128 * kc:128 * kc + 128], src[:, kc, :],
                                              start=(kc == 0), stop=(kc == kn_ - 1))
                                    if kc == 0:
                                        last.then_inc(jobs_begun, 1)
                            last.then_inc(filled[s], 1)
                    for s in range(4):
                        c.n[s] += MOE_USES[s] * NE
                    pe.wait_ge(comb_ready, TT)
                    for kc in range(KC):
                        s = kc % 4
                        begin(s)
                        for tt in range(TT):
                            rows = 128 if tt < 4 else NS
                            last = nc.tensor.transpose(pair[s][:, 128 * tt:128 * tt + rows], gt[0][0:rows, tt, 128 * kc:128 * kc + 128],
                                                       cst[0:rows, C_ID:C_ID + rows])
                        last.then_inc(filled[s], 1)
                    all_empty()
                    left = pe.value_load(flag[0:1, 0:1], min_val=0, max_val=2 * T)
                    with pe.If(left > 0):
                        for e in range(NE):
                            if e >= 2:
                                pe.wait_ge(gb_ready, e - 1)
                            p = pair[2 + e % 2]
                            for tt in range(TT):
                                rows = 128 if tt < 4 else NS
                                last = mm(p[:, 128 * tt:128 * tt + rows], over[0:rows, tt, e:e + 1].to_broadcast([rows, 128]),
                                          cst[0:rows, C_ID:C_ID + rows], start=True, stop=True)
                            last.then_inc(gb_mm, 1)
                        pe.wait_ge(gb_ready, NE)
                        dense_blocks(n + BLOCK_JOBS * NE, NE, 2)
                layer_norm(2 + 2 * l)

        @block.scalar
        def _(act):
            A = nc.scalar.activation
            steps = [0]
            c = Count()

            def link(ins):
                steps[0] += 1
                ins.then_inc(act_step, 1)
                act.wait_ge(act_step, steps[0])

            def got(s):
                act.wait_ge(filled[s], c.take(s))

            def layer_norm(k):
                if k == 2 * L:
                    act.wait_ge(last_emptied[0], 1)
                else:
                    act.wait_ge(emptied[0], c.take(0))
                    c.take(1)
                src = x if k == 0 else acc
                A(cat[:, :, :], src[:, :, :], ACT.Square).then_inc(squares, 1)
                act.wait_ge(rstd, k + 1)
                A(rst, rst, ACT.Sqrt).then_inc(rst_ready, 1)

            layer_norm(0)
            for h in range(NH):
                act.wait_ge(f_mm, h + 1)
                A(frow[:, h, 0:512], pair[2 + h % 2][:, 0:512], ACT.Copy)
                A(frow[:, h, 512:BW], pair[2 + h % 2][:, 512:BW], ACT.Copy).then_inc(f_ready, 1)

            def step_exp(v):
                act.wait_ge(par_in, 16 * v)
                A(sm[:, 0, :], par[:, 2, :], ACT.Exp).then_inc(ldt, 1)

            def radius(v):
                act.wait_ge(theta, 2 * v - 1)
                A(sm[:, 3, :], sm[:, 1, :], ACT.Exp)
                A(sm[:, 4, :], sm[:, 1, :], ACT.Exp, scale=float(CH)).then_inc(expd, 1)

            def angle(v):
                act.wait_ge(theta, 2 * v)
                A(sm[:, 5:7, :], sm[:, 7:9, :], ACT.Sin).then_inc(sincos, 1)

            for l in range(L):
                dst = [u[:, k, :] for k in range(4)] + [q[:, k, :] for k in range(4)] + [qi[:, k, :] for k in range(4)]
                dst += [kn[:, :], kin[:, :], vn[:, :], wn[:, :]]
                for m in range(16):
                    s = m % 4
                    if m == 4:
                        step_exp(2 * l + 1)
                    elif m == 6:
                        radius(2 * l + 1)
                    elif m == 8:
                        angle(2 * l + 1)
                    got(s)
                    d = dst[m]
                    if m < 4:
                        A(d[:, 0:256], pair[s][:, 0:256], ACT.Copy)
                        A(d[:, 256:T], pair[s][:, 512:512 + T - 256], ACT.Copy).then_inc(emptied[s], 1)
                        continue
                    rows = NH if m == 15 else 128
                    dn = d[:, 0:SEQ].rearrange("p (c j) -> p j c", j=CH)
                    by = HD ** -0.5 if 4 <= m < 8 else 1.0
                    A(dn[:, 0:4, :], pair[s][0:rows, 0:256].rearrange("p (j c) -> p j c", j=4), ACT.Copy, scale=by)
                    A(dn[:, 4:8, :], pair[s][0:rows, 512:768].rearrange("p (j c) -> p j c", j=4), ACT.Copy, scale=by)
                    A(d[:, SEQ:T], pair[s][0:rows, 768:768 + NS], ACT.Copy, scale=by).then_inc(emptied[s], 1)
                act.wait_ge(tok_mm, l + 1)
                A(vtok[:, 0:NQT, :], bank(0).rearrange("p (b c) -> p b c", b=NQT), ACT.Copy)
                A(vtok[0:NS, NQT, :], bank(1)[0:NS, 0:128], ACT.Copy).then_inc(tok_ready, 1)
                A(wtok[:, :, :], bank(2)[:, 0:NQT * NH].rearrange("p (b c) -> p b c", b=NQT), ACT.Copy).then_inc(tok_ready, 1)

                for hf in range(2):
                    v = 2 * l + hf + 1
                    act.wait_ge(bt_mm, v)
                    for k in range(2):
                        ins = A(BT[:, k].rearrange("p e n -> p (e n)"), pair[k][:, :], ACT.Copy)
                    ins.then_inc(bt_ready, 1)
                    act.wait_ge(kd_mm, v)
                    for k in range(2):
                        ins = A(cf[0:GC, 1024 * k:1024 * k + 1024], pair[2 + k][0:GC, :], ACT.Copy)
                    ins.then_inc(kd_ready, 1)
                    if hf == 0:
                        step_exp(v + 1)
                        radius(v + 1)
                        angle(v + 1)
                    else:
                        act.wait_ge(y_out, 192 * (v - 1))
                    act.wait_ge(y_mm, v)
                    for a in range(2):
                        ya = Y.rearrange("p (e a) c -> p a e c", a=2)[:, a]
                        for k, n in enumerate((6, HP - 6)):
                            ins = A(ya[:, 6 * k:6 * k + n, :], bank(4 + 2 * a + k)[:, 0:CW * n].rearrange("p (g c) -> p g c", g=n), ACT.Copy)
                    ins.then_inc(y_ready, 1)
                ni, npt = 24 * l, 20 * l
                for b in range(NQT):
                    w = 128 * (b + 1)
                    for h in range(NH):
                        if h % 4 == 0:
                            act.wait_ge(nmx_ready, 2 * (NQT * l + b) + h // 4 + 1)
                        A(Lg[:, h, 0:w], Lg[:, h, 0:w], ACT.Exp, bias=nmx[:, h:h + 1],
                          accum_out=sums[:, h:h + 1]).then_inc(exp_ready, 1)
                    if b + 1 < NQT:
                        for h in range(NH):
                            act.wait_ge(idx_mm, ni + 1)
                            if ni >= 4:
                                act.wait_ge(relu_used, ni - 3)
                            A(rl[:, ni % 4, 0:w + 128], bank(ni % 2)[:, 0:w + 128], ACT.Relu).then_inc(relu_ready, 1)
                            ni += 1
                    act.wait_ge(rs_ready, NQT * l + b + 1)
                    for h in range(NH):
                        ins = A(Lg[:, h, 0:w], Lg[:, h, 0:w], ACT.Copy, scale=rs[:, h:h + 1])
                    ins.then_inc(prob_ready, 1)
                    if b == 0:
                        act.wait_ge(y_out, 192 * 2 * (l + 1))
                    for g in range(2):
                        for kt in range(b + 1):
                            act.wait_ge(pt_mm, npt + 1)
                            A(PT[:, g, kt, :], bank(5 + npt % 2), ACT.Copy).then_inc(pt_ready, 1)
                            npt += 1
                    act.wait_ge(pv_mm, NQT * l + b + 1)
                    for i in range(4):
                        o = cat[:, 4 + i, 0:SEQ].rearrange("p (j c) -> p c j", j=CH)[:, 16 * b:16 * b + 16, :]
                        ins = A(o, bank(7)[:, 128 * i:128 * i + 128].rearrange("p (c j) -> p c j", j=CH), ACT.Copy)
                    ins.then_inc(pv_ready, 1)
                    if b == 1:
                        act.wait_ge(yd_ready, l + 1)
                        A(u, u, ACT.Gelu_apprx_tanh).then_inc(gelu_ready, 1)

                for r in range(2):
                    v = 2 * l + r + 1
                    act.wait_ge(si_mm, v)
                    if r:
                        act.wait_ge(sc_mm, v - 1)
                    A(rls[:, 0:PAST], bank(0), ACT.Relu)
                    A(rls[:, PAST:SK], bank(1)[:, 0:NS], ACT.Relu).then_inc(srelu, 1)
                for r in range(2):
                    v = 2 * l + r + 1
                    act.wait_ge(snmx, v)
                    A(Ls, Ls, ACT.Exp, bias=nms[:, 0:1], accum_out=nms[:, 1:2]).then_inc(sexp, 1)
                    act.wait_ge(spt_mm, v)
                    A(PTs[:, 0:NPG, :], bank(4).rearrange("p (k c) -> p k c", k=NPG), ACT.Copy)
                    A(PTs[0:NS, NPG, :], bank(5)[0:NS, 0:128], ACT.Copy).then_inc(spt_ready, 1)
                    act.wait_ge(spv_mm, v)
                    pv = bank(6)[:, 0:128].rearrange("p (b g i t) -> p g b i t", b=4, g=2, i=4)
                    for g in range(2):
                        for i in range(4):
                            o = cat[64 * g:64 * g + 64, 4 + i, SEQ:T].rearrange("p (t b) -> p b t", b=NB)[:, 4 * r:4 * r + 4, :]
                            ins = A(o, pv[64 * g:64 * g + 64, g, :, i, :], ACT.Copy)
                    ins.then_inc(spv_ready, 1)

                for m in range(8):
                    s = m % 4
                    if m % 2 == 0:
                        a_use = c.take(s)
                        continue
                    got(s)
                    act.wait_ge(emptied[s - 1], a_use - 1)
                    A(halves(sg[:, m // 2 % 2, :]), even(s), ACT.Sigmoid).then_inc(emptied[s], 1)
                for m in range(8):
                    c.take(m % 4)
                layer_norm(1 + 2 * l)
                if l == 1:
                    for tt in range(TT):
                        rows = 128 if tt < 4 else NS
                        act.wait_ge(xt_mm, tt + 1)
                        A(xtok[0:rows, tt, :], pair[1 + tt % 3][0:rows, :], ACT.Copy).then_inc(xt_ready, 1)
                    act.wait_ge(gdiff, 1)
                    A(rlog, rlog, ACT.Exp)
                    A(rsm[:, :, 1:2], rsm[:, :, 0:1], ACT.Exp).then_inc(gexp, 1)
                for m in range(8):
                    s = (2 * m) % 4
                    got(s)
                    c.take(s + 1)
                    if m >= 2:
                        act.wait_ge(ple_used, 8 * l + m - 1)
                    A(halves(sg[:, m % 2, :]), even(s), ACT.Sigmoid).then_inc(emptied[s], 1)
                act.wait_ge(ple_used, 8 * (l + 1))

                def dense_blocks(count):
                    c0 = list(c.n)
                    with act.Fori(0, count) as e:
                        for kind, f, ps in ffn_plan():
                            if kind == "up":
                                (s, seen), (s2, seen2) = ps
                                act.wait_ge(filled[s], e * FFN_USES[s] + (c0[s] + seen + 1))
                                if f >= 2:
                                    act.wait_ge(emptied[s2], e * FFN_USES[s2] + (c0[s2] + seen2))
                                A(halves(sg[:, f % 2, :]), even(s), ACT.Silu).then_inc(emptied[s], 1)
                    for s in range(4):
                        c.n[s] += FFN_USES[s] * count

                if l == 0:
                    dense_blocks(2)
                else:
                    def rows_in(i, s):
                        A(xg[:, 4 * i:4 * i + 4, :].rearrange("p (h k) c -> p h (k c)", h=2), banks(s, 2 * CAP), ACT.Copy).then_inc(emptied[s], 1)

                    for i, s in enumerate((3, 0)):
                        got(s)
                        rows_in(i, s)
                    c0 = list(c.n)
                    with act.Fori(0, NE) as e:
                        for kind, i, s, seen in moe_plan():
                            if kind == "down":
                                continue
                            act.wait_ge(filled[s], e * MOE_USES[s] + (c0[s] + seen + 1))
                            if kind == "up":
                                if i >= 2:
                                    s2 = (i - 2) % 4
                                    act.wait_ge(emptied[s2], e * MOE_USES[s2] + (c0[s2] + (i - 2) // 4 + 1))
                                A(sg[:, i % 2, 0:CAP], pair[s][:, 0:CAP], ACT.Silu).then_inc(silu_ready, 1)
                            elif kind == "xg":
                                rows_in(i, s)
                            else:
                                if i == 0:
                                    act.wait_ge(y_free, e + 1)
                                A(ygt[0:C_ROWS[i], i, :], pair[s][0:C_ROWS[i], :], ACT.Copy).then_inc(emptied[s], 1)
                    for s in range(4):
                        c.n[s] += MOE_USES[s] * NE
                    for kc in range(KC):
                        c.take(kc % 4)
                    act.wait_ge(flag_ready, 1)
                    left = act.value_load(flag[0:1, 0:1], min_val=0, max_val=2 * T)
                    with act.If(left > 0):
                        for e in range(NE):
                            act.wait_ge(gb_mm, e + 1)
                            A(gb[:, e, :], pair[2 + e % 2][:, 0:T], ACT.Copy).then_inc(gb_ready, 1)
                        dense_blocks(NE)
                layer_norm(2 + 2 * l)

        @block.vector
        def _(dve):
            V = nc.vector
            MAGIC = 1.5 * 2.0 ** 23
            TWO_PI = (6.28125, 1.93500518798828125e-3, 2 * math.pi - 6.28125 - 1.93500518798828125e-3)
            steps = [0]
            c = Count()

            def link(ins):
                steps[0] += 1
                ins.then_inc(dve_step, 1)
                dve.wait_ge(dve_step, steps[0])

            def got(s):
                dve.wait_ge(filled[s], c.take(s))

            def layer_norm(k):
                src = x if k == 0 else acc
                f, m, n = (last_filled, last_emptied, [1, 1]) if k == 2 * L else (filled, emptied, [c.take(0), c.take(1)])
                dve.wait_ge(f[0], n[0])
                for h in range(2):
                    cols = slice(T // 2 * h, T // 2 * h + T // 2)
                    ins = V.tensor_tensor(src[:, :, cols], src[:, :, cols],
                                          bc(pair[0][:, 512 * h:512 * h + T // 2], 1, KC), ALU.subtract)
                ins.then_inc(m[0], 1)
                dve.wait_ge(f[1], n[1])
                ins = V.tensor_scalar(halves(rst), even(1), LN_EPS, None, ALU.add)
                ins.then_inc(m[1], 1)
                dve.wait_ge(m[1], n[1])
                V.reciprocal(rst, rst).then_inc(rstd, 1)
                dve.wait_ge(rst_ready, k + 1)
                link(V.tensor_tensor(src[:, :, :], src[:, :, :], bc(rst, 1, KC), ALU.mult))
                for kc in range(KC):
                    ins = V.tensor_scalar(x[:, kc, :], src[:, kc, :], lnp[:, 2 * k, kc:kc + 1], lnp[:, 2 * k + 1, kc:kc + 1],
                                          ALU.mult, ALU.add)
                ins.then_inc(x_ready, 1)

            def cmul(o, a, b, t1, t2, negate_im=False):
                V.tensor_tensor(t1, a[0], b[0], ALU.mult)
                link(V.tensor_tensor(t2, a[1], b[1], ALU.mult))
                link(V.tensor_tensor(o[0], t1, t2, ALU.subtract))
                V.tensor_tensor(t1, a[0], b[1], ALU.mult)
                link(V.tensor_tensor(t2, a[1], b[0], ALU.mult))
                if negate_im:
                    link(V.scalar_tensor_tensor(o[1], t1, -1.0, t2, ALU.mult, ALU.subtract))
                else:
                    link(V.tensor_tensor(o[1], t1, t2, ALU.add))

            def top(vals, work, eight, k, pad=None):
                src, n = vals, vals.shape[1]
                for i in range(k // 8):
                    link(V.max(eight, src))
                    link(V.match_replace(work[:, 0:n], eight, src, GONE))
                    src = work[:, 0:n]
                if k % 8:
                    link(V.max(eight, src))
                    link(V.memset(eight[:, k % 8:8], pad))
                    link(V.match_replace(work, eight, work, GONE))

            dve.wait_ge(consts_in, 80)
            dve.wait_ge(rel_in, 32)
            V.tensor_tensor(reltk, reltk, cst[:, C_MT:C_MT + 128], ALU.mult).then_inc(tk_ready, 1)
            dve.wait_ge(x_in, 32)
            layer_norm(0)
            dve.wait_ge(bs_mm, 1)
            V.tensor_copy(bs[:, 0:512], pair[2][:, 0:512])
            V.tensor_copy(bs[:, 512:SK], pair[2][:, 512:SK]).then_inc(bs_ready, 1)

            for l in range(L):
                for s in range(4):
                    for _ in range(4):
                        c.take(s)
                for hf in range(2):
                    v = 2 * l + hf + 1
                    dve.wait_ge(par_in, 16 * v)
                    dve.wait_ge(ldt, v)
                    r_ = lambda i: sm[:, i, :]
                    are, aim = par[:, 0, :], par[:, 1, :]
                    V.tensor_tensor(r_(2), aim, r_(0), ALU.mult)
                    V.tensor_tensor(r_(1), are, r_(0), ALU.mult).then_inc(theta, 1)
                    dve.wait_ge(theta, 2 * v - 1)
                    link(V.tensor_scalar(r_(9), r_(2), 1 / (2 * math.pi), MAGIC, ALU.mult, ALU.add))
                    link(V.tensor_scalar(r_(9), r_(9), MAGIC, None, ALU.subtract))
                    for i, part in enumerate(TWO_PI):
                        link(V.scalar_tensor_tensor(r_(7) if i == 2 else r_(2), r_(9), -part, r_(2), ALU.mult, ALU.add))
                    link(V.tensor_scalar(r_(10), r_(7), math.pi / 2, None, ALU.add))
                    link(V.tensor_scalar(r_(11), r_(10), math.pi, 2 * math.pi, ALU.is_gt, ALU.mult))
                    link(V.tensor_tensor(r_(8), r_(10), r_(11), ALU.subtract))
                    V.tensor_scalar(sm[:, 7:9, :], sm[:, 7:9, :], 3.1415925, -3.1415925, ALU.min, ALU.max).then_inc(theta, 1)
                    V.memset(P[0][:, 0, :], 1.0)
                    V.memset(P[1][:, 0, :], 0.0)
                    dve.wait_ge(sincos, v)
                    dve.wait_ge(expd, v)
                    V.tensor_tensor(P[0][:, 1, :], r_(6), r_(3), ALU.mult)
                    link(V.tensor_tensor(P[1][:, 1, :], r_(5), r_(3), ALU.mult))
                    for w in (1, 2, 4):
                        t1 = T1[:, 0:w * HP].rearrange("p (m e) -> p m e", e=HP)
                        t2 = T2[:, 0:w * HP].rearrange("p (m e) -> p m e", e=HP)
                        cmul([P[k][:, w + 1:2 * w + 1, :] for k in range(2)], [P[k][:, 1:w + 1, :] for k in range(2)],
                             [P[k][:, w:w + 1, :].to_broadcast([128, w, HP]) for k in range(2)], t1, t2)
                    V.tensor_scalar(r_(12), P[0][:, 1, :], -1.0, None, ALU.add)
                    V.tensor_tensor(r_(14), are, are, ALU.mult)
                    link(V.tensor_tensor(r_(15), aim, aim, ALU.mult))
                    link(V.tensor_tensor(r_(13), r_(14), r_(15), ALU.add))
                    link(V.reciprocal(r_(16), r_(13)))
                    V.tensor_tensor(r_(14), r_(12), are, ALU.mult)
                    link(V.tensor_tensor(r_(15), P[1][:, 1, :], aim, ALU.mult))
                    link(V.tensor_tensor(r_(17), r_(14), r_(15), ALU.add))
                    V.tensor_tensor(r_(14), P[1][:, 1, :], are, ALU.mult)
                    link(V.tensor_tensor(r_(15), r_(12), aim, ALU.mult))
                    link(V.tensor_tensor(r_(18), r_(14), r_(15), ALU.subtract))
                    V.tensor_tensor(r_(17), r_(17), r_(16), ALU.mult)
                    link(V.tensor_tensor(r_(18), r_(18), r_(16), ALU.mult))
                    t1 = T1[:, 0:HP * GC].rearrange("p (e c) -> p e c", e=HP)
                    t2 = T2[:, 0:HP * GC].rearrange("p (e c) -> p e c", e=HP)
                    cmul(Bb, [bc(r_(17 + k), 2, GC) for k in range(2)], [pB[:, k] for k in range(2)], t1, t2)

                    def powers(o, base, n, **kw):
                        t1 = T1[:, 0:HP * n * GC].rearrange("p (e m c) -> p e m c", e=HP, m=n)
                        t2 = T2[:, 0:HP * n * GC].rearrange("p (e m c) -> p e m c", e=HP, m=n)
                        cmul(o, [bc(P[k][:, 0:n, :].rearrange("p m e -> p e m"), 3, GC) for k in range(2)],
                             [bc(t, 2, n) for t in base], t1, t2, **kw)

                    powers(BP, Bb, CH)
                    V.memset(m8x[:, 0:1], 0.0).then_inc(bp_ready, 1)
                    if hf:
                        dve.wait_ge(y_mm, v - 1)
                    powers(CP, [pB[:, 2], pB[:, 3]], CH + 1, negate_im=True)
                    V.memset(m8x[:, 0:1], 0.0).then_inc(cp_ready, 1)
                    a, b_ = [r_(6), r_(5)], [r_(19), r_(20)]
                    for o in ([r_(19), r_(20)], [r_(21), r_(22)], [E[k][:, :, 0] for k in range(2)]):
                        cmul(o, a, a, T1[:, 0:HP], T2[:, 0:HP])
                        a = o
                    w = 1
                    while w < NC:
                        t1 = T1[:, 0:HP * w].rearrange("p (e c) -> p e c", e=HP)
                        t2 = T2[:, 0:HP * w].rearrange("p (e c) -> p e c", e=HP)
                        cmul([E[k][:, :, w:2 * w] for k in range(2)], [E[k][:, :, 0:w] for k in range(2)],
                             [E[k][:, :, w - 1:w].to_broadcast([128, HP, w]) for k in range(2)], t1, t2)
                        w *= 2
                    link(V.tensor_copy(R8, bc(r_(4), 2, NC)))
                    link(V.memset(R8[:, :, 0:1], 0.0))
                    dve.wait_ge(g_mm, v)
                    g_in = [bank(k).rearrange("p (e c) -> p e c", e=HP) for k in range(2)]
                    t1 = T1[:, 0:HP * NC].rearrange("p (e c) -> p e c", e=HP)
                    t2 = T2[:, 0:HP * NC].rearrange("p (e c) -> p e c", e=HP)
                    V.tensor_tensor(t1, E[0], g_in[0], ALU.mult)
                    link(V.tensor_tensor(t2, E[1], g_in[1], ALU.mult))
                    link(V.tensor_tensor(GM[0], t1, t2, ALU.add))
                    V.tensor_tensor(t1, E[0], g_in[1], ALU.mult)
                    link(V.tensor_tensor(t2, E[1], g_in[0], ALU.mult))
                    link(V.tensor_tensor(GM[1], t1, t2, ALU.subtract))
                    flat = lambda t: t.rearrange("p e c -> p (e c)")
                    for k in range(2):
                        ins = V.tensor_tensor_scan(flat(GS[k]), flat(R8), flat(GM[k]), 0.0, ALU.mult, ALU.add)
                    link(ins)
                    cmul([H[k][:, :, NB + 1:] for k in range(2)], E, GS, t1, t2)
                    for k in range(2):
                        V.memset(H[k][:, :, NB:NB + 1], 0.0)
                        V.tensor_copy(H[k][:, :, 0:NB], pH[:, k])
                    t1 = T1[:, 0:HP * NB].rearrange("p (e c) -> p e c", e=HP)
                    t2 = T2[:, 0:HP * NB].rearrange("p (e c) -> p e c", e=HP)
                    if hf or l:
                        dve.wait_ge(stored, 16 * (2 * l + hf + 4 * l))
                    so = [hout[:, k, :, 1:NB + 1] for k in range(2)]
                    cmul(so, [bc(P[k][:, DT, :], 2, NB) for k in range(2)], [pH[:, k] for k in range(2)], t1, t2)
                    for k in range(2):
                        V.tensor_tensor(so[k], so[k], bank(2)[:, 64 * k:64 * k + 64].rearrange("p (e b) -> p e b", e=HP), ALU.add)
                        ins = V.tensor_copy(hout[:, k, :, 0:1], H[k][:, :, NB + NC:NB + NC + 1])
                    ins.then_inc(h_ready, 1)

                dve.wait_ge(tok_ready, 2 * l + 2)
                dve.wait_ge(rbias_in, 16)
                dve.wait_ge(y_ready, 2 * l + 2)
                dve.wait_ge(stored, 16 * (2 * (l + 1) + 4 * l))
                V.tensor_scalar(negid, ident, NEG, None, ALU.mult).then_inc(hide_ready, 1)

                def scores(b, ni):
                    w = 128 * (b + 1)
                    for h in range(NH):
                        dve.wait_ge(relu_ready, ni + 1)
                        if h == 0:
                            V.tensor_scalar(sc[:, 0:w], rl[:, ni % 4, 0:w], wtok[:, b, h:h + 1], None, ALU.mult).then_inc(relu_used, 1)
                        else:
                            V.scalar_tensor_tensor(sc[:, 0:w], rl[:, ni % 4, 0:w], wtok[:, b, h:h + 1], sc[:, 0:w],
                                                   ALU.mult, ALU.add).then_inc(relu_used, 1)
                        ni += 1
                        dve.wait_ge(relu_used, ni)
                    V.tensor_scalar(sc[:, 0:w - 128], sc[:, 0:w - 128], IDX_SCALE, None, ALU.mult)
                    link(V.scalar_tensor_tensor(sc[:, w - 128:w], sc[:, w - 128:w], IDX_SCALE, cst[:, C_MC:C_MC + 128], ALU.mult, ALU.add))

                def choose(b):
                    w = 128 * (b + 1)
                    top(sc[:, 0:w], wk, m8, TOPK_P)
                    V.tensor_tensor(nosel[:, 0:w], wk[:, 0:w], sc[:, 0:w], ALU.is_equal).then_inc(hide_ready, 1)

                nl = NH * NQT * l
                for b in range(NQT):
                    w = 128 * (b + 1)
                    if l or b:
                        dve.wait_ge(pt_ready, 20 * l + b * (b + 1))
                    for h in range(NH):
                        dve.wait_ge(lg_mm, nl + 1)
                        V.tensor_tensor_reduce(Lg[:, h, 0:w], bank(2 + nl % 3)[:, 0:w], rbias[:, h, SEQ - w:SEQ], 1.0, -3.0e38,
                                               ALU.add, ALU.max, accum_out=nmx[:, h:h + 1]).then_inc(lg_used, 1)
                        nl += 1
                        if h % 4 == 3:
                            dve.wait_ge(lg_used, nl)
                            V.tensor_scalar(nmx[:, h - 3:h + 1], nmx[:, h - 3:h + 1], -1.0, None, ALU.mult).then_inc(nmx_ready, 1)
                    if b + 1 < NQT:
                        scores(b + 1, NH * (3 * l + b))
                    dve.wait_ge(exp_ready, nl)
                    V.reciprocal(rs, sums).then_inc(rs_ready, 1)
                    if b + 1 < NQT:
                        choose(b + 1)
                    if b == 1:
                        dve.wait_ge(y_in, 16 * (l + 1))
                        for k in range(4):
                            ins = V.scalar_tensor_tensor(u[:, k, :], u[:, k, :], dsk[:, l, k:k + 1], cat[:, k, :], ALU.mult, ALU.add)
                        ins.then_inc(yd_ready, 1)

                dve.wait_ge(pv_ready, NQT * (l + 1))
                V.memset(Qzi, 0.0)
                link(V.memset(Qz, 0.0))
                for a in range(2):
                    for dst, src in ((Qzi, qi), (Qz, q)):
                        for i in range(4):
                            ins = V.tensor_copy(dst[64 * a:64 * a + 64, :, a, i, :],
                                                src[64 * a:64 * a + 64, i, SEQ:T].rearrange("p (t b) -> p b t", b=NB))
                ins.then_inc(qz_ready, 1)
                dve.wait_ge(wr_mm, l + 1)
                for r in range(2):
                    ins = V.tensor_tensor(wr[:, r, :], bank(4)[:, 0:NS], cst[:, C_MW + NS * r:C_MW + NS * r + NS], ALU.mult)
                ins.then_inc(wr_ready, 1)
                dve.wait_ge(sc_mm, 2 * l + 2)
                V.tensor_scalar(scs[0:NS, 0:PAST], bank(2)[0:NS, :], IDX_SCALE, None, ALU.mult)
                V.memset(wks[0:NS, SK:SK + 7], 3.0e38)
                link(V.scalar_tensor_tensor(scs[0:NS, PAST:SK], bank(3)[0:NS, 0:NS], IDX_SCALE, cst[0:NS, C_MS:C_MS + NS],
                                            ALU.mult, ALU.add))
                top(scs[0:NS, :], wks[0:NS, :], m8s[0:NS, :], TOPK_S, 3.0e38)
                link(V.tensor_tensor(nss[0:NS, :], wks[0:NS, 0:SK], scs[0:NS, :], ALU.is_equal))
                V.tensor_scalar(nss[0:NS, :], nss[0:NS, :], NEG, None, ALU.mult).then_inc(nosel_ready, 1)
                for r in range(2):
                    v = 2 * l + r + 1
                    dve.wait_ge(sl_mm, v)
                    if r:
                        dve.wait_ge(spt_ready, v - 1)
                    V.tensor_tensor(Ls[:, 0:PAST], bank(0), bs[:, 0:PAST], ALU.add)
                    link(V.tensor_tensor(Ls[:, PAST:SK], bank(1)[:, 0:NS], bs[:, PAST:SK], ALU.add))
                    link(V.tensor_reduce(nms[:, 0:1], Ls, AX.X, ALU.max))
                    V.tensor_scalar(nms[:, 0:1], nms[:, 0:1], -1.0, None, ALU.mult).then_inc(snmx, 1)
                    dve.wait_ge(sexp, v)
                    link(V.reciprocal(nms[:, 2:3], nms[:, 1:2]))
                    V.tensor_scalar(Ls, Ls, nms[:, 2:3], None, ALU.mult).then_inc(sprob, 1)

                for m in range(0, 8, 2):
                    s = m % 4
                    got(s)
                    dve.wait_ge(emptied[s + 1], c.take(s + 1))
                    V.tensor_tensor(halves(cat[:, m // 2, :]), halves(sg[:, m // 2 % 2, :]), even(s), ALU.mult).then_inc(emptied[s], 1)
                for m in range(8):
                    s = m % 4
                    got(s)
                    V.scalar_tensor_tensor(halves(acc[:, m, :]), halves(x[:, m, :]), ALPHA, even(s), ALU.mult, ALU.add).then_inc(emptied[s], 1)
                for s in range(4):
                    dve.wait_ge(emptied[s], c.n[s])
                V.memset(m8x[:, 0:1], 0.0).then_inc(acc_ready, 1)
                layer_norm(1 + 2 * l)
                if l == 1:
                    link(V.memset(rlog, 0.0))
                    V.memset(rank, 0.0)
                    dve.wait_ge(r_mm, 1)
                    V.tensor_tensor(rlog[:, 0:4, :], bank(0)[:, 0:4 * NE].rearrange("p (n e) -> p n e", n=4), bc(brt[:, :], 1, 4), ALU.add)
                    V.memset(rwk, 3.0e38)
                    link(V.tensor_tensor(rlog[0:NS, 4, :], bank(0)[0:NS, 4 * NE:5 * NE], brt[0:NS, :], ALU.add))
                    V.tensor_copy(rwk[:, :, 0:NE], rlog)
                    for tt in range(TT):
                        ins = V.max(rtop[:, tt, :], rlog[:, tt, :])
                    link(ins)
                    V.tensor_copy(rtwo[:, :, 0:2], rtop[:, :, 0:2])
                    link(V.memset(rtwo[:, :, 2:8], 3.0e38))
                    for tt in range(TT):
                        ins = V.match_replace(rwk[:, tt, :], rtwo[:, tt, :], rwk[:, tt, :], GONE)
                    link(ins)
                    link(V.tensor_tensor(sel, rwk[:, :, 0:NE], rlog, ALU.not_equal))
                    for lo in (32, 64):
                        ins = V.memset(sel[lo:2 * lo, TT - 1, :], 0.0)
                    ins.then_inc(sel_ready, 1)
                    dve.wait_ge(sel_ready, 1)
                    V.tensor_tensor(rlog, rlog, rtop[:, :, 0:1].to_broadcast([128, TT, NE]), ALU.subtract)
                    V.tensor_tensor(rsm[:, :, 0:1], rtop[:, :, 1:2], rtop[:, :, 0:1], ALU.subtract).then_inc(gdiff, 1)
                    dve.wait_ge(gexp, 1)
                    link(V.tensor_scalar(rsm[:, :, 2:3], rsm[:, :, 1:2], 1.0, None, ALU.add))
                    link(V.reciprocal(rsm[:, :, 3:4], rsm[:, :, 2:3]))
                    link(V.tensor_tensor(gts, sel, rlog, ALU.mult))
                    link(V.tensor_tensor(gts, gts, rsm[:, :, 3:4].to_broadcast([128, TT, NE]), ALU.mult))
                    dve.wait_ge(rank_mm, 1)
                    V.tensor_copy(rank[:, 0:4, :], bank(0)[:, 64:64 + 4 * NE].rearrange("p (n e) -> p n e", n=4))
                    link(V.tensor_copy(rank[0:NS, 4, :], bank(0)[0:NS, 64 + 4 * NE:64 + 5 * NE]))
                    cc = lambda at, n=NE: bc(cst[:, at:at + n], 1, TT)
                    link(V.tensor_tensor(order, rank, cc(C_E1), ALU.add))
                    V.tensor_scalar(over, sel, -1.0, -1.0e6, ALU.add, ALU.mult)
                    link(V.tensor_tensor(tmp8, order, sel, ALU.mult))
                    link(V.tensor_reduce(v01[:, :, 1:2], tmp8, AX.X, ALU.max))
                    link(V.tensor_tensor(tmp8, tmp8, over, ALU.add))
                    link(V.tensor_reduce(v01[:, :, 0:1], tmp8, AX.X, ALU.min))
                    for k in range(2):
                        at = v01[:, :, k:k + 1].to_broadcast([128, TT, NE])
                        for what, o in ((rank, r01), (cc(C_EC), b01), (gts, g01)):
                            link(V.tensor_tensor(tmp8, order, at, ALU.is_equal))
                            link(V.tensor_tensor(tmp8, tmp8, sel, ALU.mult))
                            link(V.tensor_tensor(tmp8, tmp8, what, ALU.mult))
                            link(V.tensor_reduce(o[:, :, k:k + 1], tmp8, AX.X, ALU.add))
                    link(V.tensor_scalar(ok01, r01, float(CAP), None, ALU.is_lt))
                    V.tensor_tensor(g01, g01, ok01, ALU.mult)
                    link(V.tensor_tensor(ix01, b01, r01, ALU.add))
                    link(V.tensor_tensor(ix01, ix01, ok01, ALU.mult))
                    ixf = lambda t: t.rearrange("p t k -> p (t k)")
                    V.tensor_copy(idx[:, 2 * TT:4 * TT], ixf(ix01))
                    link(V.tensor_scalar(r01, ok01, -1.0, -1.0, ALU.add, ALU.mult))
                    for k in range(2):
                        ins = V.tensor_scalar(b01[:, :, k], cst[:, C_TI:C_TI + TT], float(XROWS + k * TT * 128), None, ALU.add)
                    link(ins)
                    link(V.tensor_tensor(b01, b01, r01, ALU.mult))
                    link(V.tensor_tensor(b01, b01, ix01, ALU.add))
                    V.tensor_copy(idx[:, 0:2 * TT], ixf(b01)).then_inc(idx_ready, 1)
                    link(V.tensor_scalar(over, rank, float(CAP), None, ALU.is_ge))
                    link(V.tensor_tensor(over, over, sel, ALU.mult))
                    V.tensor_reduce(ovs, over.rearrange("p t e -> p (t e)"), AX.X, ALU.add).then_inc(ov_ready, 1)
                    dve.wait_ge(ov_ready, 1)
                    V.tensor_tensor(over, over, gts, ALU.mult)
                    dve.wait_ge(flag_mm, 1)
                    V.tensor_copy(flag[0:1, 0:1], bank(0)[0:1, 0:1]).then_inc(flag_ready, 1)
                for m in range(8):
                    s = (2 * m) % 4
                    dve.wait_ge(emptied[s], c.take(s))
                    got(s + 1)
                    sv = halves(sg[:, m % 2, :])
                    V.tensor_tensor(sv, sv, even(s + 1), ALU.mult).then_inc(emptied[s + 1], 1)
                    dve.wait_ge(emptied[s + 1], c.n[s + 1])
                    V.scalar_tensor_tensor(acc[:, m, :], x[:, m, :], ALPHA, sg[:, m % 2, :], ALU.mult, ALU.add).then_inc(ple_used, 1)
                def dense_blocks(count):
                    c0 = list(c.n)
                    with dve.Fori(0, count) as e:
                        for kind, i, ps in ffn_plan():
                            def count_(s, seen):
                                return e * FFN_USES[s] + (c0[s] + seen + 1)
                            if kind == "up":
                                (s, seen), (s2, seen2) = ps
                                dve.wait_ge(emptied[s], count_(s, seen))
                                dve.wait_ge(filled[s2], count_(s2, seen2))
                                V.tensor_tensor(halves(hid[:, i, :]), halves(sg[:, i % 2, :]), even(s2), ALU.mult).then_inc(emptied[s2], 1)
                                dve.wait_ge(emptied[s2], count_(s2, seen2))
                                if l == 0:
                                    V.memset(m8x[:, 0:1], 0.0).then_inc(hid_ready, 1)
                                else:
                                    V.tensor_tensor(hid[:, i, :], hid[:, i, :], gb[:, bass.ds(e, 1), :].rearrange("p o t -> p (o t)"),
                                                    ALU.mult).then_inc(hid_ready, 1)
                            else:
                                (s, seen), = ps
                                dve.wait_ge(filled[s], count_(s, seen))
                                V.tensor_tensor(halves(acc[:, i, :]), halves(acc[:, i, :]), even(s), ALU.add).then_inc(emptied[s], 1)
                    for s in range(4):
                        c.n[s] += FFN_USES[s] * count
                        dve.wait_ge(emptied[s], c.n[s])

                if l == 0:
                    dense_blocks(2)
                else:
                    for s in (3, 0):
                        c.take(s)
                    c0 = list(c.n)
                    with dve.Fori(0, NE) as e:
                        for kind, i, s, seen in moe_plan():
                            if kind == "up":
                                dve.wait_ge(silu_ready, e * FT + i + 1)
                                V.tensor_tensor(hidg[:, i, :], sg[:, i % 2, 0:CAP], pair[s][:, 512:512 + CAP], ALU.mult).then_inc(emptied[s], 1)
                            elif kind == "down":
                                dve.wait_ge(filled[s], e * MOE_USES[s] + (c0[s] + seen + 1))
                                V.tensor_copy(yT[:, 2 * i:2 * i + 2, :], banks(s, CAP)).then_inc(emptied[s], 1)
                    for s in range(4):
                        c.n[s] += MOE_USES[s] * NE
                    dve.wait_ge(gt_in, 16 * 2 * TT)
                    for tt in range(TT):
                        rows = 128 if tt < 4 else NS
                        link(V.tensor_scalar(gt[0][0:rows, tt, :], gt[0][0:rows, tt, :], g01[0:rows, tt, 0:1], None, ALU.mult))
                        V.scalar_tensor_tensor(gt[0][0:rows, tt, :], gt[1][0:rows, tt, :], g01[0:rows, tt, 1:2], gt[0][0:rows, tt, :],
                                               ALU.mult, ALU.add).then_inc(comb_ready, 1)
                    for kc in range(KC):
                        s = kc % 4
                        got(s)
                        V.tensor_tensor(acc[:, kc, :], acc[:, kc, :], pair[s][:, 0:T], ALU.add).then_inc(emptied[s], 1)
                    for s in range(4):
                        dve.wait_ge(emptied[s], c.n[s])
                    left = dve.value_load(flag[0:1, 0:1], min_val=0, max_val=2 * T)
                    with dve.If(left > 0):
                        dve.wait_ge(gb_ready, NE)
                        dense_blocks(NE)
                V.memset(m8x[:, 0:1], 0.0).then_inc(acc_ready, 1)
                layer_norm(2 + 2 * l)


def _bucket(dist):
    import numpy as np
    n = np.maximum(dist, 0)
    big = 16 + (np.log(np.maximum(n, 1).astype(np.float32) / np.float32(16)) / np.float32(math.log(8.0)) * np.float32(16)).astype(np.int32)
    return np.where(n < 16, n, np.minimum(big, 31))


def _consts():
    import numpy as np
    c = np.zeros((128, C_END), np.float32)
    c[:, C_ID:C_ID + 128] = np.eye(128)
    p, f = np.arange(128)[:, None], np.arange(128)[None, :]
    c[:, C_CM:C_CM + 128] = f > p
    c[:, C_MC:C_MC + 128] = np.where(f > p, NEG, 0.0)
    row = np.arange(128)
    bi, a, i, t = row // 32, row // 16 % 2, row // 4 % 4, row % 4
    ys = np.arange(NS)
    yt, yb = ys // NB, ys % NB
    for r in range(2):
        same = (yt[:, None] == t[None]) & (yb[:, None] == 4 * r + bi[None])
        c[0:NS, C_EX + 128 * r:C_EX + 128 * r + 128] = same
        c[:, C_MW + NS * r:C_MW + NS * r + NS] = same.T
    c[0:NH, C_OH:C_OH + 128] = np.arange(NH)[:, None] == (2 * i + a)[None]
    c[0:NS, C_MS:C_MS + NS] = np.where((yb[None] == yb[:, None]) & (yt[None] <= yt[:, None]), 0.0, NEG)
    tk = np.arange(128)
    kt, kb = tk // 32, tk % 32
    past = PAST + kt[:, None] - np.arange(PAST)[None]
    new = kt[:, None] - yt[None]
    c[:, C_TK:C_TK + PAST + NS] = _bucket(np.concatenate([past, new], 1)) == kb[:, None]
    c[:, C_MT:C_MT + 128] = kt[:, None] == t[None]
    c[:, C_TI:C_TI + TT] = np.arange(128)[:, None] + 128 * np.arange(TT)[None]
    c[:, C_E1:C_E1 + NE] = ORD * np.arange(NE)
    c[:, C_EC:C_EC + NE] = CAP * np.arange(NE)
    c[0:32, C_OF:C_OF + BW] = np.arange(32)[:, None] == _bucket(SEQ - 1 - np.arange(BW))[None]
    return c


def _tokens(prompt, sample):
    import numpy as np
    f = prompt.shape[-1]
    a = np.concatenate([prompt.reshape(NC, CH, f).transpose(1, 0, 2).reshape(SEQ, f),
                        sample.transpose(1, 0, 2).reshape(NS, f)], 0)
    return np.ascontiguousarray(a.T.reshape(f // 128, 128, T).transpose(1, 0, 2))


def _tiles(w):
    k, m = w.shape
    return w.reshape(k // 128, 128, m // 128, 128).transpose(2, 1, 0, 3).reshape(m // 128, 128, k)


def _vec(v):
    return v.reshape(-1, 128).T


_OUTS = {"o_y": (128, KC, T), "o_k": (L, 128, T), "o_v": (L, 128, NQT + 1, 128), "o_ki": (L, 64, T),
         "o_h": (L, 2, 128, 2 * HP * (NB + 1))}


def _layout(a):
    import numpy as np
    o = {}
    o["x_t"] = _tokens(a["x_prompt"][0], a["x_sample"])
    o["p_t"] = np.stack([_tokens(a["p_prompt"][l, 0], a["p_sample"][l]) for l in range(L)])
    ln = [a["ln_emb_g"], a["ln_emb_b"]]
    for l in range(L):
        ln += [a["ln1_g"][l], a["ln1_b"][l], a["ln2_g"][l], a["ln2_b"][l]]
    o["ln_p"] = np.stack([_vec(v) for v in ln], 1)
    o["d_t"] = np.stack([_vec(a["ssm_d"][l]) for l in range(L)], 1)
    o["w_router_t"] = a["moe_w_router"][0].reshape(KC, 128, NE).transpose(1, 0, 2)
    o["b_router_t"] = np.broadcast_to(a["moe_b_router"][0][None], (128, NE))
    o["pages"] = a["page_table"].reshape(1, -1)
    o["rel_rows"] = np.broadcast_to(a["rel_bias"][:, :, None], (32, NH, 128))
    row = np.arange(128)
    o["rel_tk"] = np.tile(a["rel_bias"][:, 4 * (row // 16 % 2) + row // 4 % 4], (4, 1))
    win, wv, glu, wo, ple, ssm = [], [], [], [], [], []
    qcols = np.concatenate([np.arange(64) + 64 * h for i in range(4) for h in (i, i + 4)])
    rows = np.concatenate([np.arange(512), 512 + qcols])
    for l in range(L):
        w = a["w_in"][l]
        cols = np.concatenate([np.arange(512), 512 + qcols, 1280 + np.arange(512), 1024 + np.arange(128),
                               1792 + np.arange(64), 1792 + np.arange(64)])
        win.append(_tiles(w[:, cols]))
        vc = np.concatenate([1152 + np.arange(128), 1856 + np.arange(8)])
        wv.append(w[:, vc].reshape(KC, 128, 136).transpose(1, 0, 2).reshape(128, KC * 136))
        gt = _tiles(a["ssm_w_glu"][l])
        glu.append(gt[[0, 4, 1, 5, 2, 6, 3, 7]])
        wo.append(_tiles(a["w_out"][l][rows]))
        ple.append(np.concatenate([_tiles(a["ple_w_gate"][l]), _tiles(a["ple_w_proj"][l])], 2))
        halves_ = []
        for hf in range(2):
            g = slice(HG * hf, HG * hf + HG)
            st = lambda v: v.reshape(HP, 2 * SN, -1).transpose(1, 2, 0)
            parts = [st(a["ssm_a_re"][l, g]), st(a["ssm_a_im"][l, g]),
                     st(np.broadcast_to(a["ssm_log_dt"][l, g][:, None], (HG, SN))),
                     st(a["ssm_b_re"][l, g]), st(a["ssm_b_im"][l, g]),
                     st(a["ssm_c_re"][l, g].transpose(0, 2, 1)), st(a["ssm_c_im"][l, g].transpose(0, 2, 1)),
                     st(a["state_ssm_re"][l][:, g].transpose(1, 2, 0)), st(a["state_ssm_im"][l][:, g].transpose(1, 2, 0))]
            halves_.append(np.concatenate(parts, 1).reshape(128, -1))
        ssm.append(np.stack(halves_))
    o["w_in_t"], o["w_v_t"], o["w_glu_t"], o["w_out_t"], o["w_ple_t"], o["ssm_t"] = map(np.stack, (win, wv, glu, wo, ple, ssm))
    gu, dn = [], []

    def block(g, u_, d):
        gu.append(np.stack([_tiles(g), _tiles(u_)], 1).reshape(2 * FT, 128, DM))
        dn.append(_tiles(d))

    for i in range(2):
        s = slice(FE * i, FE * i + FE)
        block(a["ffn_w_gate"][0][:, s], a["ffn_w_up"][0][:, s], a["ffn_w_down"][0][s])
    for e in range(NE):
        block(a["moe_w_gate"][0, e], a["moe_w_up"][0, e], a["moe_w_down"][0, e])
    o["w_gu_t"], o["w_dn_t"] = np.stack(gu), np.stack(dn)
    o["c_k"] = a["cache_k"].reshape(L, NPOOL, PAGE, 128).transpose(0, 1, 3, 2)
    o["c_v"] = a["cache_v"].reshape(L, NPOOL, PAGE, 128)
    o["c_i"] = np.tile(a["cache_kidx"].transpose(0, 1, 3, 2), (1, 1, 2, 1))
    o["consts"] = _consts()
    return {k: np.ascontiguousarray(v) for k, v in o.items()}


def _split(t):
    return t[:, :SEQ].T, t[:, SEQ:].T.reshape(DT, NB, -1).transpose(1, 0, 2)


def kernel(**inputs):
    import numpy as np
    import concourse.bacc as bacc
    from concourse.bass_utils import run_bass_kernel_spmd

    arrays = _layout({k: np.asarray(v) for k, v in inputs.items()})
    nc = bacc.Bacc("TRN2", target_bir_lowering=False, num_devices=1)
    io = {k: nc.dram_tensor(k, v.shape, mybir.dt.from_np(v.dtype), kind="ExternalInput").ap() for k, v in arrays.items()}
    io.update({k: nc.dram_tensor(k, s, mybir.dt.float32, kind="ExternalOutput").ap() for k, s in _OUTS.items()})
    build(nc, io)
    res = run_bass_kernel_spmd(nc, [arrays], core_ids=[0]).results[0]
    y = np.asarray(res["o_y"]).transpose(1, 0, 2).reshape(DM, T)
    xp = y[:, :SEQ].reshape(DM, CH, NC).transpose(2, 1, 0).reshape(1, SEQ, DM)
    xs = y[:, SEQ:].T.reshape(DT, NB, DM).transpose(1, 0, 2)
    k = [_split(np.asarray(res["o_k"])[l]) for l in range(L)]
    ki = [_split(np.asarray(res["o_ki"])[l]) for l in range(L)]
    v = np.asarray(res["o_v"])
    vp = v[:, :, :NQT, :].transpose(0, 2, 1, 3).reshape(L, 1, SEQ, 2, HD)
    vs = v[:, :NS, NQT, :].reshape(L, DT, NB, 2, HD).transpose(0, 2, 1, 3, 4)
    h = np.asarray(res["o_h"]).reshape(L, 2, 2, SN, 2, HP, NB + 1)
    h = h.transpose(4, 0, 6, 1, 5, 2, 3).reshape(2, L, NB + 1, G, SN)
    c = np.ascontiguousarray
    return (c(xp), c(xs),
            np.stack([t[0] for t in k]).reshape(L, 1, SEQ, 2, HD), c(vp), np.stack([t[0] for t in ki])[:, None],
            c(h[0][:, :1]), c(h[1][:, :1]),
            np.stack([t[1] for t in k]).reshape(L, NB, DT, 2, HD), c(vs), np.stack([t[1] for t in ki]),
            c(h[0][:, 1:]), c(h[1][:, 1:]))
```

```python
import math

import concourse.bass as bass
from concourse import mybir
from contextlib import ExitStack

DM, SEQ, L, NB, DT, PAST, PAGE = 1024, 512, 2, 8, 4, 512, 128
NS = NB * DT
T = SEQ + NS
KC = DM // 128
CH = 8
NC = SEQ // CH
G, GC, SN = 32, 16, 64
HG = G // 2
HP = HG // 2
CW = NB + NC
NH, HD = 8, 64
NQT = SEQ // 128
TOPK_P = min(256, SEQ // 4)
TOPK_S = min(256, (PAST + DT) // 4)
NPG = PAST // PAGE
NPOOL = NB * NPG + (NB * NPG + 3) // 4
FE, NE = 1408, 8
FT = FE // 128
ALPHA = (2 * L) ** 0.25
LN_EPS = 1e-5
IDX_SCALE = (64 ** -0.5) * (8 ** -0.5)
NEG = -1e30
GONE = -3.0e38
RING = 6
SLOT = FT * 128
BLOCK_JOBS = 2 * FT + KC
WIN_T = 15
PAR_F = 3 + 4 * GC + 2 * NB
BW = SEQ + 128

C_ID, C_CM, C_MC, C_EX, C_MW, C_OH, C_MS, C_TK, C_MT, C_OF = 0, 128, 256, 384, 640, 704, 832, 864, 1408, 1536
C_TI = C_OF + BW
C_E1, C_EC = C_TI + 5, C_TI + 13
C_END = C_TI + 21
CAP = 176
ORD = 1024
TT = 5
XROWS = (NE + 1) * CAP


def build(nc, io):
    fp32, i32 = mybir.dt.float32, mybir.dt.int32
    ALU, ACT, AX = mybir.AluOpType, mybir.ActivationFunctionType, mybir.AxisListType
    ctx = ExitStack()
    with ctx:
        def sb(name, shape, dt=fp32):
            return ctx.enter_context(nc.sbuf_tensor(name, shape, dt))

        def sem(name):
            return ctx.enter_context(nc.semaphore(name))

        x = sb("x_res", [128, KC, T])
        acc = sb("acc", [128, KC, T])
        cat = sb("cat", [128, KC, T])
        ring = sb("ring", [128, RING, SLOT])
        rbias = sb("rbias", [128, NH, SEQ])
        cst = sb("cst", [128, C_END])
        bs = sb("bs", [128, PAST + NS])
        lnp = sb("lnp", [128, 2 + 4 * L, KC])
        dsk = sb("dsk", [128, L, 4])
        wrt = sb("wrt", [128, KC, NE])
        brt = sb("brt", [128, NE])
        ones = sb("ones", [128, 128])
        eps = sb("eps", [128, 1])
        ptab = sb("ptab", [1, NB * NPG], i32)
        q = sb("q", [128, 4, T])
        kn = sb("kn", [128, T])
        kin = sb("kin", [128, T])
        vn = sb("vn", [128, T])
        wn = sb("wn", [NH, T])
        vtok = sb("vtok", [128, NQT + 1, 128])
        wtok = sb("wtok", [128, NQT, NH])
        sg = sb("sg", [128, 2, T])
        m8x = sb("mark", [128, 1])
        ph = sb("phase", [128, 18340])
        idx = sb("idx", [128, 4 * TT], i32)
        flag = sb("flag", [1, 1], i32)
        u = acc[:, 0:4, :]
        qi = acc[:, 4:8, :]
        ident = cst[:, C_ID:C_ID + 128]

        class Cut:
            def __init__(self, t, at=0):
                self.t, self.at = t, at

            def __call__(self, n, rows=128, lo=0):
                self.at += n
                return self.t[lo:lo + rows, self.at - n:self.at]

        cut = Cut(ph)
        U = cut(G * CW).rearrange("p (g c) -> p g c", g=G)
        U2 = cut(G * NB).rearrange("p (g b) -> p g b", g=G)
        par_at = cut.at
        par = cut(HP * PAR_F).rearrange("p (f e) -> p f e", e=HP)
        pB = par[:, 3:3 + 4 * GC, :].rearrange("p (k c) e -> p k e c", k=4)
        pH = par[:, 3 + 4 * GC:, :].rearrange("p (k b) e -> p k e b", k=2)
        toep = cut(HG * 128).rearrange("p (g n) -> p g n", g=HG)
        BT = cut(2 * HP * 128).rearrange("p (k e n) -> p k e n", k=2, e=HP)
        CP = [cut(HP * (CH + 1) * GC).rearrange("p (e m c) -> p e m c", e=HP, c=GC) for _ in range(2)]
        BP = [cut(HP * CH * GC).rearrange("p (e m c) -> p e m c", e=HP, c=GC) for _ in range(2)]
        Bb = [cut(HP * GC).rearrange("p (e c) -> p e c", e=HP) for _ in range(2)]
        E = [cut(HP * NC).rearrange("p (e c) -> p e c", e=HP) for _ in range(2)]
        GM = [cut(HP * NC).rearrange("p (e c) -> p e c", e=HP) for _ in range(2)]
        GS = [cut(HP * NC).rearrange("p (e c) -> p e c", e=HP) for _ in range(2)]
        HW_ = NB + NC + 1
        H = [cut(HP * HW_).rearrange("p (e c) -> p e c", e=HP) for _ in range(2)]
        R8 = cut(HP * NC).rearrange("p (e c) -> p e c", e=HP)
        Y = cut(HG * CW).rearrange("p (g c) -> p g c", g=HG)
        hout = cut(2 * HP * (NB + 1)).rearrange("p (k e b) -> p k e b", k=2, e=HP)
        P = [cut((CH + 1) * HP).rearrange("p (m e) -> p m e", e=HP) for _ in range(2)]
        sm = cut(24 * HP).rearrange("p (n e) -> p n e", e=HP)
        cf = cat[:, :, :].rearrange("p k t -> p (k t)")
        Kd = cf[0:GC, 0:HG * 128].rearrange("p (g n) -> p g n", g=HG)
        T1 = cf[:, 2048:2048 + 1152]
        T2 = cf[:, 3200:3200 + 1152]
        cut = Cut(ph)
        pgK = cut(16 * PAGE).rearrange("p (n c) -> p n c", n=16)
        pgV = cut(16 * PAGE).rearrange("p (n c) -> p n c", n=16)
        pgI = cut(16 * PAGE).rearrange("p (n c) -> p n c", n=16)
        shared = cut.at
        rl = cut(4 * SEQ).rearrange("p (n c) -> p n c", n=4)
        sc = cut(SEQ)
        wk = cut(SEQ)
        nosel = cut(SEQ)
        Lg = cut(NH * SEQ).rearrange("p (h c) -> p h c", h=NH)
        PT = cut(2 * NQT * 512).rearrange("p (g k c) -> p g k c", g=2, k=NQT)
        m8 = cut(8)
        nmx = cut(NH)
        sums = cut(NH)
        rs = cut(NH)
        negid = cut(128)
        pgs = {0: (pgK, pgV, pgI)}
        two = PT.rearrange("p g k c -> p (g k c)").rearrange("p (z n c) -> p z n c", z=2, n=16)
        pgs[1] = (two[:, 0], two[:, 1], cf[:, 0:16 * PAGE].rearrange("p (n c) -> p n c", n=16))
        cut = Cut(ph, shared)
        Qzi = cut(256).rearrange("p (b a i t) -> p b a i t", b=NB, a=2, i=4)
        Qz = cut(256).rearrange("p (b a i t) -> p b a i t", b=NB, a=2, i=4)
        SK = PAST + NS
        rls = cut(SK)
        wr = cut(2 * NS).rearrange("p (r y) -> p r y", r=2)
        scs = cut(SK)
        wks = cut(SK + 7)
        nss = cut(SK)
        nms = [cut(4) for _ in range(2)]
        Ls = [cut(SK) for _ in range(2)]
        PTs = [cut(5 * 128).rearrange("p (k c) -> p k c", k=5) for _ in range(2)]
        cut = Cut(ph)
        hid = cut(FT * T).rearrange("p (f t) -> p f t", f=FT)
        gb = cut(NE * T).rearrange("p (e t) -> p e t", e=NE)
        pt = cut(2 * T).rearrange("p (k t) -> p k t", k=2)
        rlog = cut(5 * NE).rearrange("p (n e) -> p n e", n=5)
        rtop = cut(5 * NE).rearrange("p (n e) -> p n e", n=5)
        rtwo = cut(5 * NE).rearrange("p (n e) -> p n e", n=5)
        rwk = cut(5 * 14).rearrange("p (n e) -> p n e", n=5)
        gts = cut(5 * NE).rearrange("p (n e) -> p n e", n=5)
        rsm = cut(5 * 4).rearrange("p (n e) -> p n e", n=5)
        rst = cut(T)
        ygt = cut(2 * DM).rearrange("p (c d) -> p c d", c=2)
        xgt = cut(2 * DM).rearrange("p (c d) -> p c d", c=2)
        zt = ygt[:, 0, :]
        one = cut(128)
        small = lambda n: cut(TT * n).rearrange("p (t n) -> p t n", t=TT)
        sel, rank, order, tmp8 = small(NE), small(NE), small(NE), small(NE)
        over = small(NE)
        v01, r01, b01, g01, ok01, ix01 = (small(2) for _ in range(6))
        ovs = cut(1)
        cut = Cut(ph)
        xtok = cut(TT * DM).rearrange("p (t d) -> p t d", t=TT)
        gt1_at = cut.at
        xg = cut(KC * CAP).rearrange("p (k c) -> p k c", k=KC)
        hidg = cut(FT * CAP).rearrange("p (f c) -> p f c", f=FT)
        yT = cut(KC * CAP).rearrange("p (k c) -> p k c", k=KC)
        gt = [xtok, ph[:, gt1_at:gt1_at + TT * DM].rearrange("p (t d) -> p t d", t=TT)]
        cut = Cut(ph)
        relb = cut(NH * 128).rearrange("p (h n) -> p h n", h=NH)
        reltk = cut(128)
        frow = cut(NH * BW).rearrange("p (h n) -> p h n", h=NH)
        NXZ = (XROWS + 127) // 128

        pair = [ctx.enter_context(nc.psum_tensor(f"pair{i}", [128, 1024], fp32)) for i in range(4)]

        def bank(i):
            return pair[i // 2][:, 512 * (i % 2):512 * (i % 2) + 512]

        def even(i):
            return pair[i][:, :].rearrange("p (h c) -> p h c", h=2)[:, :, 0:T // 2]

        udram = nc.dram_tensor("u_scratch", (4 * 128, T), fp32, kind="Internal")
        ydram = nc.dram_tensor("y_scratch", (4 * 128, T), fp32, kind="Internal")
        fdram = nc.dram_tensor("f_scratch", (NH, 128, BW), fp32, kind="Internal")

        xs = nc.dram_tensor("gathered_x", (XROWS + 2 * TT * 128, DM), fp32, kind="Internal")
        ys = nc.dram_tensor("gathered_y", (NE * CAP, DM), fp32, kind="Internal")

        w_loaded = [sem(f"w_loaded{i}") for i in range(RING)]
        jobs_begun = sem("jobs_begun")
        filled = [sem(f"filled{i}") for i in range(4)]
        emptied = [sem(f"emptied{i}") for i in range(4)]
        dve_step, act_step, pool_step = sem("dve_step"), sem("act_step"), sem("pool_step")
        consts_in, rel_in, ln_in = sem("consts_in"), sem("rel_in"), sem("ln_in")
        x_in = [sem(f"x_in{kc}") for kc in range(KC)]
        ones_set = sem("ones_set")
        f_mm, f_ready, f_out, rbias_in = sem("f_mm"), sem("f_ready"), sem("f_out"), sem("rbias_in")
        tk_ready, bs_mm, bs_ready = sem("tk_ready"), sem("bs_mm"), sem("bs_ready")
        acc_ready, squares, x_ready = sem("acc_ready"), sem("squares"), sem("x_ready")
        summed = sem("summed")
        rst_ready, centred, scaled = sem("rstd_ready"), sem("centred"), sem("scaled")
        u_out, u_zero, u_in = sem("u_out"), sem("u_zero"), sem("u_in")
        par_in, ldt, expd, theta, sincos = sem("par_in"), sem("dt_exp"), sem("radii"), sem("theta"), sem("sincos")
        bp_ready, cp_ready, bt_mm, bt_ready = sem("bp_ready"), sem("cp_ready"), sem("bt_mm"), sem("bt_ready")
        toep_zero, kd_mm, kd_ready, toep_in = sem("toep_zero"), sem("kd_mm"), sem("kd_ready"), sem("toep_in")
        hout_ready = sem("hout_ready")
        g_mm, h_ready, y_mm, y_ready = sem("g_mm"), sem("h_ready"), sem("y_mm"), sem("y_ready")
        y_out, y_in, yd_ready, gelu_ready = sem("y_out"), sem("y_in"), sem("yd_ready"), sem("gelu_ready")
        tok_mm, tok_ready = sem("tok_mm"), sem("tok_ready")
        idx_mm, relu_ready, relu_used = sem("idx_mm"), sem("relu_ready"), sem("relu_used")
        lg_mm, lg_used, nmx_ready, exp_ready = sem("lg_mm"), sem("lg_used"), sem("nmx_ready"), sem("exp_ready")
        rs_ready, prob_ready = sem("rs_ready"), sem("prob_ready")
        pt_mm, pt_ready, pv_mm, pv_ready = sem("pt_mm"), sem("pt_ready"), sem("pv_mm"), sem("pv_ready")
        pages_kv = [sem("pages_kv0"), sem("pages_kv1")]
        pages_in = [sem("index_pages0"), sem("index_pages1")]
        hide_ready = sem("hide_ready")
        qz_ready, wr_mm, wr_ready = sem("qz_ready"), sem("wr_mm"), sem("wr_ready")
        si_mm, srelu, sc_mm, nosel_ready = sem("si_mm"), sem("srelu"), sem("sc_mm"), sem("nosel_ready")
        scs_ready = sem("scs_ready")
        sl_mm, snmx, sexp, sprob = sem("sl_mm"), sem("snmx"), sem("sexp"), sem("sprob")
        spt_mm, spt_ready, spv_mm, spv_ready = sem("spt_mm"), sem("spt_ready"), sem("spv_mm"), sem("spv_ready")
        pt_in, r_mm, gts_ready, gb_mm, gb_ready = sem("p_in"), sem("r_mm"), sem("gts_ready"), sem("gb_mm"), sem("gb_ready")
        ple_used = sem("ple_used")
        gdiff, gexp = sem("gate_diff"), sem("gate_exp")
        hid_ready = sem("hid_ready")
        zero_set, xs_zero = sem("zero_set"), sem("xs_zero")
        xt_mm, xt_ready, sel_ready, rank_mm = sem("xt_mm"), sem("xt_ready"), sem("sel_ready"), sem("rank_mm")
        one_set, idx_ready, scattered, ov_ready = sem("one_set"), sem("idx_ready"), sem("scattered"), sem("ov_ready")
        flag_mm, flag_ready = sem("flag_mm"), sem("flag_ready")
        xg_in, silu_ready, y_free, ys_out = sem("xg_in"), sem("silu_ready"), sem("y_free"), sem("ys_out")
        gt_in = [[sem(f"gt_in{k}_{tt}") for tt in range(TT)] for k in range(2)]
        gt_scaled, comb_ready = sem("gt_scaled"), sem("comb_ready")
        last_filled = [sem("last_filled0"), sem("last_filled1")]
        last_emptied = [sem("last_emptied0"), sem("last_emptied1")]
        stored, y_stored = sem("stored"), sem("y_stored")

        class Count:
            def __init__(self):
                self.n = [0] * 4

            def take(self, s):
                self.n[s] += 1
                return self.n[s]

        def experts(l):
            return 2 if l == 0 else NE

        def first_block(l):
            return 0 if l == 0 else 2

        LAYER_JOBS = WIN_T + 8 + 8 + 8
        JOBS = [0, LAYER_JOBS + BLOCK_JOBS * experts(0)]
        FFN_USES = [8, 8, 7, 7]

        def ffn_plan():
            seen = [0] * 4
            steps = [("up", f, (0, 1) if f % 2 == 0 else (2, 3)) for f in range(FT)]
            steps += [("down", m, ((2 + m) % 4,)) for m in range(KC)]
            for kind, i, ps in steps:
                yield kind, i, [(s, seen[s]) for s in ps]
                for s in ps:
                    seen[s] += 1

        def moe_plan():
            seen = [0] * 4
            steps = [("up", f, f % 4) for f in range(FT)] + [("down", i, (3, 0, 1, 2)[i]) for i in range(4)]
            steps += [("xg", 0, 3), ("xg", 1, 0), ("yg", 0, 1), ("yg", 1, 2)]
            for kind, i, s in steps:
                yield kind, i, s, seen[s]
                seen[s] += 1

        MOE_USES = [5, 5, 5, 4]
        C_ROWS = (128, CAP - 128)

        def banks(s, n):
            return pair[s][:, :].rearrange("p (h c) -> p h c", h=2)[:, :, 0:n]

        def uses_before(l, s):
            n = int(s < 2)
            for k in range(l):
                n += 12 + 2 * int(s < 2) + FFN_USES[s] * experts(k)
            return n

        def halves(t):
            return t.rearrange("p (h c) -> p h c", h=2)

        def bc(t, axis, n):
            t = t.unsqueeze(axis)
            shape = list(t.shape)
            shape[axis] = n
            return t.to_broadcast(shape)

        block = ctx.enter_context(nc.Block())

        @block.sync
        def _(sp):
            for kc in range(KC):
                sp.dma_start(x[:, kc, :], io["x_t"][:, kc, :]).then_inc(x_in[kc], 16)
            sp.dma_start(lnp[:, :, :], io["ln_p"]).then_inc(ln_in, 16)

            def load(n, cols, src):
                if n >= RING:
                    sp.wait_ge(jobs_begun, n - RING + 2)
                sp.dma_start(ring[:, n % RING, 0:cols], src).then_inc(w_loaded[n % RING], 16)

            for l in range(L):
                n = JOBS[l]
                for m in range(WIN_T - 1):
                    load(n + m, 1024, io["w_in_t"][l, m])
                load(n + WIN_T - 1, KC * 136, io["w_v_t"][l])
                n += WIN_T
                for m in range(8):
                    load(n + m, 512, io["w_glu_t"][l, m])
                for m in range(8):
                    load(n + 8 + m, 1024, io["w_out_t"][l, m])
                for m in range(8):
                    load(n + 16 + m, 1280, io["w_ple_t"][l, m])
                n += 24
                def blocks(n, first, count):
                    with sp.Fori(0, count) as e:
                        blk = e + first
                        for k in range(BLOCK_JOBS):
                            sp.wait_ge(jobs_begun, e * BLOCK_JOBS + (n + k - RING + 2))
                            if k < 2 * FT:
                                src, cols = io["w_gu_t"][bass.ds(blk, 1), k, :, :], 1024
                            else:
                                src, cols = io["w_dn_t"][bass.ds(blk, 1), k - 2 * FT, :, :], SLOT
                            sp.dma_start(ring[:, (n + k) % RING, 0:cols],
                                         src.rearrange("o p c -> p (o c)")).then_inc(w_loaded[(n + k) % RING], 16)

                blocks(n, first_block(l), experts(l))
                if l == 1:
                    sp.wait_ge(flag_ready, 1)
                    left = sp.value_load(flag[0:1, 0:1], min_val=0, max_val=2 * T)
                    with sp.If(left > 0):
                        blocks(n + BLOCK_JOBS * NE, first_block(l), NE)
            for kc in range(KC):
                sp.wait_ge(x_ready, KC * 2 * L + kc + 1)
                sp.dma_start(io["o_y"][:, kc, :], x[:, kc, :]).then_inc(y_stored, 16)
            sp.wait_ge(y_stored, 16 * KC)

        @block.gpsimd
        def _(pool):
            nc.gpsimd.memset(ones[:, :], 1.0 / DM).then_inc(ones_set, 1)
            nc.gpsimd.memset(eps[:, :], LN_EPS).then_inc(ones_set, 1)
            pool.wait_ge(x_in[KC - 3], 16)
            pool.dma_start(cst[:, :], io["consts"]).then_inc(consts_in, 16)
            pool.dma_start(dsk[:, :, :], io["d_t"]).then_inc(consts_in, 16)
            pool.dma_start(wrt[:, :, :], io["w_router_t"]).then_inc(consts_in, 16)
            pool.dma_start(brt[:, :], io["b_router_t"]).then_inc(consts_in, 16)
            pool.dma_start(ptab[:, :], io["pages"]).then_inc(consts_in, 16)
            pool.dma_start(relb[0:32, :, :], io["rel_rows"]).then_inc(rel_in, 16)
            pool.dma_start(reltk, io["rel_tk"]).then_inc(rel_in, 16)
            pool.wait_ge(f_ready, NH)
            pool.dma_start(fdram.ap().rearrange("h p n -> p h n"), frow[:, :, :]).then_inc(f_out, 16)
            pool.wait_ge(f_out, 16)
            pool.dma_start(rbias[:, :, :], bass.AP(fdram, 127, [[BW - 1, 128], [128 * BW, NH], [1, SEQ]])).then_inc(rbias_in, 16)
            pool.wait_ge(consts_in, 16 * 5)
            for l in range(L):
                pool.wait_ge(x_ready, KC * (1 + 2 * l))
                if l:
                    pool.wait_ge(xs_zero, 16 * NXZ)
                pool.dma_start(ph[:, par_at:par_at + HP * PAR_F], io["ssm_t"][l, 0]).then_inc(par_in, 16)
                for s in range(4):
                    pool.wait_ge(emptied[s], uses_before(l, s) + 1)
                pool.dma_start(udram.ap().rearrange("(k p) c -> p k c", p=128), u).then_inc(u_out, 16)
                nc.gpsimd.memset(U[0:64, :, 0:NB], 0.0).then_inc(u_zero, 1)
                pool.wait_ge(u_out, 16 * (l + 1))
                uv = udram.ap().rearrange("(g h) c -> h g c", h=GC)
                for r in range(CH):
                    j = CH - 1 - r
                    rows = slice(GC * r, GC * r + GC)
                    pool.dma_start(U[rows, :, NB:CW], uv[:, :, NC * j:NC * j + NC]).then_inc(u_in, 16)
                    if j < DT:
                        pool.dma_start(U[rows, :, 0:NB], uv[:, :, SEQ + NB * j:SEQ + NB * j + NB]).then_inc(u_in, 16)
                    else:
                        jj = j - DT
                        pool.dma_start(U2[rows, :, :], uv[:, :, SEQ + NB * jj:SEQ + NB * jj + NB]).then_inc(u_in, 16)
                nc.gpsimd.memset(toep[:, :, :], 0.0).then_inc(toep_zero, 1)
                for hf in range(2):
                    v = 2 * l + hf
                    pool.wait_ge(kd_ready, v + 1)
                    pool.wait_ge(toep_zero, v + 1)
                    for s in range(CH):
                        r = CH - 1 - s
                        pool.dma_start(toep[GC * r:GC * r + GC, :, GC * s:128],
                                       Kd[:, :, 0:128 - GC * s]).then_inc(toep_in, 16)
                    pool.wait_ge(hout_ready, v + 1)
                    if hf == 0:
                        pool.dma_start(ph[:, par_at:par_at + HP * PAR_F], io["ssm_t"][l, 1]).then_inc(par_in, 16)
                    pool.dma_start(io["o_h"][l, hf], hout[:, :, :, :].rearrange("p k e b -> p (k e b)")).then_inc(stored, 16)
                    pool.wait_ge(y_ready, v + 1)
                    if hf == 0:
                        nc.gpsimd.memset(toep[:, :, :], 0.0).then_inc(toep_zero, 1)
                    yv = ydram.ap().rearrange("(g h) c -> h g c", h=GC)[:, HG * hf:HG * hf + HG, :]
                    for t in range(CH):
                        rows = slice(GC * t, GC * t + GC)
                        pool.dma_start(yv[:, :, NC * t:NC * t + NC], Y[rows, :, NB:CW]).then_inc(y_out, 16)
                        if t < DT:
                            pool.dma_start(yv[:, :, SEQ + NB * t:SEQ + NB * t + NB], Y[rows, :, 0:NB]).then_inc(y_out, 16)
                pool.wait_ge(y_out, 16 * 12 * 2 * (l + 1))
                pool.dma_start(cat[:, 0:4, :], ydram.ap().rearrange("(k p) c -> p k c", p=128)).then_inc(y_in, 16)
                def load_pages(r, kinds, done):
                    with pool.Fori(0, 16) as i:
                        pg = pool.value_load(ptab[0:1, bass.ds(i + 16 * r, 1)], min_val=0, max_val=NPOOL - 1)
                        for dst, src in kinds:
                            pool.dma_start(dst[:, bass.ds(i, 1), :],
                                           src[l, bass.ds(pg, 1), :, :].rearrange("o p c -> p o c")).then_inc(done, 16)

                load_pages(0, ((pgs[0][2], io["c_i"]),), pages_in[0])
                load_pages(0, ((pgs[0][0], io["c_k"]), (pgs[0][1], io["c_v"])), pages_kv[0])
                pool.wait_ge(yd_ready, l + 1)
                load_pages(1, ((pgs[1][2], io["c_i"]),), pages_in[1])
                pool.wait_ge(tok_ready, 2 * l + 2)
                pool.dma_start(io["o_k"][l], kn[:, :]).then_inc(stored, 16)
                pool.dma_start(io["o_v"][l, :, 0:NQT, :], vtok[:, 0:NQT, :]).then_inc(stored, 16)
                pool.dma_start(io["o_v"][l, 0:NS, NQT, :], vtok[0:NS, NQT, :]).then_inc(stored, 16)
                pool.dma_start(io["o_ki"][l], kin[0:64, :]).then_inc(stored, 16)
                pool.wait_ge(pv_ready, NQT * (l + 1))
                load_pages(1, ((pgs[1][0], io["c_k"]), (pgs[1][1], io["c_v"])), pages_kv[1])
                pool.wait_ge(spv_ready, 2 * l + 2)
                pool.dma_start(pt[:, :, :], io["p_t"][l]).then_inc(pt_in, 16)
                if l == 0:
                    nc.gpsimd.memset(zt, 0.0).then_inc(zero_set, 1)
                    pool.wait_ge(zero_set, 1)
                    for i in range(NXZ):
                        rows = min(128, XROWS - 128 * i)
                        pool.dma_start(xs.ap()[128 * i:128 * i + rows, :], zt[0:rows, :]).then_inc(xs_zero, 16)
            nc.gpsimd.memset(one[:, :], 1.0).then_inc(one_set, 1)
            pool.wait_ge(xt_ready, TT)
            pool.wait_ge(idx_ready, 1)
            for tt in range(TT):
                rows = 128 if tt < 4 else NS
                for k in range(2):
                    pool.indirect_dma_start(xs.ap(), bass.IndirectOffsetOnAxis(ap=idx[0:rows, 2 * tt + k:2 * tt + k + 1].bitcast(mybir.dt.uint32), axis=0),
                                            xtok[0:rows, tt, :], None).then_inc(scattered, 16)
            pool.wait_ge(scattered, 16 * 2 * TT)

            def load_rows(e):
                src = xs.ap()[0:XROWS, :].rearrange("(e c) d -> e c d", c=CAP)[bass.ds(e, 1), :, :]
                pool.dma_start(xgt[:, 0, :], src[:, 0:128, :].rearrange("o c d -> c (o d)")).then_inc(xg_in, 16)
                pool.dma_start(xgt[0:C_ROWS[1], 1, :], src[:, 128:CAP, :].rearrange("o c d -> c (o d)")).then_inc(xg_in, 16)

            load_rows(0)
            pool.sem_inc(y_free, 1)
            base = [uses_before(1, s) + 12 + int(s < 2) + int(s in (0, 3)) for s in range(4)]

            def fetch(k):
                for tt in range(TT):
                    rows = 128 if tt < 4 else NS
                    col = 2 * TT + 2 * tt + k
                    src = ys.ap()[0:(NE - 1 + k) * CAP, :]
                    pool.indirect_dma_start(gt[k][0:rows, tt, :], None, src,
                                            bass.IndirectOffsetOnAxis(ap=idx[0:rows, col:col + 1].bitcast(mybir.dt.uint32), axis=0)).then_inc(gt_in[k][tt], 16)

            def rows_in_and_out(e, last=False):
                pool.wait_ge(filled[0], e * MOE_USES[0] + base[0])
                load_rows(e + 1)
                if last:
                    fetch(0)
                for s in (1, 2):
                    pool.wait_ge(emptied[s], e * MOE_USES[s] + (base[s] + MOE_USES[s]))
                dst = ys.ap().rearrange("(e c) d -> e c d", c=CAP)[bass.ds(e, 1), :, :]
                pool.dma_start(dst[:, 0:128, :].rearrange("o c d -> c (o d)"), ygt[:, 0, :]).then_inc(ys_out, 16)
                pool.dma_start(dst[:, 128:CAP, :].rearrange("o c d -> c (o d)"), ygt[0:C_ROWS[1], 1, :]).then_inc(ys_out, 16)
                pool.wait_ge(ys_out, e * 32 + 32)

            with pool.Fori(0, NE - 1) as e:
                rows_in_and_out(e)
                pool.sem_inc(y_free, 1)
            rows_in_and_out(NE - 1, last=True)
            fetch(1)
            pool.wait_ge(stored, 16 * 6 * L)

        @block.tensor
        def _(pe):
            mm = nc.tensor.matmul
            c = Count()

            def begin(s):
                n = c.take(s)
                if n > 1:
                    pe.wait_ge(emptied[s], n - 1)
                return n

            def all_empty():
                for s in range(4):
                    if c.n[s]:
                        pe.wait_ge(emptied[s], c.n[s])

            def product(s, w, kcs, rhs, split, rows=128, note=None, norm=None):
                for half, (a, b) in enumerate(((0, split), (split, T))):
                    for i, kc in enumerate(kcs):
                        if norm is not None and half == 0:
                            pe.wait_ge(x_ready, KC * norm + kc + 1)
                        last = mm(pair[s][0:rows, 512 * half:512 * half + b - a], w(kc), rhs(kc)[:, a:b],
                                  start=(i == 0), stop=(i == len(kcs) - 1))
                        if note is not None and half == 0 and i == 0:
                            last.then_inc(note, 1)
                last.then_inc(filled[s], 1)

            def job(n, s, cols, kcs, rhs, split=T // 2, norm=None):
                begin(s)
                pe.wait_ge(w_loaded[n % RING], 16 * (n // RING + 1))
                product(s, lambda kc: ring[:, n % RING, cols * kc:cols * kc + 128], kcs, rhs, split, note=jobs_begun, norm=norm)

            def layer_norm(k):
                end = k == 2 * L

                def total(s, t, tiles, ready, done):
                    for kc in tiles:
                        ready(kc)
                        for h in range(2):
                            o = pair[s][:, 512 * h:512 * h + T // 2]
                            last = mm(o, ones[:, :], t(kc)[:, T // 2 * h:T // 2 * h + T // 2],
                                      start=(kc == tiles[0]), stop=(kc == tiles[-1]))
                    last.then_inc(done, 1)

                if not end:
                    begin(0)
                if k == 0:
                    pe.wait_ge(ones_set, 2)
                    total(0, lambda kc: x[:, kc, :], range(KC), lambda kc: pe.wait_ge(x_in[kc], 16), filled[0])
                else:
                    if end:
                        pe.wait_ge(acc_ready, 1)
                    else:
                        pe.wait_ge(summed, (KC - 1) * (1, 3, 4)[k - 1])
                    total(0, lambda kc: rst, range(1), lambda kc: None, last_filled[0] if end else filled[0])
                if not end:
                    begin(1)
                total(1, lambda kc: cat[:, kc, :], range(KC), lambda kc: pe.wait_ge(squares, KC * k + kc + 1), last_filled[1] if end else filled[1])

            layer_norm(0)
            def tables():
                pe.wait_ge(rel_in, 32)
                pe.wait_ge(consts_in, 80)
                for h in range(NH):
                    p = pair[2 + h % 2]
                    if h >= 2:
                        pe.wait_ge(f_ready, h - 1)
                    mm(p[:, 0:512], relb[0:32, h, :], cst[0:32, C_OF:C_OF + 512], start=True, stop=True)
                    mm(p[:, 512:512 + 128], relb[0:32, h, :], cst[0:32, C_OF + 512:C_OF + BW], start=True, stop=True).then_inc(f_mm, 1)
                pe.wait_ge(tk_ready, 1)
                pe.wait_ge(f_ready, NH)
                mm(pair[2][:, 0:512], reltk, cst[:, C_TK:C_TK + 512], start=True, stop=True)
                mm(pair[2][:, 512:512 + NS], reltk, cst[:, C_TK + 512:C_TK + SK], start=True, stop=True).then_inc(bs_mm, 1)

            for l in range(L):
                n = JOBS[l]
                xr = lambda kc: x[:, kc, :]
                for m in range(WIN_T - 1):
                    if l == 0 and m == 2:
                        tables()
                        pe.wait_ge(bs_ready, 1)
                    job(n + m, m % 4, 128, range(KC), xr, split=256, norm=2 * l if m == 0 else None)
                nv = n + WIN_T - 1
                job(nv, 2, 136, range(KC), xr, split=256)
                begin(3)
                product(3, lambda kc: ring[:, nv % RING, 136 * kc + 128:136 * kc + 136], range(KC), xr, 256, rows=NH)
                n += WIN_T
                all_empty()
                if l == 0:
                    pe.wait_ge(consts_in, 80)
                for b in range(NQT):
                    nc.tensor.transpose(bank(0)[:, 128 * b:128 * b + 128], vn[:, 128 * b:128 * b + 128], ident)
                    nc.tensor.transpose(bank(2)[:, NH * b:NH * b + NH], wn[:, 128 * b:128 * b + 128], cst[0:NH, C_ID:C_ID + NH])
                nc.tensor.transpose(bank(1)[0:NS, 0:128], vn[:, SEQ:T], ident).then_inc(tok_mm, 1)

                for hf in range(2):
                    v = 2 * l + hf + 1
                    if hf == 0:
                        pe.wait_ge(tok_ready, 2 * l + 2)
                    pe.wait_ge(bp_ready, v)
                    if hf:
                        pe.wait_ge(hout_ready, v - 1)
                    for k in range(2):
                        for e in range(HP):
                            last = nc.tensor.transpose(pair[k][:, 128 * e:128 * e + 128],
                                                       BP[k][:, e].rearrange("p m c -> p (m c)"), ident)
                    last.then_inc(bt_mm, 1)
                    pe.wait_ge(cp_ready, v)
                    if hf:
                        pe.wait_ge(y_ready, v - 1)
                    for g in range(HG):
                        e, lo = g // 2, 64 * (g % 2)
                        o = pair[2 + g % 2][0:GC, 128 * e:128 * e + 128]
                        for k in range(2):
                            last = mm(o, Bb[k][lo:lo + 64, e], CP[k][lo:lo + 64, e, 0:CH].rearrange("p m c -> p (m c)"),
                                      start=(k == 0), stop=(k == 1))
                    last.then_inc(kd_mm, 1)
                    pe.wait_ge(bt_ready, v)
                    pe.wait_ge(u_in, 256 * (l + 1))
                    pe.wait_ge(u_zero, l + 1)
                    for part in range(2):
                        for k in range(2):
                            for gl in range(HP * part, HP * part + HP):
                                e, lo, g = gl // 2, 64 * (gl % 2), HG * hf + gl
                                o, e4 = bank(2 * part + k), e % (HP // 2)
                                mm(o[lo:lo + 64, NC * e4:NC * e4 + NC], BT[:, k, e, lo:lo + 64], U[:, g, NB:CW],
                                   start=True, stop=True)
                                last = mm(o[lo:lo + 64, 256 + NB * e4:256 + NB * e4 + NB], BT[0:64, k, e, lo:lo + 64],
                                          U2[0:64, g, :], start=True, stop=True)
                        last.then_inc(g_mm, 1)
                    pe.wait_ge(toep_in, 128 * v)
                    for gl in range(HG):
                        if gl % HP == 0:
                            pe.wait_ge(h_ready, 2 * (v - 1) + gl // HP + 1)
                        e, lo, g = gl // 2, 64 * (gl % 2), HG * hf + gl
                        o = bank(4 + 2 * (gl % 2) + e // 6)[:, CW * (e % 6):CW * (e % 6) + CW]
                        mm(o, toep[:, HP * (gl % 2) + e, :], U[:, g, :], start=True, stop=False)
                        for k in range(2):
                            last = mm(o, CP[k][lo:lo + 64, e, 1:CH + 1].rearrange("p m c -> p (m c)"),
                                      H[k][lo:lo + 64, e, 0:CW], start=False, stop=(k == 1))
                    last.then_inc(y_mm, 1)

                pe.wait_ge(y_ready, 2 * l + 2)
                pe.wait_ge(hout_ready, 2 * l + 2)
                ni, nl, npt = 8 * 3 * l, 8 * NQT * l, 20 * l
                for b in range(NQT):
                    w = 128 * (b + 1)
                    qs = slice(128 * b, 128 * b + 128)
                    for h in range(NH):
                        lo = 64 * (h // 4)
                        if nl >= 3:
                            pe.wait_ge(lg_used, nl - 2)
                        o = bank(2 + nl % 3)[:, 0:w]
                        mm(o, q[lo:lo + 64, h % 4, qs], kn[lo:lo + 64, 0:w], start=True, stop=False)
                        if h == 0:
                            pe.wait_ge(hide_ready, NQT * l + b + 1)
                        hide = nosel[:, 0:w] if b else cst[:, C_CM:C_CM + 128]
                        mm(o, negid, hide, start=False, stop=True).then_inc(lg_mm, 1)
                        nl += 1
                    if b + 1 < NQT:
                        for h in range(NH):
                            lo = 64 * (h % 2)
                            if ni >= 2:
                                pe.wait_ge(relu_ready, ni - 1)
                            mm(bank(ni % 2)[:, 0:w + 128], qi[lo:lo + 64, h // 2, 128 * b + 128:128 * b + 256], kin[lo:lo + 64, 0:w + 128],
                               start=True, stop=True).then_inc(idx_mm, 1)
                            ni += 1
                    else:
                        pe.wait_ge(lg_used, nl)
                        pe.wait_ge(relu_ready, ni)
                        mm(bank(4)[:, 0:NS], cst[0:NH, C_OH:C_OH + 128], wn[0:NH, SEQ:T], start=True, stop=True).then_inc(wr_mm, 1)
                        pe.wait_ge(qz_ready, l + 1)
                        for r in range(2):
                            pgI = pgs[r][2]
                            pe.wait_ge(pages_in[r], 256 * (l + 1))
                            lz = Qzi[:, 4 * r:4 * r + 4].rearrange("p b a i t -> p (b a i t)")
                            for bi in range(4):
                                mm(bank(0)[32 * bi:32 * bi + 32, :], lz[:, 32 * bi:32 * bi + 32],
                                   pgI[:, 4 * bi:4 * bi + 4, :], start=True, stop=True)
                            mm(bank(1)[:, 0:NS], lz, kin[:, SEQ:T], start=True, stop=True).then_inc(si_mm, 1)
                            if r == 0:
                                pe.wait_ge(wr_ready, l + 1)
                            pe.wait_ge(srelu, 2 * l + r + 1)
                            mm(bank(2)[0:NS, :], wr[:, r, :], rls[:, 0:PAST], start=(r == 0), stop=(r == 1))
                            mm(bank(3)[0:NS, 0:NS], wr[:, r, :], rls[:, PAST:SK], start=(r == 0), stop=(r == 1)).then_inc(sc_mm, 1)
                    pe.wait_ge(prob_ready, NQT * l + b + 1)
                    for g in range(2):
                        for kt in range(b + 1):
                            if npt >= 2:
                                pe.wait_ge(pt_ready, npt - 1)
                            for i in range(4):
                                last = nc.tensor.transpose(bank(5 + npt % 2)[:, 128 * i:128 * i + 128],
                                                           Lg[:, 4 * g + i, 128 * kt:128 * kt + 128], ident)
                            last.then_inc(pt_mm, 1)
                            npt += 1
                    pe.wait_ge(pt_ready, npt)
                    nb = NQT * l + b
                    if nb:
                        pe.wait_ge(pv_ready, nb)
                    for g in range(2):
                        for kt in range(b + 1):
                            last = mm(bank(7)[64 * g:64 * g + 64, :], vtok[:, kt, 64 * g:64 * g + 64], PT[:, g, kt, :],
                                      start=(kt == 0), stop=(kt == b))
                    last.then_inc(pv_mm, 1)

                pe.wait_ge(scs_ready, l + 1)
                pe.wait_ge(gelu_ready, l + 1)
                pe.wait_ge(pv_ready, NQT * (l + 1))
                for m in range(8):
                    job(n + m, m % 4, 128, range(4), lambda kc: u[:, kc, :])
                n += 8
                all_empty()
                pe.wait_ge(nosel_ready, l + 1)
                for r in range(2):
                    lz = Qz[:, 4 * r:4 * r + 4].rearrange("p b a i t -> p (b a i t)")
                    ex = cst[0:NS, C_EX + 128 * r:C_EX + 128 * r + 128]
                    pe.wait_ge(pages_kv[r], 512 * (l + 1))
                    mm(bank(2 * r), ex, nss[0:NS, 0:PAST], start=True, stop=False)
                    for bi in range(4):
                        mm(bank(2 * r)[32 * bi:32 * bi + 32, :], lz[:, 32 * bi:32 * bi + 32],
                           pgs[r][0][:, 4 * bi:4 * bi + 4, :], start=False, stop=True)
                    mm(bank(2 * r + 1)[:, 0:NS], ex, nss[0:NS, PAST:SK], start=True, stop=False)
                    mm(bank(2 * r + 1)[:, 0:NS], lz, kn[:, SEQ:T], start=False, stop=True).then_inc(sl_mm, 1)
                for r in range(2):
                    pe.wait_ge(sprob, 2 * l + r + 1)
                    for k in range(NPG):
                        nc.tensor.transpose(bank(4 + 2 * r)[:, 128 * k:128 * k + 128], Ls[r][:, 128 * k:128 * k + 128], ident)
                    nc.tensor.transpose(bank(5 + 2 * r)[0:NS, 0:128], Ls[r][:, PAST:SK], ident).then_inc(spt_mm, 1)
                for r in range(2):
                    pe.wait_ge(spt_ready, 2 * l + r + 1)
                    for bi in range(4):
                        o = bank(2 * r)[:, 32 * bi:32 * bi + 32]
                        for k in range(NPG):
                            mm(o, pgs[r][1][:, NPG * bi + k, :], PTs[r][:, k, 32 * bi:32 * bi + 32], start=(k == 0), stop=False)
                        last = mm(o, vtok[0:NS, NQT, :], PTs[r][0:NS, NPG, 32 * bi:32 * bi + 32], start=False, stop=True)
                    last.then_inc(spv_mm, 1)

                pe.wait_ge(spv_ready, 2 * l + 2)
                for m in range(8):
                    job(n + m, m % 4, 128, range(KC), lambda kc: cat[:, kc, :])
                n += 8
                layer_norm(1 + 2 * l)
                if l == 1:
                    pe.wait_ge(x_ready, KC * (2 + 2 * l))
                    all_empty()
                    for tt in range(TT):
                        rows = 128 if tt < 4 else NS
                        for kc in range(KC):
                            last = mm(bank(6)[0:rows, NE * tt:NE * tt + NE], x[:, kc, 128 * tt:128 * tt + rows], wrt[:, kc, :],
                                      start=(kc == 0), stop=(kc == KC - 1))
                    last.then_inc(r_mm, 1)
                    for tt in range(TT):
                        rows = 128 if tt < 4 else NS
                        if tt >= 3:
                            pe.wait_ge(xt_ready, tt - 2)
                        for kc in range(KC):
                            last = nc.tensor.transpose(pair[tt % 3][0:rows, 128 * kc:128 * kc + 128],
                                                       x[:, kc, 128 * tt:128 * tt + rows], ident)
                        last.then_inc(xt_mm, 1)
                    pe.wait_ge(sel_ready, 1)
                    pe.wait_ge(one_set, 1)
                    for tt in range(TT):
                        rows = 128 if tt < 4 else NS
                        o = bank(6)[0:rows, 64 + NE * tt:64 + NE * tt + NE]
                        for t0 in range(tt):
                            mm(o, one[:, 0:rows], sel[:, t0, :], start=(t0 == 0), stop=False)
                        last = mm(o, cst[0:rows, C_CM:C_CM + rows], sel[0:rows, tt, :], start=(tt == 0), stop=True)
                    last.then_inc(rank_mm, 1)
                    pe.wait_ge(xt_ready, TT)
                pe.wait_ge(pt_in, 16 * (l + 1))
                for m in range(8):
                    job(n + m, (2 * m) % 4, 128, range(KC), xr, norm=1 + 2 * l if m == 0 else None)
                    s = (2 * m + 1) % 4
                    begin(s)
                    product(s, lambda kc: ring[:, (n + m) % RING, 1024 + 128 * kc:1152 + 128 * kc], range(2),
                            lambda kc: pt[:, kc, :], T // 2)
                    if l == 1 and m == 0:
                        pe.wait_ge(ov_ready, 1)
                        mm(bank(6)[0:1, 0:1], ovs, one[:, 0:1], start=True, stop=True).then_inc(flag_mm, 1)
                        pe.wait_ge(flag_ready, 1)
                n += 8
                def dense_blocks(n, count, blocks_before):
                    c0 = list(c.n)
                    with pe.Fori(0, count) as e:
                        k = 0
                        for kind, i, ps in ffn_plan():
                            if kind == "down" and i == 0:
                                pe.wait_ge(hid_ready, e * FT + (FT * blocks_before + FT))
                            for s, seen in ps:
                                nn = n + k
                                pe.wait_ge(emptied[s], e * FFN_USES[s] + (c0[s] + seen))
                                pe.wait_ge(w_loaded[nn % RING], e * (16 * BLOCK_JOBS // RING) + 16 * (nn // RING + 1))
                                tile = lambda kc: ring[:, nn % RING, 128 * kc:128 * kc + 128]
                                if kind == "up":
                                    product(s, tile, range(KC), xr, T // 2, note=jobs_begun)
                                else:
                                    product(s, tile, range(FT), lambda kc: hid[:, kc, :], T // 2, note=jobs_begun)
                                k += 1
                    for s in range(4):
                        c.n[s] += FFN_USES[s] * count

                all_empty()
                if l == 0:
                    dense_blocks(n, 2, 0)
                else:
                    def rows_in(i):
                        s = (3, 0)[i]
                        for q_ in range(4):
                            kc = 4 * i + q_
                            o = pair[s][:, 512 * (q_ // 2) + CAP * (q_ % 2):][:, 0:CAP]
                            for ct, rows in enumerate(C_ROWS):
                                last = nc.tensor.transpose(o[:, 128 * ct:128 * ct + rows], xgt[0:rows, ct, 128 * kc:128 * kc + 128],
                                                           cst[0:rows, C_ID:C_ID + rows])
                        last.then_inc(filled[s], 1)

                    pe.wait_ge(xg_in, 32)
                    for i, s in enumerate((3, 0)):
                        begin(s)
                        rows_in(i)
                    c0 = list(c.n)
                    with pe.Fori(0, NE) as e:
                        def held(s, seen):
                            pe.wait_ge(emptied[s], e * MOE_USES[s] + (c0[s] + seen))

                        def tile_in(k):
                            nn = n + k
                            pe.wait_ge(w_loaded[nn % RING], e * (16 * BLOCK_JOBS // RING) + 16 * (nn // RING + 1))
                            return ring[:, nn % RING, :]

                        held(3, 0)
                        for kind, i, s, seen in moe_plan():
                            if kind == "down" and i == 0:
                                for s2, n2 in ((0, 3), (1, 3), (2, 3), (3, 2)):
                                    held(s2, n2)
                            if kind == "xg" and i == 0:
                                pe.wait_ge(xg_in, e * 32 + 64)
                            if kind == "yg" and i == 0:
                                for s2, n2 in ((3, 3), (0, 4), (1, 4), (2, 4)):
                                    held(s2, n2)
                            if (kind, i) != ("yg", 1):
                                held(s, seen)
                            if kind == "xg":
                                rows_in(i)
                                continue
                            if kind == "yg":
                                rows = C_ROWS[i]
                                for kc in range(KC):
                                    last = nc.tensor.transpose(pair[s][0:rows, 128 * kc:128 * kc + 128],
                                                               yT[:, kc, 128 * i:128 * i + rows], ident)
                                last.then_inc(filled[s], 1)
                                continue
                            for j in range(2):
                                w = tile_in((2 * i if kind == "up" else 2 * FT + 2 * i) + j)
                                src, kn_ = (xg, KC) if kind == "up" else (hidg, FT)
                                for kc in range(kn_):
                                    last = mm(pair[s][:, 512 * j:512 * j + CAP], w[:, 128 * kc:128 * kc + 128], src[:, kc, :],
                                              start=(kc == 0), stop=(kc == kn_ - 1))
                                    if kc == 0:
                                        last.then_inc(jobs_begun, 1)
                            last.then_inc(filled[s], 1)
                    for s in range(4):
                        c.n[s] += MOE_USES[s] * NE
                    pe.wait_ge(comb_ready, TT)
                    for kc in range(KC):
                        s = kc % 4
                        begin(s)
                        for tt in range(TT):
                            rows = 128 if tt < 4 else NS
                            last = nc.tensor.transpose(pair[s][:, 128 * tt:128 * tt + rows], gt[0][0:rows, tt, 128 * kc:128 * kc + 128],
                                                       cst[0:rows, C_ID:C_ID + rows])
                        last.then_inc(filled[s], 1)
                    all_empty()
                    left = pe.value_load(flag[0:1, 0:1], min_val=0, max_val=2 * T)
                    with pe.If(left > 0):
                        for e in range(NE):
                            if e >= 2:
                                pe.wait_ge(gb_ready, e - 1)
                            p = pair[2 + e % 2]
                            for tt in range(TT):
                                rows = 128 if tt < 4 else NS
                                last = mm(p[:, 128 * tt:128 * tt + rows], over[0:rows, tt, e:e + 1].to_broadcast([rows, 128]),
                                          cst[0:rows, C_ID:C_ID + rows], start=True, stop=True)
                            last.then_inc(gb_mm, 1)
                        pe.wait_ge(gb_ready, NE)
                        dense_blocks(n + BLOCK_JOBS * NE, NE, 2)
                layer_norm(2 + 2 * l)

        @block.scalar
        def _(act):
            A = nc.scalar.activation
            steps = [0]
            c = Count()

            def link(ins):
                steps[0] += 1
                ins.then_inc(act_step, 1)
                act.wait_ge(act_step, steps[0])

            def got(s):
                act.wait_ge(filled[s], c.take(s))

            def layer_norm(k):
                em, n = (last_emptied[0], 1) if k == 2 * L else (emptied[0], c.take(0))
                if k < 2 * L:
                    c.take(1)
                src = x if k == 0 else acc
                for kc in range(KC):
                    if kc < KC - 1:
                        act.wait_ge(centred, (KC - 1) * k + kc + 1)
                    else:
                        act.wait_ge(em, n)
                    A(cat[:, kc, :], src[:, kc, :], ACT.Square).then_inc(squares, 1)
                if k == 0:
                    act.wait_ge(ln_in, 16)
                    act.wait_ge(ones_set, 2)
                act.wait_ge(*((last_filled[1], 1) if k == 2 * L else (filled[1], c.n[1])))
                A(halves(rst), even(1), ACT.Sqrt, bias=eps[:, 0:1]).then_inc(rst_ready, 1)
                for kc in range(KC):
                    act.wait_ge(scaled, KC * k + kc + 1)
                    A(x[:, kc, :], src[:, kc, :], ACT.Identity, bias=lnp[:, 2 * k + 1, kc:kc + 1],
                      scale=lnp[:, 2 * k, kc:kc + 1]).then_inc(x_ready, 1)

            layer_norm(0)
            def step_exp(v):
                act.wait_ge(par_in, 16 * v)
                A(sm[:, 0, :], par[:, 2, :], ACT.Exp).then_inc(ldt, 1)

            def radius(v):
                act.wait_ge(theta, 2 * v - 1)
                A(sm[:, 3, :], sm[:, 1, :], ACT.Exp)
                A(sm[:, 4, :], sm[:, 1, :], ACT.Exp, scale=float(CH)).then_inc(expd, 1)

            def angle(v):
                act.wait_ge(theta, 2 * v)
                A(sm[:, 5:7, :], sm[:, 7:9, :], ACT.Sin).then_inc(sincos, 1)

            for l in range(L):
                dst = [u[:, k, :] for k in range(4)] + [q[:, k, :] for k in range(4)] + [qi[:, k, :] for k in range(4)]
                dst += [kn[:, :], kin[:, :], vn[:, :], wn[:, :]]
                for m in range(16):
                    s = m % 4
                    if l == 0 and m == 2:
                        for h in range(NH):
                            act.wait_ge(f_mm, h + 1)
                            A(frow[:, h, 0:512], pair[2 + h % 2][:, 0:512], ACT.Copy)
                            A(frow[:, h, 512:BW], pair[2 + h % 2][:, 512:BW], ACT.Copy).then_inc(f_ready, 1)
                    elif m == 5:
                        step_exp(2 * l + 1)
                    elif m == 7:
                        radius(2 * l + 1)
                    elif m == 9:
                        angle(2 * l + 1)
                    got(s)
                    d = dst[m]
                    if m < 4:
                        A(d[:, 0:256], pair[s][:, 0:256], ACT.Copy)
                        A(d[:, 256:T], pair[s][:, 512:512 + T - 256], ACT.Copy).then_inc(emptied[s], 1)
                        continue
                    rows = NH if m == 15 else 128
                    dn = d[:, 0:SEQ].rearrange("p (c j) -> p j c", j=CH)
                    by = HD ** -0.5 if 4 <= m < 8 else 1.0
                    A(dn[:, 0:4, :], pair[s][0:rows, 0:256].rearrange("p (j c) -> p j c", j=4), ACT.Copy, scale=by)
                    A(dn[:, 4:8, :], pair[s][0:rows, 512:768].rearrange("p (j c) -> p j c", j=4), ACT.Copy, scale=by)
                    A(d[:, SEQ:T], pair[s][0:rows, 768:768 + NS], ACT.Copy, scale=by).then_inc(emptied[s], 1)
                act.wait_ge(tok_mm, l + 1)
                A(vtok[:, 0:NQT, :], bank(0).rearrange("p (b c) -> p b c", b=NQT), ACT.Copy)
                A(vtok[0:NS, NQT, :], bank(1)[0:NS, 0:128], ACT.Copy).then_inc(tok_ready, 1)
                A(wtok[:, :, :], bank(2)[:, 0:NQT * NH].rearrange("p (b c) -> p b c", b=NQT), ACT.Copy).then_inc(tok_ready, 1)

                for hf in range(2):
                    v = 2 * l + hf + 1
                    act.wait_ge(bt_mm, v)
                    for k in range(2):
                        ins = A(BT[:, k].rearrange("p e n -> p (e n)"), pair[k][:, :], ACT.Copy)
                    ins.then_inc(bt_ready, 1)
                    act.wait_ge(kd_mm, v)
                    for k in range(2):
                        ins = A(cf[0:GC, 1024 * k:1024 * k + 1024], pair[2 + k][0:GC, :], ACT.Copy)
                    ins.then_inc(kd_ready, 1)
                    if hf == 0:
                        step_exp(v + 1)
                        radius(v + 1)
                        angle(v + 1)
                    else:
                        act.wait_ge(y_out, 192 * (v - 1))
                    act.wait_ge(y_mm, v)
                    for a in range(2):
                        ya = Y.rearrange("p (e a) c -> p a e c", a=2)[:, a]
                        for k, n in enumerate((6, HP - 6)):
                            ins = A(ya[:, 6 * k:6 * k + n, :], bank(4 + 2 * a + k)[:, 0:CW * n].rearrange("p (g c) -> p g c", g=n), ACT.Copy)
                    ins.then_inc(y_ready, 1)
                def sample_relu(r):
                    act.wait_ge(si_mm, 2 * l + r + 1)
                    if r:
                        act.wait_ge(sc_mm, 2 * l + 1)
                    A(rls[:, 0:PAST], bank(0), ACT.Relu)
                    A(rls[:, PAST:SK], bank(1)[:, 0:NS], ACT.Relu).then_inc(srelu, 1)

                ni, npt = 24 * l, 20 * l
                for b in range(NQT):
                    w = 128 * (b + 1)
                    for part in range(2):
                        act.wait_ge(nmx_ready, 2 * (NQT * l + b) + part + 1)
                        for h in range(4 * part, 4 * part + 4):
                            A(Lg[:, h, 0:w], Lg[:, h, 0:w], ACT.Exp, bias=nmx[:, h:h + 1],
                              accum_out=sums[:, h:h + 1]).then_inc(exp_ready, 1)
                        if b + 1 < NQT:
                            for h in range(4):
                                act.wait_ge(idx_mm, ni + 1)
                                if ni >= 4:
                                    act.wait_ge(relu_used, ni - 3)
                                A(rl[:, ni % 4, 0:w + 128], bank(ni % 2)[:, 0:w + 128], ACT.Relu).then_inc(relu_ready, 1)
                                ni += 1
                    if b == NQT - 1:
                        sample_relu(0)
                    act.wait_ge(rs_ready, NQT * l + b + 1)
                    for h in range(NH):
                        ins = A(Lg[:, h, 0:w], Lg[:, h, 0:w], ACT.Copy, scale=rs[:, h:h + 1])
                    ins.then_inc(prob_ready, 1)
                    if b == NQT - 1:
                        sample_relu(1)
                    if b == 0:
                        act.wait_ge(y_out, 192 * 2 * (l + 1))
                    for g in range(2):
                        for kt in range(b + 1):
                            act.wait_ge(pt_mm, npt + 1)
                            A(PT[:, g, kt, :], bank(5 + npt % 2), ACT.Copy).then_inc(pt_ready, 1)
                            npt += 1
                    act.wait_ge(pv_mm, NQT * l + b + 1)
                    for i in range(4):
                        o = cat[:, 4 + i, 0:SEQ].rearrange("p (j c) -> p c j", j=CH)[:, 16 * b:16 * b + 16, :]
                        ins = A(o, bank(7)[:, 128 * i:128 * i + 128].rearrange("p (c j) -> p c j", j=CH), ACT.Copy)
                    ins.then_inc(pv_ready, 1)
                    if b == 1:
                        act.wait_ge(yd_ready, l + 1)
                        A(u, u, ACT.Gelu_apprx_tanh).then_inc(gelu_ready, 1)

                for m in range(8):
                    s = m % 4
                    if m % 2 == 0:
                        a_use = c.take(s)
                        continue
                    got(s)
                    act.wait_ge(emptied[s - 1], a_use - 1)
                    A(halves(sg[:, m // 2 % 2, :]), even(s), ACT.Sigmoid).then_inc(emptied[s], 1)
                for r in range(2):
                    act.wait_ge(snmx, 2 * l + r + 1)
                    A(Ls[r], Ls[r], ACT.Exp, bias=nms[r][:, 0:1], accum_out=nms[r][:, 1:2]).then_inc(sexp, 1)
                for r in range(2):
                    act.wait_ge(spt_mm, 2 * l + r + 1)
                    A(PTs[r][:, 0:NPG, :], bank(4 + 2 * r).rearrange("p (k c) -> p k c", k=NPG), ACT.Copy)
                    A(PTs[r][0:NS, NPG, :], bank(5 + 2 * r)[0:NS, 0:128], ACT.Copy).then_inc(spt_ready, 1)
                for r in range(2):
                    act.wait_ge(spv_mm, 2 * l + r + 1)
                    pv = bank(2 * r)[:, 0:128].rearrange("p (b g i t) -> p g b i t", b=4, g=2, i=4)
                    for g in range(2):
                        for i in range(4):
                            o = cat[64 * g:64 * g + 64, 4 + i, SEQ:T].rearrange("p (t b) -> p b t", b=NB)[:, 4 * r:4 * r + 4, :]
                            ins = A(o, pv[64 * g:64 * g + 64, g, :, i, :], ACT.Copy)
                    ins.then_inc(spv_ready, 1)

                for m in range(8):
                    c.take(m % 4)
                layer_norm(1 + 2 * l)
                if l == 1:
                    for tt in range(TT):
                        rows = 128 if tt < 4 else NS
                        act.wait_ge(xt_mm, tt + 1)
                        A(xtok[0:rows, tt, :], pair[tt % 3][0:rows, :], ACT.Copy).then_inc(xt_ready, 1)
                    act.wait_ge(gdiff, 1)
                    A(rlog, rlog, ACT.Exp)
                    A(rsm[:, :, 1:2], rsm[:, :, 0:1], ACT.Exp).then_inc(gexp, 1)
                for m in range(8):
                    s = (2 * m) % 4
                    got(s)
                    c.take(s + 1)
                    if m >= 2:
                        act.wait_ge(ple_used, 8 * l + m - 1)
                    A(halves(sg[:, m % 2, :]), even(s), ACT.Sigmoid).then_inc(emptied[s], 1)
                act.wait_ge(ple_used, 8 * (l + 1))

                def dense_blocks(count):
                    c0 = list(c.n)
                    with act.Fori(0, count) as e:
                        for kind, f, ps in ffn_plan():
                            if kind == "up":
                                (s, seen), (s2, seen2) = ps
                                act.wait_ge(filled[s], e * FFN_USES[s] + (c0[s] + seen + 1))
                                if f >= 2:
                                    act.wait_ge(emptied[s2], e * FFN_USES[s2] + (c0[s2] + seen2))
                                A(halves(sg[:, f % 2, :]), even(s), ACT.Silu).then_inc(emptied[s], 1)
                    for s in range(4):
                        c.n[s] += FFN_USES[s] * count

                if l == 0:
                    dense_blocks(2)
                else:
                    def rows_in(i, s):
                        A(xg[:, 4 * i:4 * i + 4, :].rearrange("p (h k) c -> p h (k c)", h=2), banks(s, 2 * CAP), ACT.Copy).then_inc(emptied[s], 1)

                    for i, s in enumerate((3, 0)):
                        got(s)
                        rows_in(i, s)
                    c0 = list(c.n)
                    with act.Fori(0, NE) as e:
                        for kind, i, s, seen in moe_plan():
                            if kind == "down":
                                continue
                            act.wait_ge(filled[s], e * MOE_USES[s] + (c0[s] + seen + 1))
                            if kind == "up":
                                if i >= 2:
                                    s2 = (i - 2) % 4
                                    act.wait_ge(emptied[s2], e * MOE_USES[s2] + (c0[s2] + (i - 2) // 4 + 1))
                                A(sg[:, i % 2, 0:CAP], pair[s][:, 0:CAP], ACT.Silu).then_inc(silu_ready, 1)
                            elif kind == "xg":
                                rows_in(i, s)
                            else:
                                if i == 0:
                                    act.wait_ge(y_free, e + 1)
                                A(ygt[0:C_ROWS[i], i, :], pair[s][0:C_ROWS[i], :], ACT.Copy).then_inc(emptied[s], 1)
                    for s in range(4):
                        c.n[s] += MOE_USES[s] * NE
                    for tt in range(TT):
                        rows = 128 if tt < 4 else NS
                        act.wait_ge(gt_in[0][tt], 16)
                        A(gt[0][0:rows, tt, :], gt[0][0:rows, tt, :], ACT.Copy, scale=g01[0:rows, tt, 0:1]).then_inc(gt_scaled, 1)
                    for kc in range(KC):
                        c.take(kc % 4)
                    act.wait_ge(flag_ready, 1)
                    left = act.value_load(flag[0:1, 0:1], min_val=0, max_val=2 * T)
                    with act.If(left > 0):
                        for e in range(NE):
                            act.wait_ge(gb_mm, e + 1)
                            A(gb[:, e, :], pair[2 + e % 2][:, 0:T], ACT.Copy).then_inc(gb_ready, 1)
                        dense_blocks(NE)
                layer_norm(2 + 2 * l)

        @block.vector
        def _(dve):
            V = nc.vector
            sums_done = [0]
            MAGIC = 1.5 * 2.0 ** 23
            TWO_PI = (6.28125, 1.93500518798828125e-3, 2 * math.pi - 6.28125 - 1.93500518798828125e-3)
            steps = [0]
            c = Count()

            def link(ins):
                steps[0] += 1
                ins.then_inc(dve_step, 1)
                dve.wait_ge(dve_step, steps[0])

            def got(s):
                dve.wait_ge(filled[s], c.take(s))

            def layer_norm(k):
                src = x if k == 0 else acc
                f, m, n = (last_filled, last_emptied, [1, 1]) if k == 2 * L else (filled, emptied, [c.take(0), c.take(1)])
                dve.wait_ge(f[0], n[0])
                for kc in range(KC):
                    V.tensor_tensor(halves(src[:, kc, :]), halves(src[:, kc, :]), even(0),
                                    ALU.subtract).then_inc(centred if kc < KC - 1 else m[0], 1)
                dve.wait_ge(rst_ready, k + 1)
                V.reciprocal(rst, rst).then_inc(m[1], 1)
                dve.wait_ge(m[1], n[1])
                for kc in range(KC):
                    V.tensor_tensor(src[:, kc, :], src[:, kc, :], rst, ALU.mult).then_inc(scaled, 1)

            def cmul(o, a, b, t1, t2, negate_im=False):
                V.tensor_tensor(t1, a[0], b[0], ALU.mult)
                link(V.tensor_tensor(t2, a[1], b[1], ALU.mult))
                link(V.tensor_tensor(o[0], t1, t2, ALU.subtract))
                V.tensor_tensor(t1, a[0], b[1], ALU.mult)
                link(V.tensor_tensor(t2, a[1], b[0], ALU.mult))
                if negate_im:
                    link(V.scalar_tensor_tensor(o[1], t1, -1.0, t2, ALU.mult, ALU.subtract))
                else:
                    link(V.tensor_tensor(o[1], t1, t2, ALU.add))

            def add_up(m, before):
                if m == 0:
                    return
                if m > 1:
                    dve.wait_ge(summed, before + m - 1)
                V.tensor_tensor(rst, acc[:, 0, :] if m == 1 else rst, acc[:, m, :], ALU.add).then_inc(summed, 1)

            def top(vals, work, eight, k, pad=None, between=None):
                src, n = vals, vals.shape[1]
                for i in range(k // 8):
                    link(V.max(eight, src))
                    link(V.match_replace(work[:, 0:n], eight, src, GONE))
                    if between is not None:
                        between(i)
                    src = work[:, 0:n]
                if k % 8:
                    link(V.max(eight, src))
                    link(V.memset(eight[:, k % 8:8], pad))
                    link(V.match_replace(work, eight, work, GONE))

            layer_norm(0)
            dve.wait_ge(consts_in, 80)
            dve.wait_ge(rel_in, 32)
            V.tensor_tensor(reltk, reltk, cst[:, C_MT:C_MT + 128], ALU.mult).then_inc(tk_ready, 1)
            dve.wait_ge(bs_mm, 1)
            V.tensor_copy(bs[:, 0:512], pair[2][:, 0:512])
            V.tensor_copy(bs[:, 512:SK], pair[2][:, 512:SK]).then_inc(bs_ready, 1)

            for l in range(L):
                for s in range(4):
                    for _ in range(4):
                        c.take(s)
                for hf in range(2):
                    v = 2 * l + hf + 1
                    dve.wait_ge(par_in, 16 * v)
                    dve.wait_ge(ldt, v)
                    r_ = lambda i: sm[:, i, :]
                    are, aim = par[:, 0, :], par[:, 1, :]
                    V.tensor_tensor(r_(2), aim, r_(0), ALU.mult)
                    V.tensor_tensor(r_(1), are, r_(0), ALU.mult).then_inc(theta, 1)
                    dve.wait_ge(theta, 2 * v - 1)
                    link(V.tensor_scalar(r_(9), r_(2), 1 / (2 * math.pi), MAGIC, ALU.mult, ALU.add))
                    link(V.tensor_scalar(r_(9), r_(9), MAGIC, None, ALU.subtract))
                    for i, part in enumerate(TWO_PI):
                        link(V.scalar_tensor_tensor(r_(7) if i == 2 else r_(2), r_(9), -part, r_(2), ALU.mult, ALU.add))
                    link(V.tensor_scalar(r_(10), r_(7), math.pi / 2, None, ALU.add))
                    link(V.tensor_scalar(r_(11), r_(10), math.pi, 2 * math.pi, ALU.is_gt, ALU.mult))
                    link(V.tensor_tensor(r_(8), r_(10), r_(11), ALU.subtract))
                    V.tensor_scalar(sm[:, 7:9, :], sm[:, 7:9, :], 3.1415925, -3.1415925, ALU.min, ALU.max).then_inc(theta, 1)
                    V.memset(P[0][:, 0, :], 1.0)
                    V.memset(P[1][:, 0, :], 0.0)
                    dve.wait_ge(sincos, v)
                    dve.wait_ge(expd, v)
                    V.tensor_tensor(P[0][:, 1, :], r_(6), r_(3), ALU.mult)
                    link(V.tensor_tensor(P[1][:, 1, :], r_(5), r_(3), ALU.mult))
                    for w in (1, 2, 4):
                        t1 = T1[:, 0:w * HP].rearrange("p (m e) -> p m e", e=HP)
                        t2 = T2[:, 0:w * HP].rearrange("p (m e) -> p m e", e=HP)
                        cmul([P[k][:, w + 1:2 * w + 1, :] for k in range(2)], [P[k][:, 1:w + 1, :] for k in range(2)],
                             [P[k][:, w:w + 1, :].to_broadcast([128, w, HP]) for k in range(2)], t1, t2)
                    V.tensor_scalar(r_(12), P[0][:, 1, :], -1.0, None, ALU.add)
                    V.tensor_tensor(r_(14), are, are, ALU.mult)
                    link(V.tensor_tensor(r_(15), aim, aim, ALU.mult))
                    link(V.tensor_tensor(r_(13), r_(14), r_(15), ALU.add))
                    link(V.reciprocal(r_(16), r_(13)))
                    V.tensor_tensor(r_(14), r_(12), are, ALU.mult)
                    link(V.tensor_tensor(r_(15), P[1][:, 1, :], aim, ALU.mult))
                    link(V.tensor_tensor(r_(17), r_(14), r_(15), ALU.add))
                    V.tensor_tensor(r_(14), P[1][:, 1, :], are, ALU.mult)
                    link(V.tensor_tensor(r_(15), r_(12), aim, ALU.mult))
                    link(V.tensor_tensor(r_(18), r_(14), r_(15), ALU.subtract))
                    V.tensor_tensor(r_(17), r_(17), r_(16), ALU.mult)
                    link(V.tensor_tensor(r_(18), r_(18), r_(16), ALU.mult))
                    t1 = T1[:, 0:HP * GC].rearrange("p (e c) -> p e c", e=HP)
                    t2 = T2[:, 0:HP * GC].rearrange("p (e c) -> p e c", e=HP)
                    cmul(Bb, [bc(r_(17 + k), 2, GC) for k in range(2)], [pB[:, k] for k in range(2)], t1, t2)

                    def powers(o, base, n, **kw):
                        t1 = T1[:, 0:HP * n * GC].rearrange("p (e m c) -> p e m c", e=HP, m=n)
                        t2 = T2[:, 0:HP * n * GC].rearrange("p (e m c) -> p e m c", e=HP, m=n)
                        cmul(o, [bc(P[k][:, 0:n, :].rearrange("p m e -> p e m"), 3, GC) for k in range(2)],
                             [bc(t, 2, n) for t in base], t1, t2, **kw)

                    powers(BP, Bb, CH)
                    V.memset(m8x[:, 0:1], 0.0).then_inc(bp_ready, 1)
                    if hf:
                        dve.wait_ge(y_mm, v - 1)
                    powers(CP, [pB[:, 2], pB[:, 3]], CH + 1, negate_im=True)
                    V.memset(m8x[:, 0:1], 0.0).then_inc(cp_ready, 1)
                    a, b_ = [r_(6), r_(5)], [r_(19), r_(20)]
                    for o in ([r_(19), r_(20)], [r_(21), r_(22)], [E[k][:, :, 0] for k in range(2)]):
                        cmul(o, a, a, T1[:, 0:HP], T2[:, 0:HP])
                        a = o
                    w = 1
                    while w < NC:
                        t1 = T1[:, 0:HP * w].rearrange("p (e c) -> p e c", e=HP)
                        t2 = T2[:, 0:HP * w].rearrange("p (e c) -> p e c", e=HP)
                        cmul([E[k][:, :, w:2 * w] for k in range(2)], [E[k][:, :, 0:w] for k in range(2)],
                             [E[k][:, :, w - 1:w].to_broadcast([128, HP, w]) for k in range(2)], t1, t2)
                        w *= 2
                    link(V.tensor_copy(R8, bc(r_(4), 2, NC)))
                    link(V.memset(R8[:, :, 0:1], 0.0))
                    for k in range(2):
                        V.memset(H[k][:, :, NB:NB + 1], 0.0)
                        V.tensor_copy(H[k][:, :, 0:NB], pH[:, k])
                    flat = lambda t: t.rearrange("p e c -> p (e c)")
                    for part in range(2):
                        es = slice(HP // 2 * part, HP // 2 * part + HP // 2)
                        dve.wait_ge(g_mm, 2 * (v - 1) + part + 1)
                        g_in = [bank(2 * part + k)[:, 0:HP // 2 * NC].rearrange("p (e c) -> p e c", c=NC) for k in range(2)]
                        t1 = T1[:, 0:HP // 2 * NC].rearrange("p (e c) -> p e c", c=NC)
                        t2 = T2[:, 0:HP // 2 * NC].rearrange("p (e c) -> p e c", c=NC)
                        E_, GM_, GS_ = ([t[:, es] for t in ts] for ts in (E, GM, GS))
                        V.tensor_tensor(t1, E_[0], g_in[0], ALU.mult)
                        link(V.tensor_tensor(t2, E_[1], g_in[1], ALU.mult))
                        link(V.tensor_tensor(GM_[0], t1, t2, ALU.add))
                        V.tensor_tensor(t1, E_[0], g_in[1], ALU.mult)
                        link(V.tensor_tensor(t2, E_[1], g_in[0], ALU.mult))
                        link(V.tensor_tensor(GM_[1], t1, t2, ALU.subtract))
                        for k in range(2):
                            ins = V.tensor_tensor_scan(flat(GS_[k]), flat(R8[:, es]), flat(GM_[k]), 0.0, ALU.mult, ALU.add)
                        link(ins)
                        cmul([H[k][:, es, NB + 1:] for k in range(2)], E_, GS_, t1, t2)
                        V.memset(m8x[:, 0:1], 0.0).then_inc(h_ready, 1)
                    t1 = T1[:, 0:HP * NB].rearrange("p (e c) -> p e c", e=HP)
                    t2 = T2[:, 0:HP * NB].rearrange("p (e c) -> p e c", e=HP)
                    if hf or l:
                        dve.wait_ge(stored, 16 * (2 * l + hf + 4 * l))
                    so = [hout[:, k, :, 1:NB + 1] for k in range(2)]
                    cmul(so, [bc(P[k][:, DT, :], 2, NB) for k in range(2)], [pH[:, k] for k in range(2)], t1, t2)
                    for k in range(2):
                        for part in range(2):
                            o = so[k][:, HP // 2 * part:HP // 2 * part + HP // 2, :]
                            V.tensor_tensor(o, o, bank(2 * part + k)[:, 256:256 + HP // 2 * NB].rearrange("p (e b) -> p e b", b=NB), ALU.add)
                        ins = V.tensor_copy(hout[:, k, :, 0:1], H[k][:, :, NB + NC:NB + NC + 1])
                    ins.then_inc(hout_ready, 1)

                dve.wait_ge(tok_ready, 2 * l + 2)
                dve.wait_ge(rbias_in, 16)
                dve.wait_ge(y_ready, 2 * l + 2)
                dve.wait_ge(stored, 16 * (2 * (l + 1) + 4 * l))
                V.tensor_scalar(negid, ident, NEG, None, ALU.mult).then_inc(hide_ready, 1)

                def scores(b, ni):
                    w = 128 * (b + 1)
                    for h in range(NH):
                        dve.wait_ge(relu_ready, ni + 1)
                        if h == 0:
                            V.tensor_scalar(sc[:, 0:w], rl[:, ni % 4, 0:w], wtok[:, b, h:h + 1], None, ALU.mult).then_inc(relu_used, 1)
                        else:
                            V.scalar_tensor_tensor(sc[:, 0:w], rl[:, ni % 4, 0:w], wtok[:, b, h:h + 1], sc[:, 0:w],
                                                   ALU.mult, ALU.add).then_inc(relu_used, 1)
                        ni += 1
                        dve.wait_ge(relu_used, ni)
                    V.tensor_scalar(sc[:, 0:w - 128], sc[:, 0:w - 128], IDX_SCALE, None, ALU.mult)
                    link(V.scalar_tensor_tensor(sc[:, w - 128:w], sc[:, w - 128:w], IDX_SCALE, cst[:, C_MC:C_MC + 128], ALU.mult, ALU.add))

                def choose(b, between):
                    w = 128 * (b + 1)
                    top(sc[:, 0:w], wk, m8, TOPK_P, between=between)
                    V.tensor_tensor(nosel[:, 0:w], wk[:, 0:w], sc[:, 0:w], ALU.is_equal).then_inc(hide_ready, 1)

                nl = NH * NQT * l
                for b in range(NQT):
                    w = 128 * (b + 1)
                    if l or b:
                        dve.wait_ge(pt_ready, 20 * l + b * (b + 1))
                    for h in range(NH):
                        dve.wait_ge(lg_mm, nl + 1)
                        V.tensor_tensor_reduce(Lg[:, h, 0:w], bank(2 + nl % 3)[:, 0:w], rbias[:, h, SEQ - w:SEQ], 1.0, -3.0e38,
                                               ALU.add, ALU.max, accum_out=nmx[:, h:h + 1]).then_inc(lg_used, 1)
                        nl += 1
                        if h % 4 == 3:
                            dve.wait_ge(lg_used, nl)
                            V.tensor_scalar(nmx[:, h - 3:h + 1], nmx[:, h - 3:h + 1], -1.0, None, ALU.mult).then_inc(nmx_ready, 1)
                    if b + 1 < NQT:
                        scores(b + 1, NH * (3 * l + b))
                    else:
                        V.memset(Qzi, 0.0)
                        link(V.memset(Qz, 0.0))
                        for a in range(2):
                            for dst, src in ((Qzi, qi), (Qz, q)):
                                for i in range(4):
                                    ins = V.tensor_copy(dst[64 * a:64 * a + 64, :, a, i, :],
                                                        src[64 * a:64 * a + 64, i, SEQ:T].rearrange("p (t b) -> p b t", b=NB))
                        ins.then_inc(qz_ready, 1)
                        dve.wait_ge(wr_mm, l + 1)
                        for r in range(2):
                            ins = V.tensor_tensor(wr[:, r, :], bank(4)[:, 0:NS], cst[:, C_MW + NS * r:C_MW + NS * r + NS], ALU.mult)
                        ins.then_inc(wr_ready, 1)
                    def invert(i):
                        if i == 1:
                            dve.wait_ge(exp_ready, nl)
                            V.reciprocal(rs, sums).then_inc(rs_ready, 1)

                    if b + 1 < NQT:
                        choose(b + 1, invert)
                    else:
                        invert(1)
                    if b == 1:
                        dve.wait_ge(y_in, 16 * (l + 1))
                        for k in range(4):
                            ins = V.scalar_tensor_tensor(u[:, k, :], u[:, k, :], dsk[:, l, k:k + 1], cat[:, k, :], ALU.mult, ALU.add)
                        ins.then_inc(yd_ready, 1)

                dve.wait_ge(sc_mm, 2 * l + 2)
                V.tensor_scalar(scs[0:NS, 0:PAST], bank(2)[0:NS, :], IDX_SCALE, None, ALU.mult)
                V.memset(wks[0:NS, SK:SK + 7], 3.0e38)
                V.scalar_tensor_tensor(scs[0:NS, PAST:SK], bank(3)[0:NS, 0:NS], IDX_SCALE, cst[0:NS, C_MS:C_MS + NS],
                                       ALU.mult, ALU.add).then_inc(scs_ready, 1)
                dve.wait_ge(scs_ready, l + 1)

                GLU_AT = (9, 12, 15, TOPK_S)
                def glu(i):
                    if i not in GLU_AT:
                        return
                    m = 2 * GLU_AT.index(i)
                    s = m % 4
                    got(s)
                    dve.wait_ge(emptied[s + 1], c.take(s + 1))
                    V.tensor_tensor(halves(cat[:, m // 2, :]), halves(sg[:, m // 2 % 2, :]), even(s), ALU.mult).then_inc(emptied[s], 1)

                top(scs[0:NS, :], wks[0:NS, :], m8[0:NS, :], TOPK_S, 3.0e38, between=glu)
                link(V.tensor_tensor(nss[0:NS, :], wks[0:NS, 0:SK], scs[0:NS, :], ALU.is_equal))
                V.tensor_scalar(nss[0:NS, :], nss[0:NS, :], NEG, None, ALU.mult).then_inc(nosel_ready, 1)
                glu(TOPK_S)
                for r in range(2):
                    dve.wait_ge(sl_mm, 2 * l + r + 1)
                    V.tensor_tensor(Ls[r][:, 0:PAST], bank(2 * r), bs[:, 0:PAST], ALU.add)
                    link(V.tensor_tensor(Ls[r][:, PAST:SK], bank(2 * r + 1)[:, 0:NS], bs[:, PAST:SK], ALU.add))
                    link(V.tensor_reduce(nms[r][:, 0:1], Ls[r], AX.X, ALU.max))
                    V.tensor_scalar(nms[r][:, 0:1], nms[r][:, 0:1], -1.0, None, ALU.mult).then_inc(snmx, 1)
                for r in range(2):
                    dve.wait_ge(sexp, 2 * l + r + 1)
                    link(V.reciprocal(nms[r][:, 2:3], nms[r][:, 1:2]))
                    V.tensor_scalar(Ls[r], Ls[r], nms[r][:, 2:3], None, ALU.mult).then_inc(sprob, 1)

                for m in range(8):
                    s = m % 4
                    got(s)
                    V.scalar_tensor_tensor(halves(acc[:, m, :]), halves(x[:, m, :]), ALPHA, even(s), ALU.mult, ALU.add).then_inc(emptied[s], 1)
                    dve.wait_ge(emptied[s], c.n[s])
                    add_up(m, sums_done[0])
                sums_done[0] += KC - 1
                layer_norm(1 + 2 * l)
                if l == 1:
                    link(V.memset(rlog, 0.0))
                    V.memset(rank, 0.0)
                    dve.wait_ge(r_mm, 1)
                    V.tensor_tensor(rlog[:, 0:4, :], bank(6)[:, 0:4 * NE].rearrange("p (n e) -> p n e", n=4), bc(brt[:, :], 1, 4), ALU.add)
                    V.memset(rwk, 3.0e38)
                    link(V.tensor_tensor(rlog[0:NS, 4, :], bank(6)[0:NS, 4 * NE:5 * NE], brt[0:NS, :], ALU.add))
                    V.tensor_copy(rwk[:, :, 0:NE], rlog)
                    for tt in range(TT):
                        ins = V.max(rtop[:, tt, :], rlog[:, tt, :])
                    link(ins)
                    V.tensor_copy(rtwo[:, :, 0:2], rtop[:, :, 0:2])
                    link(V.memset(rtwo[:, :, 2:8], 3.0e38))
                    for tt in range(TT):
                        ins = V.match_replace(rwk[:, tt, :], rtwo[:, tt, :], rwk[:, tt, :], GONE)
                    link(ins)
                    link(V.tensor_tensor(sel, rwk[:, :, 0:NE], rlog, ALU.not_equal))
                    for lo in (32, 64):
                        ins = V.memset(sel[lo:2 * lo, TT - 1, :], 0.0)
                    ins.then_inc(sel_ready, 1)
                    dve.wait_ge(sel_ready, 1)
                    V.tensor_tensor(rlog, rlog, rtop[:, :, 0:1].to_broadcast([128, TT, NE]), ALU.subtract)
                    V.tensor_tensor(rsm[:, :, 0:1], rtop[:, :, 1:2], rtop[:, :, 0:1], ALU.subtract).then_inc(gdiff, 1)
                    dve.wait_ge(gexp, 1)
                    link(V.tensor_scalar(rsm[:, :, 2:3], rsm[:, :, 1:2], 1.0, None, ALU.add))
                    link(V.reciprocal(rsm[:, :, 3:4], rsm[:, :, 2:3]))
                    link(V.tensor_tensor(gts, sel, rlog, ALU.mult))
                    link(V.tensor_tensor(gts, gts, rsm[:, :, 3:4].to_broadcast([128, TT, NE]), ALU.mult))
                    dve.wait_ge(rank_mm, 1)
                    V.tensor_copy(rank[:, 0:4, :], bank(6)[:, 64:64 + 4 * NE].rearrange("p (n e) -> p n e", n=4))
                    link(V.tensor_copy(rank[0:NS, 4, :], bank(6)[0:NS, 64 + 4 * NE:64 + 5 * NE]))
                    cc = lambda at, n=NE: bc(cst[:, at:at + n], 1, TT)
                    link(V.tensor_tensor(order, rank, cc(C_E1), ALU.add))
                    V.tensor_scalar(over, sel, -1.0, -1.0e6, ALU.add, ALU.mult)
                    link(V.tensor_tensor(tmp8, order, sel, ALU.mult))
                    link(V.tensor_reduce(v01[:, :, 1:2], tmp8, AX.X, ALU.max))
                    link(V.tensor_tensor(tmp8, tmp8, over, ALU.add))
                    link(V.tensor_reduce(v01[:, :, 0:1], tmp8, AX.X, ALU.min))
                    for k in range(2):
                        at = v01[:, :, k:k + 1].to_broadcast([128, TT, NE])
                        for what, o in ((rank, r01), (cc(C_EC), b01), (gts, g01)):
                            link(V.tensor_tensor(tmp8, order, at, ALU.is_equal))
                            link(V.tensor_tensor(tmp8, tmp8, sel, ALU.mult))
                            link(V.tensor_tensor(tmp8, tmp8, what, ALU.mult))
                            link(V.tensor_reduce(o[:, :, k:k + 1], tmp8, AX.X, ALU.add))
                    link(V.tensor_scalar(ok01, r01, float(CAP), None, ALU.is_lt))
                    V.tensor_tensor(g01, g01, ok01, ALU.mult)
                    link(V.tensor_tensor(ix01, b01, r01, ALU.add))
                    link(V.tensor_tensor(ix01, ix01, ok01, ALU.mult))
                    ixf = lambda t: t.rearrange("p t k -> p (t k)")
                    V.tensor_copy(idx[:, 2 * TT:4 * TT], ixf(ix01))
                    link(V.tensor_scalar(r01, ok01, -1.0, -1.0, ALU.add, ALU.mult))
                    for k in range(2):
                        ins = V.tensor_scalar(b01[:, :, k], cst[:, C_TI:C_TI + TT], float(XROWS + k * TT * 128), None, ALU.add)
                    link(ins)
                    link(V.tensor_tensor(b01, b01, r01, ALU.mult))
                    link(V.tensor_tensor(b01, b01, ix01, ALU.add))
                    V.tensor_copy(idx[:, 0:2 * TT], ixf(b01)).then_inc(idx_ready, 1)
                    link(V.tensor_scalar(over, rank, float(CAP), None, ALU.is_ge))
                    link(V.tensor_tensor(over, over, sel, ALU.mult))
                    V.tensor_reduce(ovs, over.rearrange("p t e -> p (t e)"), AX.X, ALU.add).then_inc(ov_ready, 1)
                    dve.wait_ge(ov_ready, 1)
                    V.tensor_tensor(over, over, gts, ALU.mult)
                    dve.wait_ge(flag_mm, 1)
                    V.tensor_copy(flag[0:1, 0:1], bank(6)[0:1, 0:1]).then_inc(flag_ready, 1)
                for m in range(8):
                    s = (2 * m) % 4
                    dve.wait_ge(emptied[s], c.take(s))
                    got(s + 1)
                    sv = halves(sg[:, m % 2, :])
                    V.tensor_tensor(sv, sv, even(s + 1), ALU.mult).then_inc(emptied[s + 1], 1)
                    dve.wait_ge(emptied[s + 1], c.n[s + 1])
                    V.scalar_tensor_tensor(acc[:, m, :], x[:, m, :], ALPHA, sg[:, m % 2, :], ALU.mult, ALU.add).then_inc(ple_used, 1)
                def dense_blocks(count):
                    c0 = list(c.n)
                    with dve.Fori(0, count) as e:
                        for kind, i, ps in ffn_plan():
                            def count_(s, seen):
                                return e * FFN_USES[s] + (c0[s] + seen + 1)
                            if kind == "up":
                                (s, seen), (s2, seen2) = ps
                                dve.wait_ge(emptied[s], count_(s, seen))
                                dve.wait_ge(filled[s2], count_(s2, seen2))
                                V.tensor_tensor(halves(hid[:, i, :]), halves(sg[:, i % 2, :]), even(s2), ALU.mult).then_inc(emptied[s2], 1)
                                dve.wait_ge(emptied[s2], count_(s2, seen2))
                                if l == 0:
                                    V.memset(m8x[:, 0:1], 0.0).then_inc(hid_ready, 1)
                                else:
                                    V.tensor_tensor(hid[:, i, :], hid[:, i, :], gb[:, bass.ds(e, 1), :].rearrange("p o t -> p (o t)"),
                                                    ALU.mult).then_inc(hid_ready, 1)
                            else:
                                (s, seen), = ps
                                dve.wait_ge(filled[s], count_(s, seen))
                                V.tensor_tensor(halves(acc[:, i, :]), halves(acc[:, i, :]), even(s), ALU.add).then_inc(emptied[s], 1)
                                dve.wait_ge(emptied[s], count_(s, seen))
                                add_up(i, e * (KC - 1) + sums_done[0])
                    for s in range(4):
                        c.n[s] += FFN_USES[s] * count
                    sums_done[0] += (KC - 1) * count

                if l == 0:
                    dense_blocks(2)
                else:
                    for s in (3, 0):
                        c.take(s)
                    c0 = list(c.n)
                    with dve.Fori(0, NE) as e:
                        for kind, i, s, seen in moe_plan():
                            if kind == "up":
                                dve.wait_ge(silu_ready, e * FT + i + 1)
                                V.tensor_tensor(hidg[:, i, :], sg[:, i % 2, 0:CAP], pair[s][:, 512:512 + CAP], ALU.mult).then_inc(emptied[s], 1)
                            elif kind == "down":
                                dve.wait_ge(filled[s], e * MOE_USES[s] + (c0[s] + seen + 1))
                                V.tensor_copy(yT[:, 2 * i:2 * i + 2, :], banks(s, CAP)).then_inc(emptied[s], 1)
                    for s in range(4):
                        c.n[s] += MOE_USES[s] * NE
                    for tt in range(TT):
                        rows = 128 if tt < 4 else NS
                        dve.wait_ge(gt_scaled, tt + 1)
                        dve.wait_ge(gt_in[1][tt], 16)
                        V.scalar_tensor_tensor(gt[0][0:rows, tt, :], gt[1][0:rows, tt, :], g01[0:rows, tt, 1:2], gt[0][0:rows, tt, :],
                                               ALU.mult, ALU.add).then_inc(comb_ready, 1)
                    for kc in range(KC):
                        s = kc % 4
                        got(s)
                        V.tensor_tensor(acc[:, kc, :], acc[:, kc, :], pair[s][:, 0:T], ALU.add).then_inc(emptied[s], 1)
                        dve.wait_ge(emptied[s], c.n[s])
                        add_up(kc, sums_done[0])
                    sums_done[0] += KC - 1
                    for s in range(4):
                        dve.wait_ge(emptied[s], c.n[s])
                    left = dve.value_load(flag[0:1, 0:1], min_val=0, max_val=2 * T)
                    with dve.If(left > 0):
                        dve.wait_ge(gb_ready, NE)
                        dense_blocks(NE)
                if l == L - 1:
                    V.memset(m8x[:, 0:1], 0.0).then_inc(acc_ready, 1)
                layer_norm(2 + 2 * l)


def _bucket(dist):
    import numpy as np
    n = np.maximum(dist, 0)
    big = 16 + (np.log(np.maximum(n, 1).astype(np.float32) / np.float32(16)) / np.float32(math.log(8.0)) * np.float32(16)).astype(np.int32)
    return np.where(n < 16, n, np.minimum(big, 31))


def _consts():
    import numpy as np
    c = np.zeros((128, C_END), np.float32)
    c[:, C_ID:C_ID + 128] = np.eye(128)
    p, f = np.arange(128)[:, None], np.arange(128)[None, :]
    c[:, C_CM:C_CM + 128] = f > p
    c[:, C_MC:C_MC + 128] = np.where(f > p, NEG, 0.0)
    row = np.arange(128)
    bi, a, i, t = row // 32, row // 16 % 2, row // 4 % 4, row % 4
    ys = np.arange(NS)
    yt, yb = ys // NB, ys % NB
    for r in range(2):
        same = (yt[:, None] == t[None]) & (yb[:, None] == 4 * r + bi[None])
        c[0:NS, C_EX + 128 * r:C_EX + 128 * r + 128] = same
        c[:, C_MW + NS * r:C_MW + NS * r + NS] = same.T
    c[0:NH, C_OH:C_OH + 128] = np.arange(NH)[:, None] == (2 * i + a)[None]
    c[0:NS, C_MS:C_MS + NS] = np.where((yb[None] == yb[:, None]) & (yt[None] <= yt[:, None]), 0.0, NEG)
    tk = np.arange(128)
    kt, kb = tk // 32, tk % 32
    past = PAST + kt[:, None] - np.arange(PAST)[None]
    new = kt[:, None] - yt[None]
    c[:, C_TK:C_TK + PAST + NS] = _bucket(np.concatenate([past, new], 1)) == kb[:, None]
    c[:, C_MT:C_MT + 128] = kt[:, None] == t[None]
    c[:, C_TI:C_TI + TT] = np.arange(128)[:, None] + 128 * np.arange(TT)[None]
    c[:, C_E1:C_E1 + NE] = ORD * np.arange(NE)
    c[:, C_EC:C_EC + NE] = CAP * np.arange(NE)
    c[0:32, C_OF:C_OF + BW] = np.arange(32)[:, None] == _bucket(SEQ - 1 - np.arange(BW))[None]
    return c


def _tokens(prompt, sample):
    import numpy as np
    f = prompt.shape[-1]
    a = np.concatenate([prompt.reshape(NC, CH, f).transpose(1, 0, 2).reshape(SEQ, f),
                        sample.transpose(1, 0, 2).reshape(NS, f)], 0)
    return np.ascontiguousarray(a.T.reshape(f // 128, 128, T).transpose(1, 0, 2))


def _tiles(w):
    k, m = w.shape
    return w.reshape(k // 128, 128, m // 128, 128).transpose(2, 1, 0, 3).reshape(m // 128, 128, k)


def _vec(v):
    return v.reshape(-1, 128).T


_OUTS = {"o_y": (128, KC, T), "o_k": (L, 128, T), "o_v": (L, 128, NQT + 1, 128), "o_ki": (L, 64, T),
         "o_h": (L, 2, 128, 2 * HP * (NB + 1))}


def _layout(a):
    import numpy as np
    o = {}
    o["x_t"] = _tokens(a["x_prompt"][0], a["x_sample"])
    o["p_t"] = np.stack([_tokens(a["p_prompt"][l, 0], a["p_sample"][l]) for l in range(L)])
    ln = [a["ln_emb_g"], a["ln_emb_b"]]
    for l in range(L):
        ln += [a["ln1_g"][l], a["ln1_b"][l], a["ln2_g"][l], a["ln2_b"][l]]
    o["ln_p"] = np.stack([_vec(v) for v in ln], 1)
    o["d_t"] = np.stack([_vec(a["ssm_d"][l]) for l in range(L)], 1)
    o["w_router_t"] = a["moe_w_router"][0].reshape(KC, 128, NE).transpose(1, 0, 2)
    o["b_router_t"] = np.broadcast_to(a["moe_b_router"][0][None], (128, NE))
    o["pages"] = a["page_table"].reshape(1, -1)
    o["rel_rows"] = np.broadcast_to(a["rel_bias"][:, :, None], (32, NH, 128))
    row = np.arange(128)
    o["rel_tk"] = np.tile(a["rel_bias"][:, 4 * (row // 16 % 2) + row // 4 % 4], (4, 1))
    win, wv, glu, wo, ple, ssm = [], [], [], [], [], []
    qcols = np.concatenate([np.arange(64) + 64 * h for i in range(4) for h in (i, i + 4)])
    rows = np.concatenate([np.arange(512), 512 + qcols])
    for l in range(L):
        w = a["w_in"][l]
        cols = np.concatenate([np.arange(512), 512 + qcols, 1280 + np.arange(512), 1024 + np.arange(128),
                               1792 + np.arange(64), 1792 + np.arange(64)])
        win.append(_tiles(w[:, cols]))
        vc = np.concatenate([1152 + np.arange(128), 1856 + np.arange(8)])
        wv.append(w[:, vc].reshape(KC, 128, 136).transpose(1, 0, 2).reshape(128, KC * 136))
        gt = _tiles(a["ssm_w_glu"][l])
        glu.append(gt[[0, 4, 1, 5, 2, 6, 3, 7]])
        wo.append(_tiles(a["w_out"][l][rows]))
        ple.append(np.concatenate([_tiles(a["ple_w_gate"][l]), _tiles(a["ple_w_proj"][l])], 2))
        halves_ = []
        for hf in range(2):
            g = slice(HG * hf, HG * hf + HG)
            st = lambda v: v.reshape(HP, 2 * SN, -1).transpose(1, 2, 0)
            parts = [st(a["ssm_a_re"][l, g]), st(a["ssm_a_im"][l, g]),
                     st(np.broadcast_to(a["ssm_log_dt"][l, g][:, None], (HG, SN))),
                     st(a["ssm_b_re"][l, g]), st(a["ssm_b_im"][l, g]),
                     st(a["ssm_c_re"][l, g].transpose(0, 2, 1)), st(a["ssm_c_im"][l, g].transpose(0, 2, 1)),
                     st(a["state_ssm_re"][l][:, g].transpose(1, 2, 0)), st(a["state_ssm_im"][l][:, g].transpose(1, 2, 0))]
            halves_.append(np.concatenate(parts, 1).reshape(128, -1))
        ssm.append(np.stack(halves_))
    o["w_in_t"], o["w_v_t"], o["w_glu_t"], o["w_out_t"], o["w_ple_t"], o["ssm_t"] = map(np.stack, (win, wv, glu, wo, ple, ssm))
    gu, dn = [], []

    def block(g, u_, d):
        gu.append(np.stack([_tiles(g), _tiles(u_)], 1).reshape(2 * FT, 128, DM))
        dn.append(_tiles(d))

    for i in range(2):
        s = slice(FE * i, FE * i + FE)
        block(a["ffn_w_gate"][0][:, s], a["ffn_w_up"][0][:, s], a["ffn_w_down"][0][s])
    for e in range(NE):
        block(a["moe_w_gate"][0, e], a["moe_w_up"][0, e], a["moe_w_down"][0, e])
    o["w_gu_t"], o["w_dn_t"] = np.stack(gu), np.stack(dn)
    o["c_k"] = a["cache_k"].reshape(L, NPOOL, PAGE, 128).transpose(0, 1, 3, 2)
    o["c_v"] = a["cache_v"].reshape(L, NPOOL, PAGE, 128)
    o["c_i"] = np.tile(a["cache_kidx"].transpose(0, 1, 3, 2), (1, 1, 2, 1))
    o["consts"] = _consts()
    return {k: np.ascontiguousarray(v) for k, v in o.items()}


def _split(t):
    return t[:, :SEQ].T, t[:, SEQ:].T.reshape(DT, NB, -1).transpose(1, 0, 2)


def kernel(**inputs):
    import numpy as np
    import concourse.bacc as bacc
    from concourse.bass_utils import run_bass_kernel_spmd

    arrays = _layout({k: np.asarray(v) for k, v in inputs.items()})
    nc = bacc.Bacc("TRN2", target_bir_lowering=False, num_devices=1)
    io = {k: nc.dram_tensor(k, v.shape, mybir.dt.from_np(v.dtype), kind="ExternalInput").ap() for k, v in arrays.items()}
    io.update({k: nc.dram_tensor(k, s, mybir.dt.float32, kind="ExternalOutput").ap() for k, s in _OUTS.items()})
    build(nc, io)
    res = run_bass_kernel_spmd(nc, [arrays], core_ids=[0]).results[0]
    y = np.asarray(res["o_y"]).transpose(1, 0, 2).reshape(DM, T)
    xp = y[:, :SEQ].reshape(DM, CH, NC).transpose(2, 1, 0).reshape(1, SEQ, DM)
    xs = y[:, SEQ:].T.reshape(DT, NB, DM).transpose(1, 0, 2)
    k = [_split(np.asarray(res["o_k"])[l]) for l in range(L)]
    ki = [_split(np.asarray(res["o_ki"])[l]) for l in range(L)]
    v = np.asarray(res["o_v"])
    vp = v[:, :, :NQT, :].transpose(0, 2, 1, 3).reshape(L, 1, SEQ, 2, HD)
    vs = v[:, :NS, NQT, :].reshape(L, DT, NB, 2, HD).transpose(0, 2, 1, 3, 4)
    h = np.asarray(res["o_h"]).reshape(L, 2, 2, SN, 2, HP, NB + 1)
    h = h.transpose(4, 0, 6, 1, 5, 2, 3).reshape(2, L, NB + 1, G, SN)
    c = np.ascontiguousarray
    return (c(xp), c(xs),
            np.stack([t[0] for t in k]).reshape(L, 1, SEQ, 2, HD), c(vp), np.stack([t[0] for t in ki])[:, None],
            c(h[0][:, :1]), c(h[1][:, :1]),
            np.stack([t[1] for t in k]).reshape(L, NB, DT, 2, HD), c(vs), np.stack([t[1] for t in ki]),
            c(h[0][:, 1:]), c(h[1][:, 1:]))
```
